# Optimizing a Trainium2 kernel written in Bass

```python
import jax, jax.numpy as jnp
from jax import lax
import numpy as np

D_MODEL = 1024
BATCH = 1
SEQ = 512
DEPTH = 1

CHUNK = 64
N_META = 16

A_HEADS = 8
A_HEAD_DIM = 64
A_WIDTH = A_HEADS * A_HEAD_DIM
Q_RANK = 256
KV_RANK = 128
IDX_HEADS = 8
IDX_DIM = 64
INDEX_TOPK = 256
Q_BLOCK = 128

B_HEADS = 8
B_HEAD_DIM = 64
B_WIDTH = B_HEADS * B_HEAD_DIM
DECAY_LORA = 64
AAA_LORA = 64
GATE_LORA = 128
GN_EPS = 64e-5

D_FF = 2816
CONV_W = 3

LN_EPS = 1e-5
ALPHA = (2 * DEPTH) ** 0.25
BETA = (8 * DEPTH) ** -0.25

A_COLS = Q_RANK + KV_RANK + IDX_DIM + IDX_HEADS
B_COLS = 3 * B_WIDTH + DECAY_LORA + AAA_LORA + GATE_LORA
IN_COLS = A_COLS + B_COLS

kernel_name = "hymba_dsa_rwkv7_convffn_deepnorm"

def layer_norm(x, g, b, eps=LN_EPS):
    xf = x.astype(jnp.float32)
    mu = jnp.mean(xf, -1, keepdims=True)
    var = jnp.mean(jnp.square(xf - mu), -1, keepdims=True)
    return ((xf - mu) * lax.rsqrt(var + eps) * g + b).astype(x.dtype)

def rms_norm(x, g, eps=1e-6):
    xf = x.astype(jnp.float32)
    y = xf * lax.rsqrt(jnp.mean(jnp.square(xf), -1, keepdims=True) + eps) * g
    return y.astype(x.dtype)

def chunk_ids(pos):
    return (pos - N_META) // CHUNK + 1

def alibi_slopes(n_heads):
    return jnp.asarray([2.0 ** (-8.0 * (h + 1) / n_heads) for h in range(n_heads)], jnp.float32)

def sparse_indexed_attention(pa, q_norm_g, w_uq, kv_norm_g, w_ukv, w_iq, idx_ln_g, idx_ln_b):
    bsz, T, _ = pa.shape
    c_q = pa[..., :Q_RANK]
    c_kv = pa[..., Q_RANK:Q_RANK + KV_RANK]
    k_idx_raw = pa[..., Q_RANK + KV_RANK:Q_RANK + KV_RANK + IDX_DIM]
    w_idx = pa[..., Q_RANK + KV_RANK + IDX_DIM:]
    c_q = rms_norm(c_q, q_norm_g)
    q = (c_q @ w_uq).reshape(bsz, T, A_HEADS, A_HEAD_DIM)
    q_idx = (c_q @ w_iq).reshape(bsz, T, IDX_HEADS, IDX_DIM)
    kv = (rms_norm(c_kv, kv_norm_g) @ w_ukv).reshape(bsz, T, A_HEADS, 2 * A_HEAD_DIM)
    k, v = kv[..., :A_HEAD_DIM], kv[..., A_HEAD_DIM:]
    k_idx = layer_norm(k_idx_raw, idx_ln_g, idx_ln_b)
    w_idx = w_idx * (IDX_HEADS ** -0.5 * IDX_DIM ** -0.5)

    topk = min(INDEX_TOPK, T // 4)
    n_blk = -(-T // Q_BLOCK)
    t_pad = n_blk * Q_BLOCK

    def to_blocks(a):
        a = jnp.pad(a, [(0, 0), (0, t_pad - T)] + [(0, 0)] * (a.ndim - 2))
        return jnp.moveaxis(a.reshape((bsz, n_blk, Q_BLOCK) + a.shape[2:]), 1, 0)

    key_pos = jnp.arange(T, dtype=jnp.int32)
    key_chunk = chunk_ids(key_pos)
    slopes = alibi_slopes(A_HEADS)
    scale = A_HEAD_DIM ** -0.5

    def block(args):
        q_b, qi_b, wi_b, pos_b = args
        qc = chunk_ids(pos_b)
        visible = key_chunk[None, :] <= qc[:, None]
        rel = jax.nn.relu(jnp.einsum('bqhd,bsd->bqhs', qi_b, k_idx,
                                     preferred_element_type=jnp.float32))
        score = jnp.einsum('bqhs,bqh->bqs', rel, wi_b.astype(jnp.float32))
        score = jnp.where(visible[None], score, -jnp.inf)
        _, sel = lax.top_k(score, topk)
        k_sel = jax.vmap(lambda kb, ib: kb[ib])(k, sel)
        v_sel = jax.vmap(lambda vb, ib: vb[ib])(v, sel)
        sel_ok = key_chunk[sel] <= qc[None, :, None]
        dist = jnp.abs(pos_b[None, :, None] - sel).astype(jnp.float32)
        logits = jnp.einsum('bqhd,bqkhd->bqhk', q_b, k_sel,
                            preferred_element_type=jnp.float32) * scale
        logits = logits - slopes[None, None, :, None] * dist[:, :, None, :]
        logits = jnp.where(sel_ok[:, :, None, :], logits, -jnp.inf)
        p = jax.nn.softmax(logits, axis=-1)
        return jnp.einsum('bqhk,bqkhd->bqhd', p.astype(v_sel.dtype), v_sel)

    pos_blocks = jnp.arange(t_pad, dtype=jnp.int32).reshape(n_blk, Q_BLOCK)
    out = lax.map(block, (to_blocks(q), to_blocks(q_idx), to_blocks(w_idx), pos_blocks))
    out = jnp.moveaxis(out, 0, 1).reshape(bsz, t_pad, A_WIDTH)[:, :T]
    return out.astype(pa.dtype)

def token_shift(p):
    return jnp.pad(p, [(0, 0), (1, 0), (0, 0)])[:, :-1]

def rwkv7_time_mix(pb, mu_shift, w0, w_decay_up, a0, w_aaa_up, w_gate_up, k_k, k_a, r_k, gn_g, gn_b):
    bsz, T, _ = pb.shape
    pb = pb + (token_shift(pb) - pb) * mu_shift
    s1, s2, s3 = B_WIDTH, 2 * B_WIDTH, 3 * B_WIDTH
    s4, s5 = s3 + DECAY_LORA, s3 + DECAY_LORA + AAA_LORA
    r, k, v = pb[..., :s1], pb[..., s1:s2], pb[..., s2:s3]
    wd, ad, gd = pb[..., s3:s4], pb[..., s4:s5], pb[..., s5:]
    w_log = -jax.nn.softplus(-(w0 + jnp.tanh(wd) @ w_decay_up)) - 0.5
    decay = jnp.exp(-jnp.exp(w_log.astype(jnp.float32)))
    a = jax.nn.sigmoid(a0 + ad @ w_aaa_up)
    g = jax.nn.sigmoid(gd) @ w_gate_up

    def heads(t):
        return t.astype(jnp.float32).reshape(bsz, T, B_HEADS, B_HEAD_DIM)

    kk = heads(k * k_k)
    kk = kk / jnp.maximum(jnp.sqrt(jnp.sum(jnp.square(kk), -1, keepdims=True)), 1e-12)
    k = k * (1 + (a - 1) * k_a)
    r_h, k_h, v_h, a_h, w_h = heads(r), heads(k), heads(v), heads(a), heads(decay)
    a_vec = -kk
    b_vec = kk * a_h

    def step(S, inp):
        r_t, w_t, k_t, v_t, av_t, bv_t = inp
        sa = jnp.einsum('bhvk,bhk->bhv', S, av_t)
        S = S * w_t[:, :, None, :] + sa[..., None] * bv_t[:, :, None, :] + v_t[..., None] * k_t[:, :, None, :]
        return S, jnp.einsum('bhvk,bhk->bhv', S, r_t)

    xs = tuple(jnp.moveaxis(t, 1, 0) for t in (r_h, w_h, k_h, v_h, a_vec, b_vec))
    S0 = jnp.zeros((bsz, B_HEADS, B_HEAD_DIM, B_HEAD_DIM), jnp.float32)
    _, y = lax.scan(step, S0, xs)
    y = jnp.moveaxis(y, 0, 1)
    mu = jnp.mean(y, -1, keepdims=True)
    var = jnp.mean(jnp.square(y - mu), -1, keepdims=True)
    y = ((y - mu) * lax.rsqrt(var + GN_EPS)).reshape(bsz, T, B_WIDTH) * gn_g + gn_b
    bonus = jnp.sum(r_h * k_h * r_k, -1, keepdims=True) * v_h
    y = (y + bonus.reshape(bsz, T, B_WIDTH)) * g
    return y.astype(pb.dtype)

def conv_ffn(x, w_ffn_up, conv_w, conv_b, w_ffn_down):
    up = x @ w_ffn_up
    gate, val = up[..., :D_FF], up[..., D_FF:]
    gate = lax.conv_general_dilated(gate, conv_w[:, None, :], window_strides=(1,),
                                    padding=[(CONV_W - 1, 0)],
                                    dimension_numbers=('NWC', 'WIO', 'NWC'),
                                    feature_group_count=D_FF) + conv_b
    return (jax.nn.gelu(gate) * val) @ w_ffn_down

def setup_inputs(seed: int = 0) -> dict:
    key = jax.random.key(seed)
    ks = jax.random.split(key, 32)
    f32 = jnp.float32

    def nrm(k, shape, scale):
        return jax.random.normal(k, shape, f32) * scale

    def gain(k, shape):
        return 1.0 + 0.02 * jax.random.normal(k, shape, f32)

    def bias(k, shape):
        return 0.02 * jax.random.normal(k, shape, f32)

    L = DEPTH
    return {
        'x': nrm(ks[0], (BATCH, SEQ, D_MODEL), 1.0),
        'meta': nrm(ks[1], (N_META, D_MODEL), 1.0),
        'ln_in_g': gain(ks[2], (D_MODEL,)),
        'ln_in_b': bias(ks[3], (D_MODEL,)),
        'w_in': nrm(ks[4], (L, D_MODEL, IN_COLS), D_MODEL ** -0.5),
        'q_norm_g': gain(ks[5], (L, Q_RANK)),
        'w_uq': nrm(ks[6], (L, Q_RANK, A_WIDTH), Q_RANK ** -0.5),
        'kv_norm_g': gain(ks[7], (L, KV_RANK)),
        'w_ukv': nrm(ks[8], (L, KV_RANK, 2 * A_WIDTH), KV_RANK ** -0.5),
        'w_iq': nrm(ks[9], (L, Q_RANK, IDX_HEADS * IDX_DIM), Q_RANK ** -0.5),
        'idx_ln_g': gain(ks[10], (L, IDX_DIM)),
        'idx_ln_b': bias(ks[11], (L, IDX_DIM)),
        'mu_shift': jax.random.uniform(ks[12], (L, B_COLS), f32),
        'w0': jax.random.uniform(ks[13], (L, B_WIDTH), f32, -6.0, -1.0),
        'w_decay_up': nrm(ks[14], (L, DECAY_LORA, B_WIDTH), 0.1 * DECAY_LORA ** -0.5),
        'a0': nrm(ks[15], (L, B_WIDTH), 0.1),
        'w_aaa_up': nrm(ks[16], (L, AAA_LORA, B_WIDTH), 0.1 * AAA_LORA ** -0.5),
        'w_gate_up': nrm(ks[17], (L, GATE_LORA, B_WIDTH), GATE_LORA ** -0.5),
        'k_k': 0.85 + 0.02 * jax.random.normal(ks[18], (L, B_WIDTH), f32),
        'k_a': gain(ks[19], (L, B_WIDTH)),
        'r_k': nrm(ks[20], (L, B_HEADS, B_HEAD_DIM), 0.1),
        'gn_g': gain(ks[21], (L, B_WIDTH)),
        'gn_b': bias(ks[22], (L, B_WIDTH)),
        'w_out': nrm(ks[23], (L, A_WIDTH + B_WIDTH, D_MODEL), BETA * (A_WIDTH + B_WIDTH) ** -0.5),
        'ln1_g': gain(ks[24], (L, D_MODEL)),
        'ln1_b': bias(ks[25], (L, D_MODEL)),
        'w_ffn_up': nrm(ks[26], (L, D_MODEL, 2 * D_FF), D_MODEL ** -0.5),
        'conv_w': nrm(ks[27], (L, CONV_W, D_FF), CONV_W ** -0.5),
        'conv_b': bias(ks[28], (L, D_FF)),
        'w_ffn_down': nrm(ks[29], (L, D_FF, D_MODEL), BETA * D_FF ** -0.5),
        'ln2_g': gain(ks[30], (L, D_MODEL)),
        'ln2_b': bias(ks[31], (L, D_MODEL)),
    }

def reference(x, meta, ln_in_g, ln_in_b, w_in, q_norm_g, w_uq, kv_norm_g, w_ukv, w_iq,
              idx_ln_g, idx_ln_b, mu_shift, w0, w_decay_up, a0, w_aaa_up, w_gate_up,
              k_k, k_a, r_k, gn_g, gn_b, w_out, ln1_g, ln1_b, w_ffn_up, conv_w, conv_b,
              w_ffn_down, ln2_g, ln2_b):
    bsz = x.shape[0]
    meta_b = jnp.broadcast_to(meta[None].astype(x.dtype), (bsz, N_META, x.shape[-1]))
    h = jnp.concatenate([meta_b, x], axis=1)
    h = layer_norm(h, ln_in_g, ln_in_b)
    for l in range(DEPTH):
        p = h @ w_in[l]
        ya = sparse_indexed_attention(p[..., :A_COLS], q_norm_g[l], w_uq[l], kv_norm_g[l],
                                      w_ukv[l], w_iq[l], idx_ln_g[l], idx_ln_b[l])
        yb = rwkv7_time_mix(p[..., A_COLS:], mu_shift[l], w0[l], w_decay_up[l], a0[l],
                            w_aaa_up[l], w_gate_up[l], k_k[l], k_a[l], r_k[l], gn_g[l], gn_b[l])
        mix = jnp.concatenate([ya, yb], axis=-1) @ w_out[l]
        h = layer_norm(ALPHA * h + mix, ln1_g[l], ln1_b[l])
        ffn = conv_ffn(h, w_ffn_up[l], conv_w[l], conv_b[l], w_ffn_down[l])
        h = layer_norm(ALPHA * h + ffn, ln2_g[l], ln2_b[l])
    return h[:, N_META:]


_drawn_inputs = setup_inputs


def setup_inputs(seed=0):
    import zlib

    import numpy as np

    out = dict(_drawn_inputs(seed))
    spreads = {}
    factors = {'q_norm_g': 3.958,
     'kv_norm_g': 8.0,
     'idx_ln_g': 3.402,
     'idx_ln_b': 4.265,
     'w_decay_up': 8.0,
     'a0': 6.868,
     'w_aaa_up': 6.93,
     'k_k': 46.898,
     'k_a': 31.942,
     'gn_g': 41.618,
     'gn_b': 39.111,
     'ln1_g': 2.719,
     'conv_b': 8.0,
     'ln2_g': 7.684,
     'ln2_b': 8.058,
     'ln1_b': 6.176}
    for name, (base, spread) in spreads.items():
        noise = np.random.default_rng([zlib.crc32(name.encode()), seed]).standard_normal(out[name].shape)
        drawn = base * np.exp(spread * noise) if base else spread * noise
        out[name] = __import__('jax').numpy.asarray(drawn.astype(out[name].dtype))
    for name, factor in factors.items():
        out[name] = (out[name] * factor).astype(out[name].dtype)
    return out
```

```python
from contextlib import ExitStack

import concourse.bass as bass
from concourse import mybir

F32 = mybir.dt.float32
ALU = mybir.AluOpType
ACT = mybir.ActivationFunctionType
AX = mybir.AxisListType

P = 128
D = 1024
KT_D = D // P
SEQ, META = 512, 16
T = SEQ + META
HALF = T // 2
TILES = SEQ // P
CH = 64
PAD = CH - META
NCH = SEQ // CH + 1
TP = NCH * CH
HP = TP // 2
HEADS, HD = 8, 64
NJ = HEADS // 2
Q_RANK, KV_RANK, IDX = 256, 128, 64
A_COLS = Q_RANK + KV_RANK + IDX + HEADS
TOPK = T // 4
FF = 2816
NF = FF // P
CONV = 3
LN_EPS, RMS_EPS, GN_EPS = 1e-5, 1e-6, 64e-5
ALPHA = 2.0 ** 0.25
KAPPA = 0.6065306597126334
IDX_SCALE = HEADS ** -0.5 * IDX ** -0.5
INVISIBLE, TAKEN, TAKEN_BELOW = -3.0e38, -3.4e38, -3.2e38
FAR = 1.0e34
SLOPES = [2.0 ** (-8.0 * (h + 1) / HEADS) for h in range(HEADS)]
KEYS = [META + P * (i + 1) for i in range(TILES)]

META_TILE = "m"
TOKS = [META_TILE] + list(range(TILES))
IX_ORDER = (3, 2, 1, 0)

COLS = {"q0": (0, 128), "q1": (128, 128), "kv": (256, 128), "ki": (384, IDX + HEADS),
        "wa": (A_COLS + 3 * 512, 128), "gd": (A_COLS + 3 * 512 + 128, 128)}
COLS |= {f"{x}{j}": (A_COLS + 512 * n + P * j, 128) for j in range(NJ) for n, x in enumerate("rkv")}
PROJ = list(COLS)
SHIFTED = PROJ[4:]
W_RING = 5
PAR_ROWS = (("mu", 14), ("w0", 4), ("a0", 4), ("k_k", 4), ("k_a", 4), ("r_k", 4), ("gn_g", 4), ("gn_b", 4),
            ("q_g", 2), ("kv_g", 1), ("i_g", 1), ("i_b", 1))
PAR = {name: sum(r for _, r in PAR_ROWS[:n]) for n, (name, _) in enumerate(PAR_ROWS)}
NPAR = sum(r for _, r in PAR_ROWS)
MU_TILE = {f"{x}{j}": 4 * n + j for n, x in enumerate("rkv") for j in range(NJ)} | {"wa": 12, "gd": 13}

PAIRS = [(0,)] + [(2 * i + 1, 2 * i + 2) for i in range(TILES)]
BUF = [0, 1, 2, 0, 1]
GROUPS = [[0, 1, 2], [3, 4]]
BLK = 32
FIRST_BLOCK = {p: sum(16 * len(PAIRS[q]) for q in g if q < p) for g in GROUPS for p in g}
BLOCKS = [sum(16 * len(PAIRS[p]) for p in g) for g in GROUPS]


def rwkv_scores(p):
    return [f"tk{p}_0", f"sc{p}_0", f"tk{p}_1", f"sc{p}_1"]


def rwkv_local(p):
    return [f"x1_{p}", f"u0_{p}", f"nu_{p}", f"u_{p}", f"qg_{p}", f"hy_{p}"]


def rwkv_chain(p):
    return [f"zy_{c}" for c in PAIRS[p] if c]


def attention(i):
    jobs = []
    for n in range(HEADS + 3):
        jobs += [f"S{i}_{n}"] * (n < HEADS) + [f"T{i}_{n - 2}"] * (2 <= n < HEADS + 2) + [f"O{i}_{n - 3}"] * (n >= 3)
    return jobs


def mixers():
    yield from (("scores", p) for p in GROUPS[0])
    yield "invert", 0
    yield "attend", 3
    for p in GROUPS[0]:
        yield "local", p
        yield "chain", p
    yield from (("scores", p) for p in GROUPS[1])
    yield "invert", 1
    yield "attend", 2
    yield "attend", 1
    for p in GROUPS[1]:
        yield "local", p
        yield "chain", p
    yield "center", None
    yield "attend", 0
    yield "attend", "m"


def psum_jobs():
    jobs = ["par"] + [f"hT{i}" for i in TOKS]
    jobs += ["p_q0", "p_q1", "p_kv", "p_ki", "ssq", "sskv", "p_wa", "kmean", "p_gd", "kvar", "widx"]
    jobs += [f"qi{j}" for j in range(NJ)] + ["p_r0"] + [f"qp{j}" for j in range(NJ)] + ["p_k0"]
    jobs += [f"kp{j}" for j in range(NJ)] + ["vp0", "vp1", "vp2"]
    rest = [f"p_{n}" for n in PROJ[8:]]
    for i in IX_ORDER:
        for h in range(HEADS):
            jobs.append(f"ix{i}_{h}")
            if h % 4 == 3 and rest:
                jobs.append(rest.pop(0))
    jobs += rest
    for name in ("z", "a", "ss", "bo"):
        jobs += [f"{name}{j}" for j in range(NJ)]
    stages = {"scores": rwkv_scores, "local": rwkv_local, "chain": rwkv_chain, "attend": attention,
              "invert": lambda g: [], "center": lambda _: [f"ym{j}" for j in range(NJ)]}
    for stage, n in mixers():
        jobs += stages[stage](n)
    for j in range(NJ):
        jobs += [f"yv{j}", f"g{j}"]
    jobs += [f"mix{i}" for i in TOKS]
    jobs += [f"h1T{i}" for i in TOKS]
    for f in range(NF):
        jobs += [f"gate{f}", f"val{f}"]
    return jobs + [f"down{i}" for i in range(TILES)]


ORDER = psum_jobs()
JOBS = {name: n for n, name in enumerate(ORDER)}
NSLOT = 4
ATT = {(i, h): HEADS * n + h for n, i in enumerate(i for st, i in mixers() if st == "attend") for h in range(HEADS)}
ATT_LIST = list(ATT)
N_CONST = 18
N_PAR_DMA = 16
ROWS = {i: P for i in range(TILES)} | {META_TILE: META}
NKEYS = {i: KEYS[i] for i in range(TILES)} | {META_TILE: META}
QCOLS = {i: slice(META + P * i, META + P * (i + 1)) for i in range(TILES)} | {META_TILE: slice(0, META)}
YCOLS = {i: slice(CH + P * i, CH + P * (i + 1)) for i in range(TILES)} | {META_TILE: slice(PAD, CH)}
HROW = {i: i for i in range(TILES)} | {META_TILE: TILES}


def head_rows(h):
    return slice(HD * (h % 2), HD * (h % 2) + HD)


def chunk_rows(c):
    return slice(CH * c, CH * c + CH)


def flat(v):
    n = len(v.shape)
    names = " ".join("abcde"[:n - 1])
    return v.rearrange(f"p {names} -> p ({names})")


def halves(v):
    return v.rearrange("p (b c) -> p b c", b=2)


def hymba(nc, x, meta, ln_in_g, ln_in_b, w_in, q_norm_g, w_uq, kv_norm_g, w_ukv, w_iq,
          idx_ln_g, idx_ln_b, mu_shift, w0, w_decay_up, a0, w_aaa_up, w_gate_up,
          k_k, k_a, r_k, gn_g, gn_b, w_out, ln1_g, ln1_b, w_ffn_up, conv_w, conv_b,
          w_ffn_down, ln2_g, ln2_b, out):
    with ExitStack() as ctx:
        def sb(name, *shape):
            return ctx.enter_context(nc.sbuf_tensor(name, [P, *shape], F32))

        ident, ones, blk, mask, eye2 = sb("ident", P), sb("ones", P), sb("blk", P), sb("mask", P), sb("eye2", CH)
        dist = sb("dist", T)
        parT = sb("parT", NPAR + 4 * NF)
        h_tok = sb("h_tok", TILES + 1, D)
        stats, mv, mhalf, eps = sb("stats", 2, 6), sb("mv", 2, 4), sb("mhalf", 1), sb("eps", 3)
        wix = sb("wix", TILES, HEADS)
        m8 = sb("m8", 2, 8)
        nmax, rsum, rinv = sb("nmax", HEADS), sb("rsum", HEADS), sb("rinv", HEADS)
        Z = sb("Z", 2, NJ, HD)
        PL = sb("PL", NJ, NCH)
        SIZE = 46130
        arena = sb("arena", SIZE)
        slots = [ctx.enter_context(nc.psum_tensor(f"slot{i}", [P, 1024], F32)) for i in range(NSLOT)]
        blocks_in = nc.dram_tensor("blocks_in", (sum(BLOCKS), BLK, BLK), F32, kind="Internal").ap()
        blocks_out = nc.dram_tensor("blocks_out", (sum(BLOCKS), BLK, BLK), F32, kind="Internal").ap()

        end = {}

        def lay(at, **shapes):
            views = []
            for name, shape in shapes.items():
                n = 1
                for d in shape:
                    n *= d
                assert at + n <= SIZE, (name, at + n)
                v = arena[:, at:at + n]
                at += n
                end[name] = at
                if len(shape) > 1:
                    dims = "abcd"[:len(shape)]
                    v = v.rearrange(f"p ({' '.join(dims)}) -> p {' '.join(dims)}", **dict(zip(dims, shape)))
                views.append(v)
            return views

        AR, KT, BT, VY, BONUS, qT, kT, vtok, SC, praw, ptmp, wad, sgd = lay(
            0, AR=(NJ, 2, TP), KT=(NJ, TP), BT=(NJ, TP), VY=(NJ, TP), BONUS=(NJ, TP), qT=(NJ, T), kT=(NJ, T),
            vtok=(TILES + 1, 512), SC=(sum(KEYS),), praw=(3, 1 + T), ptmp=(T,), wad=(T,), sgd=(T,))
        base = end["sgd"]
        wring, hT, aRaw, tmpA, kiT, wuq, wiq, wuk, wuv, qiT, relu = lay(
            base, wring=(W_RING, KT_D, P), hT=(KT_D, T), aRaw=(4, T), tmpA=(3, T), kiT=(T,), wuq=(2, 512), wiq=(2, 512),
            wuk=(512,), wuv=(512,), qiT=(NJ, T), relu=(2, T))
        xin, = lay(0, xin=(TILES + 1, D))
        gain_in, = lay(end["wuv"], gain_in=(2, D))
        par_rows = flat(tmpA)[:, 0:2 * P]
        csig, aT, Pp, wlora = lay(base, csig=(NJ, NCH * 65), aT=(NJ, TP), Pp=(NJ, NCH * 65), wlora=(512,))
        assert end["wlora"] <= end["hT"]
        tw = flat(tmpA)[:, 0:2 * TP].rearrange("p (a b) -> p a b", a=2)
        reset = flat(praw)[:, 0:NCH * 65]
        wgate = wad[:, 0:512]
        R, Vtok, Ni, Xi, Ti, QB, GT, U0, MSX, DI, PT, PTm = lay(
            base, R=(3, NJ, 2, P), Vtok=(3, NJ, 2, HD), Ni=(BLK * BLK,), Xi=(BLK * BLK,), Ti=(256,), QB=(NJ, 2, HD),
            GT=(NJ, 2, HD), U0=(NJ, 2, P), MSX=(3, NJ, 2, 384), DI=(3, NJ, 2, HD), PT=(2, 4 * P), PTm=(2, P))
        H = flat(U0)[:, 0:2 * NJ * HD].rearrange("p (c j v) -> p c j v", c=2, j=NJ)
        Lb, Pb = lay(end["SC"], Lb=(2, T), Pb=(2, T))
        assert end["Pb"] <= end["ptmp"]
        wout, = lay(0, wout=(KT_D, D))
        assert end["wout"] <= end["BT"]
        actT, = lay(0, actT=(NF, SEQ))
        wup, h1T, wdn, gs, cv, ge, gain2, gain1 = lay(
            end["VY"], wup=(3, 2, KT_D, P), h1T=(KT_D, SEQ + 2), wdn=(16, D), gs=(2, SEQ + 2), cv=(2, SEQ), ge=(2, SEQ),
            gain2=(2, D), gain1=(2, D))
        wdn2, = lay(end["VY"], wdn2=(NF - 16, D))
        assert end["wdn2"] <= end["wup"]

        written = [ctx.enter_context(nc.semaphore(f"slot{i}_written")) for i in range(NSLOT)]
        emptied = [ctx.enter_context(nc.semaphore(f"slot{i}_emptied")) for i in range(NSLOT)]
        named = {}

        def s(name):
            if name not in named:
                named[name] = ctx.enter_context(nc.semaphore(name))
            return named[name]

        def slot(job):
            return slots[JOBS[job] % NSLOT]

        def banks(job, n):
            return halves(slot(job)[:, :])[:, :, 0:n]

        def product(eng, job):
            eng.wait_ge(written[JOBS[job] % NSLOT], JOBS[job] // NSLOT + 1)

        def empties(ins, job):
            ins.then_inc(emptied[JOBS[job] % NSLOT], 1)

        def evacuated(eng, job):
            eng.wait_ge(emptied[JOBS[job] % NSLOT], JOBS[job] // NSLOT + 1)

        def par(name, j=0):
            return parT[:, PAR[name] + j:PAR[name] + j + 1]

        def distances(i):
            if i == META_TILE:
                return dist[0:META, T - P:T - P + META]
            return dist[:, T - KEYS[i]:T]

        block = ctx.enter_context(nc.Block())

        @block.sync
        def _(sp):
            win = w_in[0].rearrange("(k p) n -> p k n", p=P)
            for i in TOKS:
                src = meta if i == META_TILE else x[0, P * i:P * (i + 1), :]
                sp.dma_start(xin[0:ROWS[i], HROW[i], :], src).then_inc(s(f"x_in{i}"), 16)
            for n, name in enumerate(PROJ):
                lo, m = COLS[name]
                if n == 4:
                    for dst, src in ((wuq, w_uq), (wiq, w_iq)):
                        sp.dma_start(dst, src[0].rearrange("(k p) n -> p k n", p=P)).then_inc(s("w_low"), 16)
                    ukv = w_ukv[0].rearrange("p (h t d) -> p h t d", h=HEADS, t=2)
                    for t, dst in enumerate((wuk, wuv)):
                        sp.dma_start(dst.rearrange("p (h d) -> p h d", h=HEADS), ukv[:, :, t, :]).then_inc(s("w_low"), 16)
                if n >= W_RING:
                    product(sp, f"p_{PROJ[n - W_RING]}")
                sp.dma_start(wring[:, n % W_RING, :, 0:m], win[:, :, lo:lo + m]).then_inc(s(f"w_ring{n % W_RING}"), 16)
                if n == 10:
                    sp.wait_ge(s("index_keys"), 1)
                    sp.dma_start(kiT[HD:2 * HD, :], kiT[0:HD, :]).then_inc(s("index_keys2"), 16)
            product(sp, f"p_{PROJ[-1]}")
            sp.dma_start(wlora[0:64, :], w_decay_up[0]).then_inc(s("w_lora"), 16)
            sp.dma_start(wlora[64:128, :], w_aaa_up[0]).then_inc(s("w_lora"), 16)
            product(sp, f"a{NJ - 1}")
            sp.dma_start(wgate, w_gate_up[0]).then_inc(s("w_gate"), 16)
            first, came, went = 0, 0, 0
            for g, pairs in enumerate(GROUPS):
                for p in pairs:
                    evacuated(sp, f"sc{p}_0")
                    evacuated(sp, f"sc{p}_1")
                    for q in range(2 * len(PAIRS[p])):
                        src = MSX[BLK * q:BLK * (q + 1), BUF[p], :, :, BLK * (q % 2):BLK * (q % 2 + 1)]
                        lo = first + FIRST_BLOCK[p] + HEADS * q
                        dst = blocks_in[lo:lo + HEADS].rearrange("i s t -> s i t")
                        sp.dma_start(dst, src.rearrange("s j h t -> s (j h) t")).then_inc(s("blocks_out1"), 16)
                        went += 16
                sp.wait_ge(s("blocks_out1"), went)
                src = blocks_in[first:first + BLOCKS[g]].rearrange("i s t -> i (s t)")
                sp.dma_start(Ni[0:BLOCKS[g], :], src).then_inc(s("blocks_here"), 16)
                sp.wait_ge(s("inverted"), g + 1)
                dst = blocks_out[first:first + BLOCKS[g]].rearrange("i s t -> i (s t)")
                sp.dma_start(dst, Xi[0:BLOCKS[g], :]).then_inc(s("inverses_out"), 16)
                sp.wait_ge(s("inverses_out"), 16 * (g + 1))
                for p in pairs:
                    for q in range(2 * len(PAIRS[p])):
                        dst = DI[BLK * q:BLK * (q + 1), BUF[p], :, :, BLK * (q % 2):BLK * (q % 2 + 1)]
                        lo = first + FIRST_BLOCK[p] + HEADS * q
                        src = blocks_out[lo:lo + HEADS].rearrange("i s t -> s i t")
                        sp.dma_start(dst.rearrange("s j h t -> s (j h) t"), src).then_inc(s("inverses_here"), 16)
                first += BLOCKS[g]
            evacuated(sp, f"qg_{len(PAIRS) - 1}")
            for k in range(0, KT_D, 4):
                src = w_out[0, P * k:P * (k + 4), :].rearrange("(k p) n -> p k n", p=P)
                sp.dma_start(wout[:, k:k + 4, :], src).then_inc(s("w_out"), 16)
            evacuated(sp, f"g{NJ - 1}")
            wu = w_ffn_up[0].rearrange("(k p) n -> p k n", p=P)
            gates, ups = 2, 0

            def load_up(f):
                for g in range(2):
                    sp.dma_start(wup[:, f % 3, g], wu[:, :, FF * g + P * f:FF * g + P * (f + 1)]).then_inc(s(f"w_up{f % 3}"), 16)

            def load_down(f):
                sp.dma_start(wdn[:, f, :], w_ffn_down[0, P * f:P * (f + 1), :]).then_inc(s("w_down"), 16)

            load_up(0)
            for f in range(8):
                load_down(f)
            product(sp, f"mix{TILES - 1}")
            load_up(1)
            load_up(2)
            for f in range(8, 16):
                load_down(f)
            for f in range(3, NF):
                product(sp, f"val{f - 3}")
                load_up(f)
            product(sp, f"val{NF - 1}")
            for f in range(16, NF):
                sp.dma_start(wdn2[:, f - 16, :], w_ffn_down[0, P * f:P * (f + 1), :]).then_inc(s("w_down2"), 16)
            for i in range(TILES):
                sp.wait_ge(s("out_ready"), i + 1)
                sp.dma_start(out[0, P * i:P * (i + 1), :], h_tok[:, i, :]).then_inc(s("stored"), 16)
            sp.wait_ge(s("stored"), 16 * TILES)

        @block.gpsimd
        def _(pool):
            def select(v, pattern, base, mult, op, value):
                return pool.affine_select(out=v, in_=v, compare_op=op, fill=value, base=base,
                                          pattern=pattern, channel_multiplier=mult)

            pool.memset(ident[:, :], 0.0).then_inc(s("const"), 1)
            pool.memset(eye2[:, :], 0.0).then_inc(s("const"), 1)
            pool.memset(mask[:, :], 1.0).then_inc(s("const"), 1)
            pool.memset(blk[:, :], 0.0).then_inc(s("const"), 1)
            pool.memset(ones[:, :], 1.0).then_inc(s("const"), 1)
            pool.memset(mhalf[:, :], -0.5).then_inc(s("const"), 1)
            for k, v in enumerate((LN_EPS, RMS_EPS, GN_EPS)):
                pool.memset(eps[:, k:k + 1], v).then_inc(s("const"), 1)
            n_const = 9
            pool.wait_ge(s("const"), n_const)

            def const(ins):
                nonlocal n_const
                ins.then_inc(s("const"), 1)
                n_const += 1
                pool.wait_ge(s("const"), n_const)

            const(select(ident[:, :], [[-1, P]], 0, 1, ALU.not_equal, 1.0))
            for g in range(2):
                rows = slice(HD * g, HD * (g + 1))
                const(select(eye2[rows, :], [[-1, HD]], 0, 1, ALU.not_equal, 1.0))
                const(pool.memset(blk[rows, rows], 1.0))
                for kind in range(2):
                    const(select(mask[rows, CH * kind:CH * (kind + 1)], [[1, CH]], kind - 1, -1, ALU.is_ge, 0.0))
            pool.iota(dist[:, :], pattern=[[-1, T]], base=META + T - KEYS[0], channel_multiplier=1,
                      allow_small_or_imprecise_dtypes=True).then_inc(s("positions"), 1)

            def rstds(k0, k1):
                for k in range(k0, k1):
                    r = ROWS[(TOKS + TOKS + list(range(TILES)))[k]]
                    pool.wait_ge(s("var"), k + 1)
                    pool.tensor_tensor(mv[0:r, k % 2, 3:4], mv[0:r, k % 2, 2:3], mhalf[0:r, :], ALU.pow).then_inc(s("rstd"), 1)

            rstds(0, 5)
            pool.wait_ge(s("normed"), 5)
            for v in (AR[:, :, 1, 0:PAD], KT[:, :, 0:PAD], VY[:, :, 0:PAD], praw[:, :, 0:1]):
                pool.memset(v, 0.0).then_inc(s("pads"), 1)
            for n, name in enumerate(SHIFTED):
                raw = praw[:, n % 3, :]
                evacuated(pool, f"p_{name}")
                pool.tensor_tensor(ptmp, raw[:, 0:T], raw[:, 1:T + 1], ALU.subtract).then_inc(s("shift_line"), 1)
                pool.wait_ge(s("shift_line"), 2 * n + 1)
                pool.tensor_scalar(ptmp, ptmp, par("mu", MU_TILE[name]), None, ALU.mult).then_inc(s("shift_line"), 1)
                pool.wait_ge(s("shift_line"), 2 * n + 2)
                if name in ("wa", "gd"):
                    dst = {"wa": wad, "gd": sgd}[name]
                else:
                    j = int(name[1])
                    dst = {"r": AR[:, j, 1], "k": KT[:, j], "v": VY[:, j]}[name[0]][:, PAD:TP]
                pool.tensor_tensor(dst, ptmp, raw[:, 1:T + 1], ALU.add).then_inc(s("shifted"), 1)
                pool.wait_ge(s("shifted"), n + 1)
            for (i, h), n in ATT.items():
                pool.wait_ge(s("rinv"), n + 1)
                v = Pb[0:ROWS[i], n % 2, 0:NKEYS[i]]
                pool.tensor_scalar(v, v, rinv[0:ROWS[i], h:h + 1], None, ALU.mult).then_inc(s("probs"), 1)
            rstds(5, 14)

        @block.scalar
        def _(act):
            A = act.activation
            row = 0
            for v, (name, n) in zip((mu_shift, w0, a0, k_k, k_a, r_k, gn_g, gn_b, q_norm_g, kv_norm_g, idx_ln_g, idx_ln_b), PAR_ROWS):
                if name == "r_k":
                    v = v.rearrange("l h d -> l (h d)")
                if name in ("i_g", "i_b"):
                    for c in range(2):
                        act.dma_start(par_rows[row:row + 1, IDX * c:IDX * (c + 1)], v).then_inc(s("par_in"), 16)
                else:
                    act.dma_start(par_rows[row:row + n, 0:P], v.rearrange("l (r p) -> (l r) p", p=P)).then_inc(s("par_in"), 16)
                row += n
            act.dma_start(par_rows[0:3 * NF, P:2 * P], conv_w[0].rearrange("t (r p) -> (t r) p", p=P)).then_inc(s("par_in"), 16)
            act.dma_start(par_rows[3 * NF:4 * NF, P:2 * P], conv_b.rearrange("l (r p) -> (l r) p", p=P)).then_inc(s("par_in"), 16)
            for k, v in enumerate((ln_in_g, ln_in_b)):
                act.dma_start(gain_in[:, k, :], v.rearrange("(o n) -> o n", o=1).to_broadcast([P, D])).then_inc(s("gain_in"), 16)

            def evacuate(job, dst, src, func=ACT.Copy, **kw):
                product(act, job)
                empties(A(dst, src, func, **kw), job)

            evacuate("par", parT[:, :], slot("par")[:, 0:NPAR + 4 * NF])
            for i in TOKS:
                v = slot(f"hT{i}")[:, :].rearrange("p (k t) -> p k t", k=KT_D)[:, :, 0:ROWS[i]]
                evacuate(f"hT{i}", hT[:, :, QCOLS[i]], v)

            order = list(JOBS)
            n_shift = n_relu = 0
            for job in order[order.index("p_q0"):order.index("z0")]:
                kind, n = job[:2], job[2:]
                if job in ("p_q0", "p_q1", "p_kv"):
                    k = ("p_q0", "p_q1", "p_kv").index(job)
                    product(act, job)
                    A(halves(aRaw[:, k, :]), banks(job, HALF), ACT.Copy)
                    empties(A(halves(tmpA[:, k, :]), banks(job, HALF), ACT.Square), job)
                elif job == "p_ki":
                    m = IDX + HEADS
                    evacuate(job, halves(aRaw[0:m, 3, :]), banks(job, HALF)[0:m])
                elif kind == "p_":
                    if n_shift >= 3:
                        act.wait_ge(s("shifted"), n_shift - 2)
                    else:
                        act.wait_ge(s("pads"), 4)
                    evacuate(job, halves(praw[:, n_shift % 3, 1:T + 1]), banks(job, HALF))
                    n_shift += 1
                elif kind == "ss":
                    k, rank = (0, Q_RANK) if job == "ssq" else (2, KV_RANK)
                    evacuate(job, halves(tmpA[:, k, :]), banks(job, HALF), ACT.Sqrt, bias=eps[:, 1:2], scale=1.0 / rank)
                elif job == "kmean":
                    evacuated(act, job)
                    A(tmpA[0:IDX, 1, :], aRaw[0:IDX, 3, :], ACT.Square).then_inc(s("key_squares"), 1)
                elif job == "kvar":
                    evacuated(act, job)
                    A(kiT[0:IDX, :], tmpA[0:IDX, 0, :], ACT.Sqrt).then_inc(s("key_root"), 1)
                elif job == "widx":
                    v = slot(job)[:, 0:TILES * HEADS].rearrange("p (i h) -> p i h", i=TILES)
                    evacuate(job, wix[:, :, :], v, scale=IDX_SCALE)
                elif kind in ("qp", "qi", "kp"):
                    dst = {"qp": qT, "qi": qiT, "kp": kT}[kind]
                    evacuate(job, halves(dst[:, int(n), :]), banks(job, HALF), scale=HD ** -0.5 if kind == "qp" else 1.0)
                elif job == "vp0":
                    product(act, job)
                    A(vtok[0:META, TILES, :], slot(job)[0:META, 0:512], ACT.Copy)
                    empties(A(vtok[:, 0, :], slot(job)[:, 512:1024], ACT.Copy), job)
                elif job == "vp1":
                    evacuate(job, vtok[:, 1:3, :], banks(job, 512))
                elif job == "vp2":
                    evacuate(job, vtok[:, 3, :], slot(job)[:, 0:512])
                else:
                    i = int(job[2])
                    if n_relu >= 2:
                        act.wait_ge(s("index_sum"), n_relu - 1)
                    evacuate(job, relu[:, n_relu % 2, 0:KEYS[i]], slot(job)[:, 0:KEYS[i]], ACT.Relu)
                    n_relu += 1

            act.wait_ge(s("shifted"), 2)
            A(wad[0:64, :], wad[0:64, :], ACT.Tanh).then_inc(s("lora_in"), 1)
            A(sgd, sgd, ACT.Sigmoid).then_inc(s("lora_in"), 1)
            act.wait_ge(s("cleared"), 3)
            for j in range(NJ):
                job = f"z{j}"
                product(act, job)
                cs = csig[:, j, :].rearrange("p (c t) -> p c t", t=CH + 1)
                A(cs[:, 0, CH + 1 - META:], slot(job)[:, 0:META], ACT.Sigmoid, bias=par("w0", j))
                v = slot(job)[:, 512:1024].rearrange("p (c t) -> p c t", t=CH)
                empties(A(cs[:, 1:NCH, 1:], v, ACT.Sigmoid, bias=par("w0", j)), job)
            for j in range(NJ):
                job = f"a{j}"
                product(act, job)
                A(aT[:, j, PAD:CH], slot(job)[:, 0:META], ACT.Sigmoid, bias=par("a0", j))
                empties(A(aT[:, j, CH:TP], slot(job)[:, 512:1024], ACT.Sigmoid, bias=par("a0", j)), job)
            act.wait_ge(s("shifted"), len(SHIFTED))
            act.wait_ge(s("index_keys"), 1)
            for j in range(NJ):
                if j >= 2:
                    product(act, f"ss{j - 2}")
                A(tw[:, j % 2, :], KT[:, j, :], ACT.Square, scale=par("k_k", j)).then_inc(s("kk_squares"), 1)
            for j in range(NJ):
                evacuate(f"ss{j}", halves(AR[:, j, 0, :]), banks(f"ss{j}", HP), ACT.Sqrt)
            for j in range(NJ):
                act.wait_ge(s("summed"), j + 1)
                A(Pp[:, j, :], csig[:, j, :], ACT.Exp, scale=-KAPPA).then_inc(s("decay"), 1)
                act.wait_ge(s("decay"), 2 * j + 1)
                A(csig[:, j, :], csig[:, j, :], ACT.Exp, scale=KAPPA).then_inc(s("decay"), 1)

            def scores(p):
                rows, b = slice(0, CH * len(PAIRS[p])), BUF[p]
                for half in range(2):
                    job = f"tk{p}_{half}"
                    product(act, job)
                    v = slot(job)[rows, :].rearrange("p (j q h k) -> p j q h k", j=2, q=4, h=2)
                    for jj in range(2):
                        j = 2 * half + jj
                        A(R[rows, b, j, :, CH:P], v[:, jj, 0], ACT.Copy)
                        A(MSX[rows, b, j, :, 128:192], v[:, jj, 1], ACT.Copy)
                        A(MSX[rows, b, j, :, 320:384], v[:, jj, 2], ACT.Copy)
                        last = A(Vtok[rows, b, j], v[:, jj, 3], ACT.Copy)
                    empties(last, job)

            def attend(i):
                r, nk = ROWS[i], NKEYS[i]
                for n in range(HEADS + 3):
                    if n < HEADS:
                        k = ATT[i, n]
                        act.wait_ge(s("max"), k + 1)
                        if k >= 2:
                            product(act, "T{}_{}".format(*ATT_LIST[k - 2]))
                        A(Pb[0:r, k % 2, 0:nk], Lb[0:r, k % 2, 0:nk], ACT.Exp, bias=nmax[0:r, n:n + 1],
                          accum_out=rsum[0:r, n:n + 1]).then_inc(s("exp"), 1)
                    if 2 <= n < HEADS + 2:
                        k = ATT[i, n - 2]
                        job = f"T{i}_{n - 2}"
                        product(act, job)
                        if k >= 2:
                            product(act, "O{}_{}".format(*ATT_LIST[k - 2]))
                        last = A(PTm[0:META, k % 2, 0:r], slot(job)[0:META, 0:r], ACT.Copy)
                        if i != META_TILE:
                            last = A(PT[:, k % 2, 0:P * (i + 1)], slot(job)[:, P:P * (i + 2)], ACT.Copy)
                        empties(last, job)
                    if n >= 3:
                        h = n - 3
                        evacuate(f"O{i}_{h}", qT[head_rows(h), h // 2, QCOLS[i]], slot(f"O{i}_{h}")[head_rows(h), 0:r])

            def local(p):
                rows, b = slice(0, CH * len(PAIRS[p])), BUF[p]
                v = slot(f"x1_{p}")[rows, 0:512].rearrange("p (j h v) -> p j h v", j=NJ, h=2)
                evacuate(f"x1_{p}", R[rows, b, :, :, 0:CH], v)
                job = f"u0_{p}"
                product(act, job)
                if p:
                    act.wait_ge(s("state"), PAIRS[p][0])
                for c in range(len(PAIRS[p])):
                    first = slice(CH * c, CH * c + BLK)
                    last = A(flat(U0[first]), slot(job)[first, :], ACT.Copy)
                empties(last, job)
                evacuate(f"u_{p}", flat(R[rows, b]), slot(f"u_{p}")[rows, :])
                job = f"hy_{p}"
                product(act, job)
                for c, chunk in enumerate(PAIRS[p]):
                    v = slot(job)[:, 512 * c:512 * (c + 1)].rearrange("p (k j t) -> p k j t", k=2, j=NJ)
                    A(H[:, c], v[:, 0], ACT.Copy)
                    last = A(VY[:, :, CH * chunk:CH * (chunk + 1)], v[:, 1], ACT.Copy)
                empties(last, job)

            stages = {"scores": scores, "attend": attend, "local": local}
            for stage, n in mixers():
                if stage in stages:
                    stages[stage](n)
            for j in range(NJ):
                evacuated(act, f"ym{j}")
                if j >= 2:
                    product(act, f"yv{j - 2}")
                A(Lb[:, j % 2, :], VY[:, j, PAD:TP], ACT.Square).then_inc(s("y_squares"), 1)
                if j >= 2:
                    evacuated(act, f"g{j - 2}")
                evacuate(f"yv{j}", halves(Pb[:, j % 2, :]), banks(f"yv{j}", HALF), ACT.Sqrt, bias=eps[:, 2:3], scale=1.0 / HD)
            for dst, g, b in ((gain1, ln1_g, ln1_b), (gain2, ln2_g, ln2_b)):
                for k, v in enumerate((g, b)):
                    act.dma_start(dst[:, k, :], v.to_broadcast([P, D])).then_inc(s("gains"), 16)
            for i in TOKS:
                job = f"h1T{i}"
                v = slot(job)[:, :].rearrange("p (k t) -> p k t", k=KT_D)
                if i == META_TILE:
                    evacuate(job, h1T[:, :, 0:CONV - 1], v[:, :, META - CONV + 1:META])
                else:
                    evacuate(job, h1T[:, :, CONV - 1 + P * i:CONV - 1 + P * (i + 1)], v)

            def gelu(f):
                act.wait_ge(s("conv"), f + 1)
                if f >= 2:
                    evacuated(act, f"val{f - 2}")
                A(ge[:, f % 2, :], cv[:, f % 2, :], ACT.Gelu_apprx_tanh).then_inc(s("gelu"), 1)

            for f in range(NF):
                if f >= 2:
                    act.wait_ge(s("conv"), f - 1)
                evacuate(f"gate{f}", halves(gs[:, f % 2, :]), banks(f"gate{f}", SEQ // 2 + 1))
                if f >= 1:
                    gelu(f - 1)
            gelu(NF - 1)

        @block.vector
        def _(dve):
            V = dve
            steps = [0]

            def then(ins):
                ins.then_inc(s("vector_step"), 1)
                steps[0] += 1
                dve.wait_ge(s("vector_step"), steps[0])

            def statistics(k, v, r):
                m = mv[0:r, k % 2, :]
                V.bn_stats(stats[0:r, 0, :], v[:, 0:512])
                then(V.bn_stats(stats[0:r, 1, :], v[:, 512:1024]))
                then(V.bn_aggr(m[:, 0:2], flat(stats[0:r])))
                V.tensor_scalar(m[:, 2:3], m[:, 1:2], LN_EPS, None, ALU.add).then_inc(s("var"), 1)

            def normalise(k, dst, v, r, gain, signal):
                m = mv[0:r, k % 2, :]
                dve.wait_ge(s("rstd"), k + 1)
                then(V.tensor_scalar(dst, v, m[:, 0:1], m[:, 3:4], ALU.subtract, ALU.mult))
                then(V.tensor_tensor(dst, dst, gain[0:r, 0, :], ALU.mult))
                V.tensor_tensor(dst, dst, gain[0:r, 1, :], ALU.add).then_inc(signal, 1)

            def norm_in(n):
                i = TOKS[n]
                if n == 0:
                    dve.wait_ge(s("gain_in"), 32)
                normalise(n, h_tok[0:ROWS[i], HROW[i], :], xin[0:ROWS[i], HROW[i], :], ROWS[i], gain_in, s("normed"))

            for n, i in enumerate(TOKS):
                dve.wait_ge(s(f"x_in{i}"), 16)
                statistics(n, xin[0:ROWS[i], HROW[i], :], ROWS[i])
                if n:
                    norm_in(n - 1)
            norm_in(len(TOKS) - 1)

            dve.wait_ge(s("positions"), 1)
            then(V.scalar_tensor_tensor(dist[:, :], dist[:, :], -1.0, dist[:, :], ALU.mult, ALU.max))
            then(V.tensor_scalar(dist[0:CH, T - CH:T], dist[0:CH, T - CH:T], FAR, None, ALU.add))

            for k, (job, name, j) in enumerate((("ssq", "q_g", 0), ("ssq", "q_g", 1), ("sskv", "kv_g", 0))):
                root = tmpA[:, 0 if job == "ssq" else 2, :]
                evacuated(dve, job)
                if k != 1:
                    then(V.reciprocal(root, root))
                V.scalar_tensor_tensor(aRaw[:, k, :], aRaw[:, k, :], par(name, j), root, ALU.mult, ALU.mult).then_inc(s("low_normed"), 1)
            dve.wait_ge(s("low_normed"), 3)
            key = aRaw[0:IDX, 3, :]
            product(dve, "kmean")
            empties(V.scalar_tensor_tensor(halves(key), banks("kmean", HALF)[0:IDX], -1.0 / IDX, halves(key), ALU.mult, ALU.add), "kmean")
            v0, t1, y = tmpA[0:IDX, 0, :], tmpA[0:IDX, 2, :], kiT[0:IDX, :]
            product(dve, "kvar")
            empties(V.tensor_scalar(halves(v0), banks("kvar", HALF)[0:IDX], 1.0 / IDX, LN_EPS, ALU.mult, ALU.add), "kvar")
            dve.wait_ge(s("key_root"), 1)
            then(V.reciprocal(y, y))
            then(V.tensor_tensor(t1, v0, y, ALU.mult))
            then(V.tensor_tensor(t1, t1, y, ALU.mult))
            then(V.tensor_scalar(t1, t1, -0.5, 1.5, ALU.mult, ALU.add))
            then(V.tensor_tensor(y, y, t1, ALU.mult))
            then(V.tensor_tensor(y, y, key, ALU.mult))
            V.tensor_scalar(y, y, par("i_g")[0:IDX], par("i_b")[0:IDX], ALU.mult, ALU.add).then_inc(s("index_keys"), 1)

            then(V.memset(m8[:, 1, :], TAKEN))
            evacuated(dve, "widx")
            n_sum = 0
            for i in IX_ORDER:
                n = KEYS[i]
                sc = SC[:, sum(KEYS[:i]):sum(KEYS[:i]) + n]
                for h in range(HEADS):
                    evacuated(dve, f"ix{i}_{h}")
                    if n_sum:
                        dve.wait_ge(s("index_sum"), n_sum)
                    v, w = relu[:, n_sum % 2, 0:n], wix[:, i, h:h + 1]
                    ins = V.scalar_tensor_tensor(sc, v, w, sc, ALU.mult, ALU.add) if h else V.tensor_scalar(sc, v, w, None, ALU.mult)
                    ins.then_inc(s("index_sum"), 1)
                    n_sum += 1
                dve.wait_ge(s("index_sum"), n_sum)
                then(V.memset(sc[0:CH, n - CH:n], INVISIBLE))
                for _ in range(TOPK // 8):
                    then(V.max(m8[:, 0, :], sc))
                    then(V.match_replace(sc, m8[:, 0, :], sc, TAKEN))
                then(V.max(m8[:, 0, :], sc))
                then(V.tensor_copy(m8[:, 1, 0:TOPK % 8], m8[:, 0, 0:TOPK % 8]))
                then(V.match_replace(sc, m8[:, 1, :], sc, TAKEN))
                then(V.tensor_scalar(sc, sc, TAKEN_BELOW, FAR, ALU.is_gt, ALU.mult))
                then(V.tensor_tensor(sc, sc, distances(i), ALU.add))

            product(dve, f"p_{PROJ[-1]}")
            V.memset(flat(csig), 0.0).then_inc(s("cleared"), 1)
            V.memset(aT[:, :, 0:PAD], 0.0).then_inc(s("cleared"), 1)
            dve.wait_ge(s("shifted"), len(SHIFTED))
            then(V.memset(reset, 1.0))
            V.memset(reset.rearrange("p (c t) -> p c t", t=CH + 1)[:, :, 0:1], 0.0).then_inc(s("cleared"), 1)
            dve.wait_ge(s("cleared"), 3)
            for j in range(NJ):
                evacuated(dve, f"z{j}")
                V.tensor_tensor_scan(csig[:, j, :], reset, csig[:, j, :], 0.0, ALU.mult, ALU.add).then_inc(s("summed"), 1)
            for j in range(NJ):
                grow = csig[:, j, :].rearrange("p (c t) -> p c t", t=CH + 1)[:, :, 1:]
                decay = Pp[:, j, :].rearrange("p (c t) -> p c t", t=CH + 1)
                chunks = lambda v: v.rearrange("p (c t) -> p c t", t=CH)
                a_, r_, k_, b_ = AR[:, j, 0, :], AR[:, j, 1, :], KT[:, j, :], BT[:, j, :]
                evacuated(dve, f"ss{j}")
                then(V.tensor_scalar(a_, a_, 1e-12, None, ALU.max))
                then(V.reciprocal(a_, a_))
                then(V.scalar_tensor_tensor(a_, k_, par("k_k", j), a_, ALU.mult, ALU.mult))
                evacuated(dve, f"a{j}")
                then(V.tensor_scalar(b_, aT[:, j, :], -1.0, par("k_a", j), ALU.add, ALU.mult))
                then(V.scalar_tensor_tensor(k_, b_, 1.0, k_, ALU.add, ALU.mult))
                product(dve, f"bo{j - 1}" if j else f"ss{NJ - 1}")
                V.scalar_tensor_tensor(tw[:, 0, :], r_, par("r_k", j), k_, ALU.mult, ALU.mult).then_inc(s("bonus_in"), 1)
                then(V.tensor_tensor(b_, a_, aT[:, j, :], ALU.mult))
                dve.wait_ge(s("decay"), 2 * j + 2)
                V.tensor_tensor(chunks(b_), chunks(b_), grow, ALU.mult).then_inc(s("prepped"), 1)
                dve.wait_ge(s("bonus_in"), j + 1)
                V.tensor_tensor(chunks(k_), chunks(k_), grow, ALU.mult).then_inc(s("prepped"), 1)
                V.tensor_tensor(chunks(r_), chunks(r_), decay[:, :, 1:], ALU.mult).then_inc(s("prepped"), 1)
                V.scalar_tensor_tensor(chunks(a_), chunks(a_), -1.0, decay[:, :, 0:CH], ALU.mult, ALU.mult).then_inc(s("prepped"), 1)
                V.tensor_copy(PL[:, j, :], decay[:, :, CH]).then_inc(s("prepped"), 1)
                product(dve, f"bo{j}")
                empties(V.tensor_tensor(halves(BONUS[:, j, :]), halves(VY[:, j, :]), banks(f"bo{j}", HP), ALU.mult), f"bo{j}")
            dve.wait_ge(s("prepped"), 5 * NJ)
            V.memset(flat(DI), 0.0).then_inc(s("no_inverses"), 1)
            dve.wait_ge(s("no_inverses"), 1)

            def scores(p):
                rows, b = slice(0, CH * len(PAIRS[p])), BUF[p]
                m = mask[rows, :].rearrange("p (o n) -> p o n", o=1).to_broadcast([rows.stop, 2, P])
                for half in range(2):
                    job = f"sc{p}_{half}"
                    product(dve, job)
                    for n in range(4):
                        j, h = 2 * half + n // 2, n % 2
                        dst = MSX[rows, b, j, h, :].rearrange("p (g n) -> p g n", g=2)[:, :, 0:P]
                        lo = 512 * h + 256 * (n // 2)
                        src = slot(job)[rows, lo:lo + 256].rearrange("p (g n) -> p g n", g=2)
                        last = V.tensor_tensor(dst, src, m, ALU.mult)
                    empties(last, job)

            def invert(g):
                r = BLOCKS[g]
                dve.wait_ge(s("blocks_here"), 16 * (g + 1))
                if g:
                    dve.wait_ge(s("inverses_out"), 16 * g)
                then(V.tensor_copy(Xi[0:r, :], Ni[0:r, :]))
                then(V.memset(Xi[0:r, 0:BLK * BLK:BLK + 1], 1.0))
                N3 = Ni[0:r, :].rearrange("i (s t) -> i s t", t=BLK)
                X3 = Xi[0:r, :].rearrange("i (s t) -> i s t", t=BLK)
                for j in range(1, BLK - 1):
                    w = BLK - 1 - j
                    new = Ti[0:r, 0:j * w].rearrange("i (c t) -> i c t", c=j)
                    then(V.tensor_tensor(new, N3[:, j:j + 1, j + 1:BLK].to_broadcast([r, j, w]),
                                         X3[:, 0:j, j:j + 1].to_broadcast([r, j, w]), ALU.mult))
                    then(V.tensor_tensor(X3[:, 0:j, j + 1:BLK], X3[:, 0:j, j + 1:BLK], new, ALU.add))
                V.tensor_copy(Ti[0:r, 0:1], Xi[0:r, 0:1]).then_inc(s("inverted"), 1)

            def attend(i):
                r, nk = ROWS[i], NKEYS[i]
                far = distances(i) if i == META_TILE else SC[:, sum(KEYS[:i]):sum(KEYS[:i]) + nk]
                for h in range(HEADS + 1):
                    if h < HEADS:
                        k = ATT[i, h]
                        job = f"S{i}_{h}"
                        product(dve, job)
                        if k >= 2:
                            dve.wait_ge(s("exp"), k - 1)
                        L = Lb[0:r, k % 2, 0:nk]
                        empties(V.scalar_tensor_tensor(L, far, -SLOPES[h], slot(job)[0:r, 0:nk], ALU.mult, ALU.add), job)
                        evacuated(dve, job)
                        V.tensor_reduce(nmax[0:r, h:h + 1], L, AX.X, ALU.max, negate=True).then_inc(s("max"), 1)
                    if h >= 1:
                        k = ATT[i, h - 1]
                        dve.wait_ge(s("exp"), k + 1)
                        if k >= HEADS:
                            dve.wait_ge(s("probs"), k - HEADS + 1)
                        V.reciprocal(rinv[0:r, h - 1:h], rsum[0:r, h - 1:h]).then_inc(s("rinv"), 1)

            def local(p):
                b, n_ch = BUF[p], len(PAIRS[p])
                job = f"nu_{p}"
                product(dve, job)
                for c in range(n_ch):
                    second = slice(CH * c + BLK, CH * (c + 1))
                    last = V.tensor_tensor(flat(R[second, b]), flat(R[second, b]), slot(job)[second, :], ALU.add)
                empties(last, job)
                job = f"qg_{p}"
                product(dve, job)
                v = slot(job)[:, :].rearrange("p (c j n) -> p j c n", j=NJ, c=2)
                eye = eye2[:, :].rearrange("p (o n) -> p o n", o=1).to_broadcast([P, NJ, CH])
                for c in range(n_ch):
                    r_ = AR[:, :, 1, CH * (PAIRS[p][c]):CH * (PAIRS[p][c] + 1)]
                    V.tensor_tensor(QB[:, :, c, :], v[:, :, c, 0:CH], r_, ALU.add)
                    last = V.tensor_tensor(GT[:, :, c, :], v[:, :, c, CH:P], eye, ALU.add)
                empties(last, job)

            def chain(p):
                evacuated(dve, f"hy_{p}")
                for n, c in enumerate(PAIRS[p]):
                    new, decay = Z[:, (c + 1) % 2], PL[:, :, c:c + 1].to_broadcast([P, NJ, CH])
                    if c:
                        job = f"zy_{c}"
                        product(dve, job)
                        v = slot(job)[:, :].rearrange("p (b j t) -> p b j t", b=2, j=2 * NJ)[:, :, 0:NJ]
                        then(V.tensor_tensor(new, v[:, 0], H[:, n], ALU.add))
                        V.tensor_tensor(new, new, decay, ALU.mult).then_inc(s("state"), 1)
                        y = VY[:, :, CH * c:CH * (c + 1)]
                        empties(V.tensor_tensor(y, y, v[:, 1], ALU.add), job)
                    else:
                        V.tensor_tensor(new, H[:, n], decay, ALU.mult).then_inc(s("state"), 1)

            def center(_):
                for j in range(NJ):
                    product(dve, f"ym{j}")
                    y = halves(VY[:, j, PAD:TP])
                    empties(V.scalar_tensor_tensor(y, banks(f"ym{j}", HALF), -1.0 / HD, y, ALU.mult, ALU.add), f"ym{j}")

            stages = {"scores": scores, "invert": invert, "attend": attend, "local": local, "chain": chain, "center": center}
            for stage, n in mixers():
                stages[stage](n)
            for j in range(NJ):
                y, root = VY[:, j, PAD:TP], Pb[:, j % 2, :]
                evacuated(dve, f"yv{j}")
                then(V.reciprocal(root, root))
                then(V.tensor_tensor(y, y, root, ALU.mult))
                then(V.tensor_scalar(y, y, par("gn_g", j), par("gn_b", j), ALU.mult, ALU.add))
                then(V.tensor_tensor(y, y, BONUS[:, j, PAD:TP], ALU.add))
                product(dve, f"g{j}")
                empties(V.tensor_tensor(halves(y), halves(y), banks(f"g{j}", HALF), ALU.mult), f"g{j}")

            def residual(job, k, i):
                ht = h_tok[0:ROWS[i], HROW[i], :]
                product(dve, job)
                empties(V.scalar_tensor_tensor(ht, ht, ALPHA, slot(job)[0:ROWS[i], :], ALU.mult, ALU.add), job)
                evacuated(dve, job)
                statistics(k, ht, ROWS[i])

            dve.wait_ge(s("gains"), 64)
            for n, i in enumerate(TOKS):
                ht = h_tok[0:ROWS[i], HROW[i], :]
                residual(f"mix{i}", 5 + n, i)
                normalise(5 + n, ht, ht, ROWS[i], gain1, s("mixed"))

            def gated(f):
                dve.wait_ge(s("gelu"), f + 1)
                product(dve, f"val{f}")
                empties(V.tensor_tensor(actT[:, f, :], ge[:, f % 2, :], slot(f"val{f}")[:, 0:SEQ], ALU.mult), f"val{f}")

            for f in range(NF):
                g, c_ = gs[:, f % 2, :], cv[:, f % 2, :]
                tap = lambda t: parT[:, NPAR + NF * t + f:NPAR + NF * t + f + 1]
                evacuated(dve, f"gate{f}")
                if f >= 2:
                    dve.wait_ge(s("gelu"), f - 1)
                then(V.tensor_scalar(c_, g[:, 2:SEQ + 2], tap(2), tap(CONV), ALU.mult, ALU.add))
                then(V.scalar_tensor_tensor(c_, g[:, 1:SEQ + 1], tap(1), c_, ALU.mult, ALU.add))
                V.scalar_tensor_tensor(c_, g[:, 0:SEQ], tap(0), c_, ALU.mult, ALU.add).then_inc(s("conv"), 1)
                if f >= 1:
                    gated(f - 1)
            gated(NF - 1)
            for i in range(TILES):
                residual(f"down{i}", 10 + i, i)
                normalise(10 + i, h_tok[:, i, :], h_tok[:, i, :], P, gain2, s("out_ready"))

        @block.tensor
        def _(pe):
            def begin(job):
                if JOBS[job] >= NSLOT:
                    evacuated(pe, ORDER[JOBS[job] - NSLOT])

            def end_job(ins, job):
                ins.then_inc(written[JOBS[job] % NSLOT], 1)

            def mm(dst, pairs):
                for n, (a, b) in enumerate(pairs):
                    last = pe.matmul(dst, a, b, start=n == 0, stop=n == len(pairs) - 1)
                return last

            def by_halves(job, m, pairs, n=HALF):
                for b in range(2):
                    last = mm(slot(job)[0:m, 512 * b:512 * b + n], [(a, v[:, n * b:n * (b + 1)]) for a, v in pairs])
                end_job(last, job)

            def wide(dst, a, v, n):
                for lo in range(0, n, 512):
                    hi = min(n, lo + 512)
                    last = mm(dst[:, lo:hi], [(a, v[:, lo:hi])])
                return last

            pe.wait_ge(s("const"), N_CONST)
            pe.wait_ge(s("par_in"), 16 * N_PAR_DMA)
            pe.transpose(slot("par")[:, 0:NPAR], par_rows[0:NPAR, 0:P], ident[0:NPAR, 0:NPAR])
            end_job(pe.transpose(slot("par")[:, NPAR:NPAR + 4 * NF], par_rows[0:4 * NF, P:2 * P], ident[0:4 * NF, 0:4 * NF]), "par")

            def to_features(job, i, ready, count):
                begin(job)
                pe.wait_ge(ready, count)
                r = ROWS[i]
                for k in range(KT_D):
                    last = pe.transpose(slot(job)[:, P * k:P * k + r], h_tok[0:r, HROW[i], P * k:P * (k + 1)], ident[0:r, 0:r])
                end_job(last, job)

            for n, i in enumerate(TOKS):
                to_features(f"hT{i}", i, s("normed"), n + 1)

            for i in TOKS:
                evacuated(pe, f"hT{i}")
            for job in ORDER[JOBS["p_q0"]:JOBS["z0"]]:
                kind, n = job[:2], job[2:]
                begin(job)
                if kind == "p_":
                    k = PROJ.index(n)
                    pe.wait_ge(s(f"w_ring{k % W_RING}"), 16 * (k // W_RING + 1))
                    m = COLS[n][1]
                    by_halves(job, m, [(wring[:, k % W_RING, d, 0:m], hT[:, d, :]) for d in range(KT_D)])
                elif job == "ssq":
                    evacuated(pe, "p_q1")
                    by_halves(job, P, [(ones[:, :], tmpA[:, d, :]) for d in range(2)])
                elif job == "sskv":
                    evacuated(pe, "p_kv")
                    by_halves(job, P, [(ones[:, :], tmpA[:, 2, :])])
                elif job == "kmean":
                    evacuated(pe, "p_ki")
                    by_halves(job, IDX, [(ones[0:IDX, 0:IDX], aRaw[0:IDX, 3, :])])
                elif job == "kvar":
                    pe.wait_ge(s("key_squares"), 1)
                    by_halves(job, IDX, [(ones[0:IDX, 0:IDX], tmpA[0:IDX, 1, :])])
                elif job == "widx":
                    for i in range(TILES):
                        rows = slice(IDX, IDX + HEADS)
                        last = pe.transpose(slot(job)[:, HEADS * i:HEADS * (i + 1)], aRaw[rows, 3, QCOLS[i]], ident[rows, rows])
                    end_job(last, job)
                elif kind in ("qp", "qi"):
                    w = {"qp": wuq, "qi": wiq}[kind]
                    pe.wait_ge(s("w_low"), 64)
                    pe.wait_ge(s("low_normed"), 2)
                    by_halves(job, P, [(w[:, d, P * int(n):P * (int(n) + 1)], aRaw[:, d, :]) for d in range(2)])
                elif kind == "kp":
                    pe.wait_ge(s("low_normed"), 3)
                    by_halves(job, P, [(wuk[:, P * int(n):P * (int(n) + 1)], aRaw[:, 2, :])])
                elif kind == "vp":
                    for b, i in enumerate(((META_TILE, 0), (1, 2), (3,))[int(n)]):
                        last = mm(slot(job)[0:ROWS[i], 512 * b:512 * (b + 1)], [(aRaw[:, 2, QCOLS[i]], wuv)])
                    end_job(last, job)
                else:
                    i, h = int(job[2]), int(job[4])
                    r = head_rows(h)
                    pe.wait_ge(s("index_keys"), 1)
                    if h % 2:
                        pe.wait_ge(s("index_keys2"), 16)
                    evacuated(pe, f"qi{h // 2}")
                    end_job(wide(slot(job)[:, :], qiT[r, h // 2, QCOLS[i]], kiT[r, :], KEYS[i]), job)

            for kind, rows in (("z", slice(0, 64)), ("a", slice(64, 128))):
                for j in range(NJ):
                    job = f"{kind}{j}"
                    begin(job)
                    pe.wait_ge(s("w_lora"), 32)
                    pe.wait_ge(s("lora_in"), 1)
                    w = wlora[rows, P * j:P * (j + 1)]
                    mm(slot(job)[:, 0:META], [(w, wad[rows, 0:META])])
                    end_job(mm(slot(job)[:, 512:1024], [(w, wad[rows, META:T])]), job)
            for j in range(NJ):
                begin(f"ss{j}")
                pe.wait_ge(s("kk_squares"), j + 1)
                by_halves(f"ss{j}", P, [(blk[:, :], tw[:, j % 2, :])], HP)
            for j in range(NJ):
                begin(f"bo{j}")
                pe.wait_ge(s("bonus_in"), j + 1)
                by_halves(f"bo{j}", P, [(blk[:, :], tw[:, 0, :])], HP)

            def scores(p):
                pair = PAIRS[p]
                cols = slice(CH * pair[0], CH * (pair[0] + len(pair)))
                rows = slice(0, CH * len(pair))
                pe.wait_ge(s("prepped"), 5 * NJ)
                evacuated(pe, f"bo{NJ - 1}")
                for half in range(2):
                    job = f"tk{p}_{half}"
                    begin(job)
                    for n in range(8):
                        j = 2 * half + n // 4
                        src = (AR[:, j, 0], BT[:, j], KT[:, j], VY[:, j])[n % 4]
                        last = pe.transpose(slot(job)[rows, P * n:P * (n + 1)], src[:, cols], ident[:, :])
                    end_job(last, job)
                    job = f"sc{p}_{half}"
                    begin(job)
                    for n in range(8):
                        jj, src, h = n // 4, (BT, KT)[n // 2 % 2], n % 2
                        j, lo = 2 * half + jj, 512 * h + P * (n // 2)
                        for c in range(len(pair)):
                            cc = slice(CH * pair[c], CH * (pair[c] + 1))
                            last = mm(slot(job)[chunk_rows(c), lo:lo + P],
                                      [(src[head_rows(h), j, cc], AR[head_rows(h), j, :, cc])])
                    end_job(last, job)

            def per_instance(p, job, width, product_of):
                begin(job)
                for c in range(len(PAIRS[p])):
                    for n in range(HEADS):
                        last = product_of(c, n // 2, n % 2, slice(width * n, width * (n + 1)))
                end_job(last, job)

            def local(p):
                b = BUF[p]
                g = 0 if p in GROUPS[0] else 1
                done = sum(2 * len(PAIRS[q]) for grp in GROUPS[:g + 1] for q in grp)
                pe.wait_ge(s("inverses_here"), 16 * done)
                for half in range(2):
                    evacuated(pe, f"tk{p}_{half}")
                    evacuated(pe, f"sc{p}_{half}")
                job = f"x1_{p}"
                per_instance(p, job, CH, lambda c, j, h, cols: mm(
                    slots[JOBS[job] % NSLOT][chunk_rows(c), cols],
                    [(MSX[chunk_rows(c), b, j, h, 192:256], Vtok[chunk_rows(c), b, j, h])]))
                job2 = f"u0_{p}"
                first = lambda c: slice(CH * c, CH * c + BLK)
                second = lambda c: slice(CH * c + BLK, CH * (c + 1))
                evacuated(pe, job)
                per_instance(p, job2, P, lambda c, j, h, cols: mm(
                    slot(job2)[first(c), cols], [(DI[first(c), b, j, h, 0:BLK], R[first(c), b, j, h])]))
                job3 = f"nu_{p}"
                evacuated(pe, job2)
                per_instance(p, job3, P, lambda c, j, h, cols: mm(
                    slot(job3)[second(c), cols], [(MSX[first(c), b, j, h, BLK:2 * BLK], U0[first(c), j, h])]))
                job4 = f"u_{p}"
                evacuated(pe, job3)
                per_instance(p, job4, P, lambda c, j, h, cols: mm(
                    slot(job4)[chunk_rows(c), cols], [(DI[chunk_rows(c), b, j, h], R[chunk_rows(c), b, j, h])]))
                job5 = f"qg_{p}"
                evacuated(pe, job4)
                begin(job5)
                for c in range(len(PAIRS[p])):
                    for j in range(NJ):
                        for h in range(2):
                            lo = 512 * c + P * j
                            last = mm(slot(job5)[head_rows(h), lo:lo + P],
                                      [(R[chunk_rows(c), b, j, h, CH:P], MSX[chunk_rows(c), b, j, h, 64:192])])
                end_job(last, job5)
                job6 = f"hy_{p}"
                begin(job6)
                for c in range(len(PAIRS[p])):
                    r = chunk_rows(c)
                    for j in range(NJ):
                        for h in range(2):
                            u, v, m = R[r, b, j, h, 0:CH], Vtok[r, b, j, h], MSX[r, b, j, h]
                            lo = 512 * c + CH * j
                            mm(slot(job6)[head_rows(h), lo:lo + CH], [(m[:, 128:192], u), (m[:, 320:384], v)])
                            lo += NJ * CH
                            last = mm(slot(job6)[head_rows(h), lo:lo + CH], [(u, m[:, 64:128]), (v, m[:, 256:320])])
                end_job(last, job6)

            def chain(p):
                evacuated(pe, f"qg_{p}")
                for n, c in enumerate(PAIRS[p]):
                    if not c:
                        continue
                    job = f"zy_{c}"
                    begin(job)
                    pe.wait_ge(s("state"), c)
                    for k in range(2):
                        for j in range(NJ):
                            for h in range(2):
                                hr = head_rows(h)
                                z = Z[hr, c % 2, j]
                                term = (GT[hr, j, n], z) if k == 0 else (z, QB[hr, j, n])
                                last = mm(slot(job)[hr, 512 * k + CH * j:512 * k + CH * (j + 1)], [term])
                    end_job(last, job)

            def attend(i):
                r, nk = ROWS[i], NKEYS[i]
                for n in range(HEADS + 3):
                    if n < HEADS:
                        job, hr = f"S{i}_{n}", head_rows(n)
                        begin(job)
                        end_job(wide(slot(job)[0:r, :], qT[hr, n // 2, QCOLS[i]], kT[hr, n // 2, :], nk), job)
                    if 2 <= n < HEADS + 2:
                        k = ATT[i, n - 2]
                        job = f"T{i}_{n - 2}"
                        begin(job)
                        pe.wait_ge(s("probs"), k + 1)
                        last = pe.transpose(slot(job)[0:META, 0:r], Pb[0:r, k % 2, 0:META], ident[0:r, 0:r])
                        for lo in range(META, nk, P):
                            last = pe.transpose(slot(job)[:, lo + P - META:lo + 2 * P - META], Pb[0:r, k % 2, lo:lo + P], ident[0:r, 0:r])
                        end_job(last, job)
                    if n >= 3:
                        h = n - 3
                        k = ATT[i, h]
                        job, cols = f"O{i}_{h}", slice(HD * h, HD * (h + 1))
                        begin(job)
                        evacuated(pe, f"T{i}_{h}")
                        terms = [(vtok[0:META, TILES, cols], PTm[0:META, k % 2, 0:r])]
                        if i != META_TILE:
                            terms += [(vtok[:, t, cols], PT[:, k % 2, P * t:P * (t + 1)]) for t in range(i + 1)]
                        end_job(mm(slot(job)[head_rows(h), 0:r], terms), job)

            def center(_):
                for p in range(len(PAIRS)):
                    evacuated(pe, f"hy_{p}")
                for c in range(1, NCH):
                    evacuated(pe, f"zy_{c}")
                for j in range(NJ):
                    begin(f"ym{j}")
                    by_halves(f"ym{j}", P, [(blk[:, :], VY[:, j, PAD:TP])])

            stages = {"scores": scores, "attend": attend, "local": local, "chain": chain, "center": center}
            for stage, n in mixers():
                if stage in stages:
                    stages[stage](n)
            for j in range(NJ):
                begin(f"yv{j}")
                pe.wait_ge(s("y_squares"), j + 1)
                by_halves(f"yv{j}", P, [(blk[:, :], Lb[:, j % 2, :])])
                begin(f"g{j}")
                pe.wait_ge(s("w_gate"), 16)
                by_halves(f"g{j}", P, [(wgate[:, P * j:P * (j + 1)], sgd)])

            pe.wait_ge(s("w_out"), 32)
            for j in range(NJ):
                evacuated(pe, f"g{j}")
            for i in TOKS:
                job = f"mix{i}"
                begin(job)
                for b in range(2):
                    cols = slice(512 * b, 512 * (b + 1))
                    last = mm(slot(job)[0:ROWS[i], cols],
                              [(qT[:, j, QCOLS[i]], wout[:, j, cols]) for j in range(NJ)] +
                              [(VY[:, j, YCOLS[i]], wout[:, NJ + j, cols]) for j in range(NJ)])
                end_job(last, job)
            for n, i in enumerate(TOKS):
                to_features(f"h1T{i}", i, s("mixed"), n + 1)

            for i in TOKS:
                evacuated(pe, f"h1T{i}")
            for f in range(NF):
                pe.wait_ge(s(f"w_up{f % 3}"), 32 * (f // 3 + 1))
                begin(f"gate{f}")
                by_halves(f"gate{f}", P, [(wup[:, f % 3, 0, d, :], h1T[:, d, :]) for d in range(KT_D)], SEQ // 2 + 1)
                job = f"val{f}"
                begin(job)
                end_job(mm(slot(job)[:, 0:SEQ], [(wup[:, f % 3, 1, d, :], h1T[:, d, CONV - 1:]) for d in range(KT_D)]), job)

            for f in range(NF):
                evacuated(pe, f"val{f}")
            pe.wait_ge(s("w_down"), 16 * 16)
            pe.wait_ge(s("w_down2"), 16 * (NF - 16))
            for i in range(TILES):
                job = f"down{i}"
                begin(job)
                for b in range(2):
                    cols = slice(512 * b, 512 * (b + 1))
                    last = mm(slot(job)[:, cols], [(actT[:, f, P * i:P * (i + 1)], (wdn[:, f] if f < 16 else wdn2[:, f - 16])[:, cols])
                                                   for f in range(NF)])
                end_job(last, job)


_INS = ['x', 'meta', 'ln_in_g', 'ln_in_b', 'w_in', 'q_norm_g', 'w_uq', 'kv_norm_g', 'w_ukv', 'w_iq', 'idx_ln_g', 'idx_ln_b',
        'mu_shift', 'w0', 'w_decay_up', 'a0', 'w_aaa_up', 'w_gate_up', 'k_k', 'k_a', 'r_k', 'gn_g', 'gn_b', 'w_out',
        'ln1_g', 'ln1_b', 'w_ffn_up', 'conv_w', 'conv_b', 'w_ffn_down', 'ln2_g', 'ln2_b']
_OUTS = [((1, SEQ, D), 'float32')]


def kernel(**inputs):
    import numpy as _np
    import concourse.bacc as _bacc
    from concourse import mybir as _mybir
    from concourse.bass_utils import run_bass_kernel_spmd as _run

    nc = _bacc.Bacc("TRN2", target_bir_lowering=False, num_devices=1)
    arrays, args = {}, []
    for name in _INS:
        a = _np.ascontiguousarray(inputs[name])
        arrays[f"in_{name}_dram"] = a
        args.append(nc.dram_tensor(f"in_{name}_dram", a.shape, _mybir.dt.from_np(a.dtype), kind="ExternalInput").ap())
    for i, (shape, dtype) in enumerate(_OUTS):
        dt = _mybir.dt.from_np(_np.dtype(dtype))
        args.append(nc.dram_tensor(f"out_{i}_dram", shape, dt, kind="ExternalOutput").ap())
    hymba(nc, *args)
    r = _run(nc, [arrays], core_ids=[0])
    return r.results[0]["out_0_dram"]
```

```python
from contextlib import ExitStack

import concourse.bass as bass
from concourse import mybir

F32 = mybir.dt.float32
F32R = mybir.dt.float32r
ALU = mybir.AluOpType
ACT = mybir.ActivationFunctionType
AX = mybir.AxisListType

P = 128
D = 1024
KT_D = D // P
SEQ, META = 512, 16
T = SEQ + META
HALF = T // 2
TILES = SEQ // P
CH = 64
PAD = CH - META
NCH = SEQ // CH + 1
TP = NCH * CH
HP = TP // 2
HEADS, HD = 8, 64
NJ = HEADS // 2
Q_RANK, KV_RANK, IDX = 256, 128, 64
A_COLS = Q_RANK + KV_RANK + IDX + HEADS
TOPK = T // 4
FF = 2816
NF = FF // P
CONV = 3
LN_EPS, RMS_EPS, GN_EPS = 1e-5, 1e-6, 64e-5
ALPHA = 2.0 ** 0.25
KAPPA = 0.6065306597126334
IDX_SCALE = HEADS ** -0.5 * IDX ** -0.5
INVISIBLE, TAKEN, TAKEN_BELOW = -3.0e38, -3.4e38, -3.2e38
FAR = 1.0e34
SLOPES = [2.0 ** (-8.0 * (h + 1) / HEADS) for h in range(HEADS)]
KEYS = [META + P * (i + 1) for i in range(TILES)]

META_TILE = "m"
TOKS = [META_TILE] + list(range(TILES))
IX_ORDER = (3, 2, 1, 0)

COLS = {"q0": (0, 128), "q1": (128, 128), "kv": (256, 128), "ki": (384, 128),
        "wa": (A_COLS + 3 * 512, 128), "gd": (A_COLS + 3 * 512 + 128, 128)}
COLS |= {f"{x}{j}": (A_COLS + 512 * n + P * j, 128) for j in range(NJ) for n, x in enumerate("rkv")}
PROJ = list(COLS)
SHIFTED = PROJ[4:]
PAR_ROWS = (("mu", 14), ("w0", 4), ("a0", 4), ("k_k", 4), ("k_a", 4), ("r_k", 4), ("gn_g", 4), ("gn_b", 4),
            ("q_g", 2), ("kv_g", 1), ("i_g", 1), ("i_b", 1))
PAR = {name: sum(r for _, r in PAR_ROWS[:n]) for n, (name, _) in enumerate(PAR_ROWS)}
NPAR = sum(r for _, r in PAR_ROWS)
MU_TILE = {f"{x}{j}": 4 * n + j for n, x in enumerate("rkv") for j in range(NJ)} | {"wa": 12, "gd": 13}

PAIRS = [(0,)] + [(2 * i + 1, 2 * i + 2) for i in range(TILES)]
BUF = [0, 1, 2, 0, 1]
GROUPS = [[0, 1, 2], [3, 4]]
BLK = 32
FIRST_BLOCK = {p: sum(16 * len(PAIRS[q]) for q in g if q < p) for g in GROUPS for p in g}
BLOCKS = [sum(16 * len(PAIRS[p]) for p in g) for g in GROUPS]


PIECES = [range(j, min(j + 5, BLK - 1)) for j in range(1, BLK - 1, 5)]


def scores(p):
    return [(kind, p, half) for half in range(2) for kind in ("tk", "sc")]


def inversion(g):
    return [("inv", g, n) for n in range(len(PIECES))]


def local(p):
    return [(kind, p) for kind in ("x", "u0", "nu", "u", "qg", "hy")] + [("zy", c) for c in PAIRS[p]]


def attention(i):
    steps = []
    for n in range(HEADS + 3):
        for kind, h in (("S", n), ("V", n - 1), ("T", n - 2), ("O", n - 3), ("E", n)):
            if 0 <= h < HEADS:
                steps.append((kind, i, h))
    return steps


def merged(a, b):
    out, k = [], 0
    for n, step in enumerate(a):
        out.append(step)
        while k < len(b) and (k + 1) * len(a) <= (n + 1) * len(b):
            out.append(b[k])
            k += 1
    return out + b[k:]


def mixers():
    steps = [(kind, j) for kind in ("z", "a", "ss", "sum") for j in range(NJ)]
    steps += merged(attention(3), [("bo", j) for j in range(NJ)])
    steps += scores(0) + scores(1) + scores(2)
    rwkv = inversion(0) + local(0) + local(1) + scores(3) + scores(4) + local(2)
    rwkv += inversion(1) + local(3) + local(4)
    att = attention(2) + attention(1) + attention(0) + attention(META_TILE)
    return steps + merged(att, rwkv) + [("ym", j) for j in range(NJ)]


RAW, RING = 2, 3
KEPT = list(range(NF - 4, NF))
STREAMED = list(range(NF - 4 - RING))


def weight_units():
    units = [f"p_{name}" for name in PROJ] + [f"{x}{f}" for f in range(NF) for x in ("gate", "val")]
    rest = [f for f in range(NF) if f not in KEPT]
    for n, f in enumerate(rest):
        units.append(f"down_{f}")
        if n in (3, 5, 7, 9):
            units.append(f"down_{KEPT[(n - 3) // 2]}")
    return units


UNITS = weight_units()
IN_RING = [n for n, name in enumerate(UNITS) if name not in [f"down_{f}" for f in KEPT]]
UNIT = {name: n for n, name in enumerate(UNITS)}
FIRST_UP = len(PROJ)
POOL_UNITS = range(11, len(PROJ), 2)


def name_of(step):
    return "_".join(map(str, step))


NO_SLOT = ("V", "E", "inv", "sum")
MIXERS = mixers()


def psum_jobs():
    jobs = [f"hT{i}" for i in TOKS] + ["par"]
    jobs += ["p_q0", "p_q1", "p_kv", "p_ki", "ssq", "sskv", "p_wa", "kmean", "p_gd", "kvar", "widx"]
    jobs += [f"qi{j}" for j in range(NJ)] + ["p_r0"] + [f"qp{j}" for j in range(NJ)] + ["p_k0"]
    jobs += [f"kp{j}" for j in range(NJ)] + ["vp0", "vp1", "vp2"]
    rest = [f"p_{n}" for n in PROJ[8:]]
    for i in IX_ORDER:
        for h in range(HEADS):
            jobs.append(f"ix{i}_{h}")
            if h % 4 == 3 and i > 1:
                jobs.append(rest.pop(0))
    jobs += rest
    jobs += [name_of(step) for step in MIXERS if step[0] not in NO_SLOT and step != ("zy", 0)]
    for j in range(NJ):
        jobs += [f"yv{j}", f"g{j}"]
    jobs += [f"mix{i}" for i in TOKS]
    jobs += [f"h1T{i}" for i in TOKS]
    for f in range(NF):
        jobs += [f"gate{f}", f"val{f}"]
    return jobs + [f"down{i}" for i in range(TILES)]


ORDER = psum_jobs()
JOBS = {name: n for n, name in enumerate(ORDER)}


def due(job):
    n = RING + sum(name in JOBS and JOBS[name] < JOBS[job] for name in UNITS)
    return min(n, len(PROJ)) if JOBS[job] < JOBS["z_0"] else n


NSLOT = 4
ATT = {step[1:]: n for n, step in enumerate(st for st in MIXERS if st[0] == "S")}
ATT_LIST = list(ATT)
N_CONST = 18
N_PAR_DMA = 16
ROWS = {i: P for i in range(TILES)} | {META_TILE: META}
NKEYS = {i: KEYS[i] for i in range(TILES)} | {META_TILE: META}
QCOLS = {i: slice(META + P * i, META + P * (i + 1)) for i in range(TILES)} | {META_TILE: slice(0, META)}
YCOLS = {i: slice(CH + P * i, CH + P * (i + 1)) for i in range(TILES)} | {META_TILE: slice(PAD, CH)}
H1COLS = {i: slice(CONV - 1 + P * i, CONV - 1 + P * (i + 1)) for i in range(TILES)} | {META_TILE: slice(0, CONV - 1)}
H1FROM = {i: 0 for i in range(TILES)} | {META_TILE: META - CONV + 1}
GATE_AT = 254
HROW = {i: i for i in range(TILES)} | {META_TILE: TILES}


def head_rows(h):
    return slice(HD * (h % 2), HD * (h % 2) + HD)


def chunk_rows(c):
    return slice(CH * c, CH * c + CH)


def flat(v):
    n = len(v.shape)
    names = " ".join("abcde"[:n - 1])
    return v.rearrange(f"p {names} -> p ({names})")


def halves(v):
    return v.rearrange("p (b c) -> p b c", b=2)


def hymba(nc, x, meta, ln_in_g, ln_in_b, w_in, q_norm_g, w_uq, kv_norm_g, w_ukv, w_iq,
          idx_ln_g, idx_ln_b, mu_shift, w0, w_decay_up, a0, w_aaa_up, w_gate_up,
          k_k, k_a, r_k, gn_g, gn_b, w_out, ln1_g, ln1_b, w_ffn_up, conv_w, conv_b,
          w_ffn_down, ln2_g, ln2_b, out):
    with ExitStack() as ctx:
        def sb(name, *shape):
            return ctx.enter_context(nc.sbuf_tensor(name, [P, *shape], F32))

        ident, ones, blk, mask, eye2 = sb("ident", P), sb("ones", P), sb("blk", P), sb("mask", P), sb("eye2", CH)
        dist = sb("dist", T)
        parT = sb("parT", NPAR + 4 * NF)
        h_tok = sb("h_tok", TILES + 1, D)
        stats, mv, mhalf, eps = sb("stats", 2, 6), sb("mv", 2, 4), sb("mhalf", 1), sb("eps", 3)
        wix = sb("wix", TILES, HEADS)
        m8 = sb("m8", 2, 8)
        nmax, rsum, rinv = sb("nmax", HEADS), sb("rsum", HEADS), sb("rinv", HEADS)
        Z = sb("Z", 2, NJ, HD)
        PL = sb("PL", NJ, NCH)
        SIZE = 46144
        arena_at = -(-nc.sbuf_base // 32) * 32
        sb("arena", SIZE)
        slots = [ctx.enter_context(nc.psum_tensor(f"slot{i}", [P, 1024], F32)) for i in range(NSLOT)]
        blocks_in = nc.dram_tensor("blocks_in", (sum(BLOCKS), BLK, BLK), F32, kind="Internal").ap()
        blocks_out = nc.dram_tensor("blocks_out", (sum(BLOCKS), BLK, BLK), F32, kind="Internal").ap()

        end = {}

        def lay(at, parts=False, **shapes):
            views = []
            for name, shape in shapes.items():
                n = 1
                for d in shape:
                    n *= d
                at = -(-at // 8) * 8
                assert at + n <= SIZE, (name, at + n)
                v = nc.alloc_sbuf_tensor_at(name, [P, n], F32R if parts else F32, offset=arena_at + 4 * at)[:, :]
                at += n
                end[name] = at
                if len(shape) > 1:
                    dims = "abcd"[:len(shape)]
                    v = v.rearrange(f"p ({' '.join(dims)}) -> p {' '.join(dims)}", **dict(zip(dims, shape)))
                views.append(v)
            return views

        AR, KT, BT, BONUS, VY, qT, kT, vtok, SC, praw, ptmp, wad, sgd = lay(
            0, AR=(2, NJ, TP), KT=(NJ, TP), BT=(NJ, TP), BONUS=(NJ, TP), VY=(NJ, TP), qT=(NJ, T), kT=(NJ, T),
            vtok=(TILES + 1, 512), SC=(sum(KEYS),), praw=(3, 1 + T), ptmp=(T,), wad=(T,), sgd=(T,))
        base = end["sgd"]
        w_hi, w_lo, hT_hi = lay(base, parts=True, w_hi=(RING, KT_D * P), w_lo=(RING, KT_D * P), hT_hi=(KT_D, T))
        hT_lo, = lay(end["KT"], parts=True, hT_lo=(KT_D, T))
        assert end["hT_lo"] <= end["BONUS"]
        w_raw, = lay(0, w_raw=(RAW, KT_D * P))
        assert end["w_raw"] <= NJ * TP
        aRaw, tmpA, kiT, wuq, wiq, wuk, wuv, qiT, relu = lay(
            end["hT_hi"], aRaw=(4, T), tmpA=(3, T), kiT=(T,), wuq=(2, 512), wiq=(2, 512),
            wuk=(512,), wuv=(512,), qiT=(NJ, T), relu=(2, T))
        xin, = lay(end["VY"], xin=(TILES + 1, D))
        assert end["xin"] <= end["vtok"]
        gain_in, = lay(end["wuv"], gain_in=(2, D))
        par_rows = flat(tmpA)[:, 0:2 * P]
        csig, aT, Pp, wlora = lay(base, csig=(NJ, NCH * 65), aT=(NJ, TP), Pp=(NJ, NCH * 65), wlora=(512,))
        assert end["wlora"] <= end["hT_hi"]
        tw = flat(tmpA)[:, 0:2 * TP].rearrange("p (a b) -> p a b", a=2)
        reset = flat(praw)[:, 0:NCH * 65]
        wgate = wad[:, 0:512]
        R, Vtok, Ni, Xi, Ti, QB, GT, U0, MSX, DI, PT, PTm = lay(
            base, R=(3, NJ, 2, P), Vtok=(3, NJ, 2, HD), Ni=(BLK * BLK,), Xi=(BLK * BLK,), Ti=(256,), QB=(NJ, 2, HD),
            GT=(NJ, 2, HD), U0=(NJ, 2, P), MSX=(3, NJ, 2, 384), DI=(3, NJ, 2, HD), PT=(2, 4 * P), PTm=(2, P))
        H = flat(U0)[:, 0:2 * NJ * HD].rearrange("p (c j v) -> p c j v", c=2, j=NJ)
        Lb, Pb = lay(end["SC"], Lb=(2, T), Pb=(2, T))
        assert end["Pb"] <= end["ptmp"]
        wout, = lay(0, wout=(KT_D, D))
        assert end["wout"] <= end["BT"]
        act_hi, act_lo = lay(0, parts=True, act_hi=(NF, SEQ), act_lo=(NF, SEQ))
        gs, cv = lay(end["act_lo"], gs=(2, SEQ + 2), cv=(2, SEQ))
        h1T_hi, h1T_lo, u_hi, u_lo = lay(
            base, parts=True, h1T_hi=(KT_D, SEQ + 2), h1T_lo=(KT_D, SEQ + 2), u_hi=(RING, KT_D * P), u_lo=(RING, KT_D * P))
        u_raw, gain1, gain2 = lay(end["u_lo"], u_raw=(RAW, KT_D * P), gain1=(2, D), gain2=(2, D))
        k_hi, k_lo = lay(base, parts=True, k_hi=(len(KEPT), D), k_lo=(len(KEPT), D))
        assert end["cv"] <= base and end["k_lo"] <= end["h1T_lo"]

        written = [ctx.enter_context(nc.semaphore(f"slot{i}_written")) for i in range(NSLOT)]
        emptied = [ctx.enter_context(nc.semaphore(f"slot{i}_emptied")) for i in range(NSLOT)]
        named = {}

        def s(name):
            if name not in named:
                named[name] = ctx.enter_context(nc.semaphore(name))
            return named[name]

        def slot(job):
            return slots[JOBS[job] % NSLOT]

        def banks(job, n):
            return halves(slot(job)[:, :])[:, :, 0:n]

        def product(eng, job):
            eng.wait_ge(written[JOBS[job] % NSLOT], JOBS[job] // NSLOT + 1)

        def empties(ins, job):
            ins.then_inc(emptied[JOBS[job] % NSLOT], 1)

        def evacuated(eng, job):
            eng.wait_ge(emptied[JOBS[job] % NSLOT], JOBS[job] // NSLOT + 1)

        def ring(u):
            return IN_RING.index(u)

        def raw_weights(u):
            return (w_raw if u < FIRST_UP else u_raw)[:, u % RAW]

        def weight_parts(u):
            if u not in IN_RING:
                k = KEPT.index(int(UNITS[u][5:]))
                return k_hi[:, k], k_lo[:, k]
            hi, lo = (w_hi, w_lo) if u < FIRST_UP else (u_hi, u_lo)
            return hi[:, ring(u) % RING], lo[:, ring(u) % RING]

        def unit_used(eng, u):
            if UNITS[u] in JOBS:
                product(eng, UNITS[u])
            else:
                eng.wait_ge(s("rows_used"), int(UNITS[u][5:]) + 1)

        def room_for(eng, u):
            if u not in IN_RING:
                product(eng, f"val{NF - 1}")
            elif ring(u) >= RING:
                unit_used(eng, IN_RING[ring(u) - RING])

        def low_part_made(eng, u):
            on_pool = sum(n <= u for n in POOL_UNITS)
            if u in POOL_UNITS:
                eng.wait_ge(s("low_pool"), on_pool)
            else:
                eng.wait_ge(s("low"), u + 1 - on_pool)

        def low_part(eng, u):
            hi, lo = weight_parts(u)
            eng.wait_ge(s("high"), u + 1)
            eng.tensor_tensor(lo, raw_weights(u), hi, ALU.subtract).then_inc(s("low_pool" if u in POOL_UNITS else "low"), 1)

        def par(name, j=0):
            return parT[:, PAR[name] + j:PAR[name] + j + 1]

        def distances(i):
            if i == META_TILE:
                return dist[0:META, T - P:T - P + META]
            return dist[:, T - KEYS[i]:T]

        block = ctx.enter_context(nc.Block())

        @block.sync
        def _(sp):
            win = w_in[0].rearrange("(k p) n -> p k n", p=P)
            wu = w_ffn_up[0].rearrange("(k p) n -> p k n", p=P)

            def load_unit(u):
                name = UNITS[u]
                if u >= RAW:
                    sp.wait_ge(s("high"), u - RAW + 1)
                    low_part_made(sp, u - RAW)
                if name.startswith("down"):
                    f = int(name[5:])
                    dst, src = raw_weights(u), w_ffn_down[0, P * f:P * (f + 1), :]
                else:
                    if name.startswith("p_"):
                        lo = COLS[name[2:]][0]
                    else:
                        n = u - FIRST_UP
                        lo = FF * (n % 2) + P * (n // 2)
                    dst = raw_weights(u).rearrange("p (k n) -> p k n", k=KT_D)
                    src = (win if name.startswith("p_") else wu)[:, :, lo:lo + P]
                sp.dma_start(dst, src).then_inc(s(f"raw{u % RAW}"), 16)

            for i in TOKS:
                src = meta if i == META_TILE else x[0, P * i:P * (i + 1), :]
                sp.dma_start(xin[0:ROWS[i], HROW[i], :], src).then_inc(s(f"x_in{i}"), 16)
            for n, name in enumerate(PROJ):
                if n == 4:
                    for dst, src in ((wuq, w_uq), (wiq, w_iq)):
                        sp.dma_start(dst, src[0].rearrange("(k p) n -> p k n", p=P)).then_inc(s("w_low"), 16)
                    ukv = w_ukv[0].rearrange("p (h t d) -> p h t d", h=HEADS, t=2)
                    for t, dst in enumerate((wuk, wuv)):
                        sp.dma_start(dst.rearrange("p (h d) -> p h d", h=HEADS), ukv[:, :, t, :]).then_inc(s("w_low"), 16)
                load_unit(n)
                if n == 10:
                    sp.wait_ge(s("index_keys"), 1)
                    sp.dma_start(kiT[HD:2 * HD, :], kiT[0:HD, :]).then_inc(s("index_keys2"), 16)
            product(sp, f"p_{PROJ[-1]}")
            sp.dma_start(wlora[0:64, :], w_decay_up[0]).then_inc(s("w_lora"), 16)
            sp.dma_start(wlora[64:128, :], w_aaa_up[0]).then_inc(s("w_lora"), 16)
            product(sp, f"a_{NJ - 1}")
            sp.dma_start(wgate, w_gate_up[0]).then_inc(s("w_gate"), 16)
            first, came, went = 0, 0, 0
            for g, pairs in enumerate(GROUPS):
                for p in pairs:
                    evacuated(sp, f"sc_{p}_0")
                    evacuated(sp, f"sc_{p}_1")
                    for q in range(2 * len(PAIRS[p])):
                        src = MSX[BLK * q:BLK * (q + 1), BUF[p], :, :, BLK * (q % 2):BLK * (q % 2 + 1)]
                        lo = first + FIRST_BLOCK[p] + HEADS * q
                        dst = blocks_in[lo:lo + HEADS].rearrange("i s t -> s i t")
                        sp.dma_start(dst, src.rearrange("s j h t -> s (j h) t")).then_inc(s("blocks_out1"), 16)
                        went += 16
                sp.wait_ge(s("blocks_out1"), went)
                src = blocks_in[first:first + BLOCKS[g]].rearrange("i s t -> i (s t)")
                sp.dma_start(Ni[0:BLOCKS[g], :], src).then_inc(s("blocks_here"), 16)
                sp.wait_ge(s("inverted"), g + 1)
                dst = blocks_out[first:first + BLOCKS[g]].rearrange("i s t -> i (s t)")
                sp.dma_start(dst, Xi[0:BLOCKS[g], :]).then_inc(s("inverses_out"), 16)
                sp.wait_ge(s("inverses_out"), 16 * (g + 1))
                for p in pairs:
                    for q in range(2 * len(PAIRS[p])):
                        dst = DI[BLK * q:BLK * (q + 1), BUF[p], :, :, BLK * (q % 2):BLK * (q % 2 + 1)]
                        lo = first + FIRST_BLOCK[p] + HEADS * q
                        src = blocks_out[lo:lo + HEADS].rearrange("i s t -> s i t")
                        sp.dma_start(dst.rearrange("s j h t -> s (j h) t"), src).then_inc(s("inverses_here"), 16)
                first += BLOCKS[g]
            evacuated(sp, f"qg_{len(PAIRS) - 1}")
            for k in range(0, KT_D, 4):
                src = w_out[0, P * k:P * (k + 4), :].rearrange("(k p) n -> p k n", p=P)
                sp.dma_start(wout[:, k:k + 4, :], src).then_inc(s("w_out"), 16)
            product(sp, "ym_0")
            for u in range(FIRST_UP, len(UNITS)):
                load_unit(u)
            for i in range(TILES):
                sp.wait_ge(s("out_ready"), i + 1)
                sp.dma_start(out[0, P * i:P * (i + 1), :], h_tok[:, i, :]).then_inc(s("stored"), 16)
            sp.wait_ge(s("stored"), 16 * TILES)

        @block.gpsimd
        def _(pool):
            def select(v, pattern, base, mult, op, value):
                return pool.affine_select(out=v, in_=v, compare_op=op, fill=value, base=base,
                                          pattern=pattern, channel_multiplier=mult)

            pool.memset(ident[:, :], 0.0).then_inc(s("const"), 1)
            pool.memset(eye2[:, :], 0.0).then_inc(s("const"), 1)
            pool.memset(mask[:, :], 1.0).then_inc(s("const"), 1)
            pool.memset(blk[:, :], 0.0).then_inc(s("const"), 1)
            pool.memset(ones[:, :], 1.0).then_inc(s("const"), 1)
            pool.memset(mhalf[:, :], -0.5).then_inc(s("const"), 1)
            for k, v in enumerate((LN_EPS, RMS_EPS, GN_EPS)):
                pool.memset(eps[:, k:k + 1], v).then_inc(s("const"), 1)
            n_const = 9
            pool.wait_ge(s("const"), n_const)

            def const(ins):
                nonlocal n_const
                ins.then_inc(s("const"), 1)
                n_const += 1
                pool.wait_ge(s("const"), n_const)

            const(select(ident[:, :], [[-1, P]], 0, 1, ALU.not_equal, 1.0))
            for g in range(2):
                rows = slice(HD * g, HD * (g + 1))
                const(select(eye2[rows, :], [[-1, HD]], 0, 1, ALU.not_equal, 1.0))
                const(pool.memset(blk[rows, rows], 1.0))
                for kind in range(2):
                    const(select(mask[rows, CH * kind:CH * (kind + 1)], [[1, CH]], kind - 1, -1, ALU.is_ge, 0.0))
            pool.iota(dist[:, :], pattern=[[-1, T]], base=META + T - KEYS[0], channel_multiplier=1,
                      allow_small_or_imprecise_dtypes=True).then_inc(s("positions"), 1)

            def rstds(k0, k1):
                for k in range(k0, k1):
                    r = ROWS[(TOKS + TOKS + list(range(TILES)))[k]]
                    pool.wait_ge(s("var"), k + 1)
                    pool.tensor_tensor(mv[0:r, k % 2, 3:4], mv[0:r, k % 2, 2:3], mhalf[0:r, :], ALU.pow).then_inc(s("rstd"), 1)

            rstds(0, 5)
            for v in (AR[:, 1, :, 0:PAD], KT[:, :, 0:PAD], VY[:, :, 0:PAD], praw[:, :, 0:1]):
                pool.memset(v, 0.0).then_inc(s("pads"), 1)
            low_units = list(POOL_UNITS)
            for n, name in enumerate(SHIFTED):
                while low_units and low_units[0] < due(f"p_{name}"):
                    low_part(pool, low_units.pop(0))
                raw = praw[:, n % 3, :]
                evacuated(pool, f"p_{name}")
                pool.tensor_tensor(ptmp, raw[:, 0:T], raw[:, 1:T + 1], ALU.subtract).then_inc(s("shift_line"), 1)
                pool.wait_ge(s("shift_line"), 2 * n + 1)
                pool.tensor_scalar(ptmp, ptmp, par("mu", MU_TILE[name]), None, ALU.mult).then_inc(s("shift_line"), 1)
                pool.wait_ge(s("shift_line"), 2 * n + 2)
                if name in ("wa", "gd"):
                    dst = {"wa": wad, "gd": sgd}[name]
                else:
                    j = int(name[1])
                    dst = {"r": AR[:, 1, j], "k": KT[:, j], "v": VY[:, j]}[name[0]][:, PAD:TP]
                pool.tensor_tensor(dst, ptmp, raw[:, 1:T + 1], ALU.add).then_inc(s("shifted"), 1)
                pool.wait_ge(s("shifted"), n + 1)
            for (i, h), n in ATT.items():
                pool.wait_ge(s("rinv"), n + 1)
                v = Pb[0:ROWS[i], n % 2, 0:NKEYS[i]]
                pool.tensor_scalar(v, v, rinv[0:ROWS[i], h:h + 1], None, ALU.mult).then_inc(s("probs"), 1)
            rstds(5, 14)

        @block.scalar
        def _(act):
            A = act.activation
            for k, v in enumerate((ln_in_g, ln_in_b)):
                act.dma_start(gain_in[:, k, :], v.rearrange("(o n) -> o n", o=1).to_broadcast([P, D])).then_inc(s("gain_in"), 16)
            row = 0
            for v, (name, n) in zip((mu_shift, w0, a0, k_k, k_a, r_k, gn_g, gn_b, q_norm_g, kv_norm_g, idx_ln_g, idx_ln_b), PAR_ROWS):
                if name == "r_k":
                    v = v.rearrange("l h d -> l (h d)")
                if name in ("i_g", "i_b"):
                    for c in range(2):
                        act.dma_start(par_rows[row:row + 1, IDX * c:IDX * (c + 1)], v).then_inc(s("par_in"), 16)
                else:
                    act.dma_start(par_rows[row:row + n, 0:P], v.rearrange("l (r p) -> (l r) p", p=P)).then_inc(s("par_in"), 16)
                row += n
            act.dma_start(par_rows[0:3 * NF, P:2 * P], conv_w[0].rearrange("t (r p) -> (t r) p", p=P)).then_inc(s("par_in"), 16)
            act.dma_start(par_rows[3 * NF:4 * NF, P:2 * P], conv_b.rearrange("l (r p) -> (l r) p", p=P)).then_inc(s("par_in"), 16)

            def evacuate(job, dst, src, func=ACT.Copy, **kw):
                product(act, job)
                empties(A(dst, src, func, **kw), job)

            made = [0]

            def high_parts(n):
                while made[0] < len(UNITS) and (made[0] not in IN_RING or ring(made[0]) < n):
                    u = made[0]
                    act.wait_ge(s(f"raw{u % RAW}"), 16 * (u // RAW + 1))
                    room_for(act, u)
                    A(weight_parts(u)[0], raw_weights(u), ACT.Copy).then_inc(s("high"), 1)
                    made[0] += 1

            for i in TOKS:
                v = slot(f"hT{i}")[:, :].rearrange("p (k t) -> p k t", k=KT_D)[:, :, 0:ROWS[i]]
                product(act, f"hT{i}")
                A(hT_hi[:, :, QCOLS[i]], v, ACT.Copy).then_inc(s("h_high"), 1)
            high_parts(RING)
            evacuate("par", parT[:, :], slot("par")[:, 0:NPAR + 4 * NF])

            order = list(JOBS)
            n_shift = n_relu = 0
            for job in order[order.index("p_q0"):order.index("z_0")]:
                kind, n = job[:2], job[2:]
                high_parts(due(job))
                if job in ("p_q0", "p_q1", "p_kv"):
                    k = ("p_q0", "p_q1", "p_kv").index(job)
                    product(act, job)
                    A(halves(aRaw[:, k, :]), banks(job, HALF), ACT.Copy)
                    empties(A(halves(tmpA[:, k, :]), banks(job, HALF), ACT.Square), job)
                elif job == "p_ki":
                    m = IDX + HEADS
                    evacuate(job, halves(aRaw[0:m, 3, :]), banks(job, HALF)[0:m])
                elif kind == "p_":
                    if n_shift >= 3:
                        act.wait_ge(s("shifted"), n_shift - 2)
                    else:
                        act.wait_ge(s("pads"), 4)
                    evacuate(job, halves(praw[:, n_shift % 3, 1:T + 1]), banks(job, HALF))
                    n_shift += 1
                elif kind == "ss":
                    k, rank = (0, Q_RANK) if job == "ssq" else (2, KV_RANK)
                    evacuate(job, halves(tmpA[:, k, :]), banks(job, HALF), ACT.Sqrt, bias=eps[:, 1:2], scale=1.0 / rank)
                elif job == "kmean":
                    evacuated(act, job)
                    A(tmpA[0:IDX, 1, :], aRaw[0:IDX, 3, :], ACT.Square).then_inc(s("key_squares"), 1)
                elif job == "kvar":
                    evacuated(act, job)
                    A(kiT[0:IDX, :], tmpA[0:IDX, 0, :], ACT.Sqrt).then_inc(s("key_root"), 1)
                elif job == "widx":
                    v = slot(job)[:, 0:TILES * HEADS].rearrange("p (i h) -> p i h", i=TILES)
                    evacuate(job, wix[:, :, :], v, scale=IDX_SCALE)
                elif kind in ("qp", "qi", "kp"):
                    dst = {"qp": qT, "qi": qiT, "kp": kT}[kind]
                    evacuate(job, halves(dst[:, int(n), :]), banks(job, HALF), scale=HD ** -0.5 if kind == "qp" else 1.0)
                elif job == "vp0":
                    product(act, job)
                    A(vtok[0:META, TILES, :], slot(job)[0:META, 0:512], ACT.Copy)
                    empties(A(vtok[:, 0, :], slot(job)[:, 512:1024], ACT.Copy), job)
                elif job == "vp1":
                    evacuate(job, vtok[:, 1:3, :], banks(job, 512))
                elif job == "vp2":
                    evacuate(job, vtok[:, 3, :], slot(job)[:, 0:512])
                else:
                    i = int(job[2])
                    if n_relu >= 2:
                        act.wait_ge(s("index_sum"), n_relu - 1)
                    evacuate(job, relu[:, n_relu % 2, 0:KEYS[i]], slot(job)[:, 0:KEYS[i]], ACT.Relu)
                    n_relu += 1

            act.wait_ge(s("shifted"), 2)
            A(wad[0:64, :], wad[0:64, :], ACT.Tanh).then_inc(s("lora_in"), 1)
            A(sgd, sgd, ACT.Sigmoid).then_inc(s("lora_in"), 1)
            act.wait_ge(s("cleared"), 3)

            def decay(j):
                job = f"z_{j}"
                product(act, job)
                cs = csig[:, j, :].rearrange("p (c t) -> p c t", t=CH + 1)
                A(cs[:, 0, CH + 1 - META:], slot(job)[:, 0:META], ACT.Sigmoid, bias=par("w0", j))
                v = slot(job)[:, 512:1024].rearrange("p (c t) -> p c t", t=CH)
                empties(A(cs[:, 1:NCH, 1:], v, ACT.Sigmoid, bias=par("w0", j)), job)

            def rate(j):
                job = f"a_{j}"
                product(act, job)
                A(aT[:, j, PAD:CH], slot(job)[:, 0:META], ACT.Sigmoid, bias=par("a0", j))
                empties(A(aT[:, j, CH:TP], slot(job)[:, 512:1024], ACT.Sigmoid, bias=par("a0", j)), job)

            def key_squares(j):
                if j == 0:
                    act.wait_ge(s("shifted"), len(SHIFTED))
                    act.wait_ge(s("index_keys"), 1)
                if j >= 2:
                    product(act, f"ss_{j - 2}")
                A(tw[:, j % 2, :], KT[:, j, :], ACT.Square, scale=par("k_k", j)).then_inc(s("kk_squares"), 1)

            def key_roots(j):
                if j == 0:
                    key_squares(0)
                if j < NJ - 1:
                    key_squares(j + 1)
                evacuate(f"ss_{j}", halves(AR[:, 0, j, :]), banks(f"ss_{j}", HP), ACT.Sqrt)

            def powers(j):
                act.wait_ge(s("summed"), j + 1)
                A(Pp[:, j, :], csig[:, j, :], ACT.Exp, scale=-KAPPA).then_inc(s("decay"), 1)
                act.wait_ge(s("decay"), 2 * j + 1)
                A(csig[:, j, :], csig[:, j, :], ACT.Exp, scale=KAPPA).then_inc(s("decay"), 1)

            def tokens(p, half):
                rows, b = slice(0, CH * len(PAIRS[p])), BUF[p]
                job = f"tk_{p}_{half}"
                product(act, job)
                v = slot(job)[rows, :].rearrange("p (j q h k) -> p j q h k", j=2, q=4, h=2)
                for jj in range(2):
                    j = 2 * half + jj
                    A(R[rows, b, j, :, CH:P], v[:, jj, 0], ACT.Copy)
                    A(MSX[rows, b, j, :, 128:192], v[:, jj, 1], ACT.Copy)
                    A(MSX[rows, b, j, :, 320:384], v[:, jj, 2], ACT.Copy)
                    last = A(Vtok[rows, b, j], v[:, jj, 3], ACT.Copy)
                empties(last, job)

            def exponentials(i, h):
                k, r, nk = ATT[i, h], ROWS[i], NKEYS[i]
                act.wait_ge(s("max"), k + 1)
                if k >= 2:
                    product(act, "T_{}_{}".format(*ATT_LIST[k - 2]))
                A(Pb[0:r, k % 2, 0:nk], Lb[0:r, k % 2, 0:nk], ACT.Exp, bias=nmax[0:r, h:h + 1],
                  accum_out=rsum[0:r, h:h + 1]).then_inc(s("exp"), 1)

            def transposed(i, h):
                k, r = ATT[i, h], ROWS[i]
                job = f"T_{i}_{h}"
                product(act, job)
                if k >= 2:
                    product(act, "O_{}_{}".format(*ATT_LIST[k - 2]))
                last = A(PTm[0:META, k % 2, 0:r], slot(job)[0:META, 0:r], ACT.Copy)
                if i != META_TILE:
                    last = A(PT[:, k % 2, 0:P * (i + 1)], slot(job)[:, P:P * (i + 2)], ACT.Copy)
                empties(last, job)

            def attended(i, h):
                evacuate(f"O_{i}_{h}", qT[head_rows(h), h // 2, QCOLS[i]], slot(f"O_{i}_{h}")[head_rows(h), 0:ROWS[i]])

            def x1(p):
                rows = slice(0, CH * len(PAIRS[p]))
                v = slot(f"x_{p}")[rows, 0:512].rearrange("p (j h v) -> p j h v", j=NJ, h=2)
                evacuate(f"x_{p}", R[rows, BUF[p], :, :, 0:CH], v)

            def first_blocks(p):
                job = f"u0_{p}"
                product(act, job)
                if p:
                    act.wait_ge(s("state"), PAIRS[p][0])
                for c in range(len(PAIRS[p])):
                    first = slice(CH * c, CH * c + BLK)
                    last = A(flat(U0[first]), slot(job)[first, :], ACT.Copy)
                empties(last, job)

            def solved(p):
                rows = slice(0, CH * len(PAIRS[p]))
                evacuate(f"u_{p}", flat(R[rows, BUF[p]]), slot(f"u_{p}")[rows, :])

            def without_state(p):
                job = f"hy_{p}"
                product(act, job)
                for c, chunk in enumerate(PAIRS[p]):
                    v = slot(job)[:, 512 * c:512 * (c + 1)].rearrange("p (k j t) -> p k j t", k=2, j=NJ)
                    A(H[:, c], v[:, 0], ACT.Copy)
                    last = A(VY[:, :, CH * chunk:CH * (chunk + 1)], v[:, 1], ACT.Copy)
                empties(last, job)

            mine = {"z": decay, "a": rate, "ss": key_roots, "sum": powers, "tk": tokens, "E": exponentials,
                    "T": transposed, "O": attended, "x": x1, "u0": first_blocks, "u": solved, "hy": without_state}
            for kind, *which in MIXERS:
                if kind in mine:
                    mine[kind](*which)
            for j in range(NJ):
                evacuated(act, f"ym_{j}")
                if j >= 2:
                    product(act, f"yv{j - 2}")
                A(Lb[:, j % 2, :], VY[:, j, PAD:TP], ACT.Square).then_inc(s("y_squares"), 1)
                if j >= 2:
                    evacuated(act, f"g{j - 2}")
                evacuate(f"yv{j}", halves(Pb[:, j % 2, :]), banks(f"yv{j}", HALF), ACT.Sqrt, bias=eps[:, 2:3], scale=1.0 / HD)
            high_parts(len(PROJ) + RING)
            for dst, g, b in ((gain1, ln1_g, ln1_b), (gain2, ln2_g, ln2_b)):
                for k, v in enumerate((g, b)):
                    act.dma_start(dst[:, k, :], v.to_broadcast([P, D])).then_inc(s("gains"), 16)
            for i in TOKS:
                v = slot(f"h1T{i}")[:, :].rearrange("p (k t) -> p k t", k=KT_D)
                product(act, f"h1T{i}")
                A(h1T_hi[:, :, H1COLS[i]], v[:, :, H1FROM[i]:ROWS[i]], ACT.Copy).then_inc(s("h_high"), 1)

            def gelu(f):
                act.wait_ge(s("conv"), f + 1)
                A(cv[:, f % 2, :], cv[:, f % 2, :], ACT.Gelu_apprx_tanh).then_inc(s("gelu"), 1)

            def high_act(f):
                evacuated(act, f"val{f}")
                A(act_hi[:, f, :], cv[:, f % 2, :], ACT.Copy).then_inc(s("act_high"), 1)

            for f in range(NF):
                high_parts(due(f"gate{f}"))
                if f >= 2:
                    high_act(f - 2)
                    act.wait_ge(s("conv"), f - 1)
                evacuate(f"gate{f}", gs[:, f % 2, :], slot(f"gate{f}")[:, GATE_AT:GATE_AT + SEQ + CONV - 1])
                high_parts(due(f"val{f}"))
                if f >= 1:
                    gelu(f - 1)
            high_act(NF - 2)
            gelu(NF - 1)
            high_act(NF - 1)
            high_parts(len(UNITS))

        @block.vector
        def _(dve):
            V = dve
            steps = [0]

            def then(ins):
                ins.then_inc(s("vector_step"), 1)
                steps[0] += 1
                dve.wait_ge(s("vector_step"), steps[0])

            def statistics(k, v, r):
                m = mv[0:r, k % 2, :]
                V.bn_stats(stats[0:r, 0, :], v[:, 0:512])
                then(V.bn_stats(stats[0:r, 1, :], v[:, 512:1024]))
                then(V.bn_aggr(m[:, 0:2], flat(stats[0:r])))
                V.tensor_scalar(m[:, 2:3], m[:, 1:2], LN_EPS, None, ALU.add).then_inc(s("var"), 1)

            def normalise(k, dst, v, r, gain, signal):
                m = mv[0:r, k % 2, :]
                dve.wait_ge(s("rstd"), k + 1)
                then(V.tensor_scalar(dst, v, m[:, 0:1], m[:, 3:4], ALU.subtract, ALU.mult))
                then(V.tensor_tensor(dst, dst, gain[0:r, 0, :], ALU.mult))
                V.tensor_tensor(dst, dst, gain[0:r, 1, :], ALU.add).then_inc(signal, 1)

            def norm_in(n):
                i = TOKS[n]
                if n == 0:
                    dve.wait_ge(s("gain_in"), 32)
                normalise(n, h_tok[0:ROWS[i], HROW[i], :], xin[0:ROWS[i], HROW[i], :], ROWS[i], gain_in, s("normed"))

            def low_features(n, i, job, hi, lo, first=0):
                v = slot(job)[:, :].rearrange("p (k t) -> p k t", k=KT_D)[:, :, first:ROWS[i]]
                dve.wait_ge(s("h_high"), n + 1)
                empties(V.tensor_tensor(lo, v, hi, ALU.subtract), job)

            def low_in(n):
                i = TOKS[n]
                low_features(n, i, f"hT{i}", hT_hi[:, :, QCOLS[i]], hT_lo[:, :, QCOLS[i]])

            for n, i in enumerate(TOKS):
                dve.wait_ge(s(f"x_in{i}"), 16)
                statistics(n, xin[0:ROWS[i], HROW[i], :], ROWS[i])
                if n:
                    norm_in(n - 1)
                if n >= 3:
                    low_in(n - 3)
            norm_in(len(TOKS) - 1)
            for n in range(len(TOKS) - 3, len(TOKS)):
                low_in(n)

            low_units = [u for u in range(len(UNITS)) if u not in POOL_UNITS]

            def low_parts(n):
                while low_units and (low_units[0] not in IN_RING or ring(low_units[0]) < n):
                    low_part(dve, low_units.pop(0))

            low_parts(RING)

            dve.wait_ge(s("positions"), 1)
            then(V.scalar_tensor_tensor(dist[:, :], dist[:, :], -1.0, dist[:, :], ALU.mult, ALU.max))
            then(V.tensor_scalar(dist[0:CH, T - CH:T], dist[0:CH, T - CH:T], FAR, None, ALU.add))

            for k, (job, name, j) in enumerate((("ssq", "q_g", 0), ("ssq", "q_g", 1), ("sskv", "kv_g", 0))):
                root = tmpA[:, 0 if job == "ssq" else 2, :]
                low_parts(due(job))
                evacuated(dve, job)
                if k != 1:
                    then(V.reciprocal(root, root))
                V.scalar_tensor_tensor(aRaw[:, k, :], aRaw[:, k, :], par(name, j), root, ALU.mult, ALU.mult).then_inc(s("low_normed"), 1)
            dve.wait_ge(s("low_normed"), 3)
            key = aRaw[0:IDX, 3, :]
            low_parts(due("kmean"))
            product(dve, "kmean")
            empties(V.scalar_tensor_tensor(halves(key), banks("kmean", HALF)[0:IDX], -1.0 / IDX, halves(key), ALU.mult, ALU.add), "kmean")
            v0, t1, y = tmpA[0:IDX, 0, :], tmpA[0:IDX, 2, :], kiT[0:IDX, :]
            low_parts(due("kvar"))
            product(dve, "kvar")
            empties(V.tensor_scalar(halves(v0), banks("kvar", HALF)[0:IDX], 1.0 / IDX, LN_EPS, ALU.mult, ALU.add), "kvar")
            dve.wait_ge(s("key_root"), 1)
            then(V.reciprocal(y, y))
            then(V.tensor_tensor(t1, v0, y, ALU.mult))
            then(V.tensor_tensor(t1, t1, y, ALU.mult))
            then(V.tensor_scalar(t1, t1, -0.5, 1.5, ALU.mult, ALU.add))
            then(V.tensor_tensor(y, y, t1, ALU.mult))
            then(V.tensor_tensor(y, y, key, ALU.mult))
            V.tensor_scalar(y, y, par("i_g")[0:IDX], par("i_b")[0:IDX], ALU.mult, ALU.add).then_inc(s("index_keys"), 1)

            then(V.memset(m8[:, 1, :], TAKEN))
            evacuated(dve, "widx")
            n_sum = 0
            for i in IX_ORDER:
                n = KEYS[i]
                sc = SC[:, sum(KEYS[:i]):sum(KEYS[:i]) + n]
                for h in range(HEADS):
                    low_parts(due(f"ix{i}_{h}"))
                    evacuated(dve, f"ix{i}_{h}")
                    if n_sum:
                        dve.wait_ge(s("index_sum"), n_sum)
                    v, w = relu[:, n_sum % 2, 0:n], wix[:, i, h:h + 1]
                    ins = V.scalar_tensor_tensor(sc, v, w, sc, ALU.mult, ALU.add) if h else V.tensor_scalar(sc, v, w, None, ALU.mult)
                    ins.then_inc(s("index_sum"), 1)
                    n_sum += 1
            dve.wait_ge(s("index_sum"), n_sum)
            for i in IX_ORDER:
                n = KEYS[i]
                sc = SC[:, sum(KEYS[:i]):sum(KEYS[:i]) + n]
                then(V.memset(sc[0:CH, n - CH:n], INVISIBLE))
                for k in range(TOPK // 8):
                    if k % 5 == 0:
                        low_parts(min(len(PROJ), ring(low_units[0]) + 1))
                    then(V.max(m8[:, 0, :], sc))
                    then(V.match_replace(sc, m8[:, 0, :], sc, TAKEN))
                then(V.max(m8[:, 0, :], sc))
                then(V.tensor_copy(m8[:, 1, 0:TOPK % 8], m8[:, 0, 0:TOPK % 8]))
                then(V.match_replace(sc, m8[:, 1, :], sc, TAKEN))
                then(V.tensor_scalar(sc, sc, TAKEN_BELOW, FAR, ALU.is_gt, ALU.mult))
                then(V.tensor_tensor(sc, sc, distances(i), ALU.add))

            product(dve, f"p_{PROJ[-1]}")
            V.memset(flat(csig), 0.0).then_inc(s("cleared"), 1)
            V.memset(aT[:, :, 0:PAD], 0.0).then_inc(s("cleared"), 1)
            dve.wait_ge(s("shifted"), len(SHIFTED))
            then(V.memset(reset, 1.0))
            V.memset(reset.rearrange("p (c t) -> p c t", t=CH + 1)[:, :, 0:1], 0.0).then_inc(s("cleared"), 1)
            dve.wait_ge(s("cleared"), 3)

            def decay_sums(j):
                evacuated(dve, f"z_{j}")
                V.tensor_tensor_scan(csig[:, j, :], reset, csig[:, j, :], 0.0, ALU.mult, ALU.add).then_inc(s("summed"), 1)

            def features(j):
                grow = csig[:, j, :].rearrange("p (c t) -> p c t", t=CH + 1)[:, :, 1:]
                decay = Pp[:, j, :].rearrange("p (c t) -> p c t", t=CH + 1)
                chunks = lambda v: v.rearrange("p (c t) -> p c t", t=CH)
                a_, r_, k_, b_ = AR[:, 0, j, :], AR[:, 1, j, :], KT[:, j, :], BT[:, j, :]
                evacuated(dve, f"ss_{j}")
                then(V.tensor_scalar(a_, a_, 1e-12, None, ALU.max))
                then(V.reciprocal(a_, a_))
                then(V.scalar_tensor_tensor(a_, k_, par("k_k", j), a_, ALU.mult, ALU.mult))
                evacuated(dve, f"a_{j}")
                then(V.tensor_scalar(b_, aT[:, j, :], -1.0, par("k_a", j), ALU.add, ALU.mult))
                then(V.scalar_tensor_tensor(k_, b_, 1.0, k_, ALU.add, ALU.mult))
                product(dve, f"bo_{j - 1}" if j else f"ss_{NJ - 1}")
                V.scalar_tensor_tensor(tw[:, 0, :], r_, par("r_k", j), k_, ALU.mult, ALU.mult).then_inc(s("bonus_in"), 1)
                then(V.tensor_tensor(b_, a_, aT[:, j, :], ALU.mult))
                dve.wait_ge(s("decay"), 2 * j + 2)
                V.tensor_tensor(chunks(b_), chunks(b_), grow, ALU.mult).then_inc(s("prepped"), 1)
                dve.wait_ge(s("bonus_in"), j + 1)
                V.tensor_tensor(chunks(k_), chunks(k_), grow, ALU.mult).then_inc(s("prepped"), 1)
                V.tensor_tensor(chunks(r_), chunks(r_), decay[:, :, 1:], ALU.mult).then_inc(s("prepped"), 1)
                V.scalar_tensor_tensor(chunks(a_), chunks(a_), -1.0, decay[:, :, 0:CH], ALU.mult, ALU.mult).then_inc(s("prepped"), 1)
                V.tensor_copy(PL[:, j, :], decay[:, :, CH]).then_inc(s("prepped"), 1)
                product(dve, f"bo_{j}")
                empties(V.tensor_tensor(halves(BONUS[:, j, :]), halves(VY[:, j, :]), banks(f"bo_{j}", HP), ALU.mult), f"bo_{j}")
                if j == NJ - 1:
                    dve.wait_ge(s("prepped"), 5 * NJ)
                    V.memset(flat(DI), 0.0).then_inc(s("no_inverses"), 1)
                    dve.wait_ge(s("no_inverses"), 1)

            def triangles(p, half):
                rows, b = slice(0, CH * len(PAIRS[p])), BUF[p]
                m = mask[rows, :].rearrange("p (o n) -> p o n", o=1).to_broadcast([rows.stop, 2, P])
                job = f"sc_{p}_{half}"
                product(dve, job)
                for n in range(4):
                    j, h = 2 * half + n // 2, n % 2
                    dst = MSX[rows, b, j, h, :].rearrange("p (g n) -> p g n", g=2)[:, :, 0:P]
                    lo = 512 * h + 256 * (n // 2)
                    src = slot(job)[rows, lo:lo + 256].rearrange("p (g n) -> p g n", g=2)
                    last = V.tensor_tensor(dst, src, m, ALU.mult)
                empties(last, job)

            def invert(g, piece):
                r = BLOCKS[g]
                if piece == 0:
                    dve.wait_ge(s("blocks_here"), 16 * (g + 1))
                    if g:
                        dve.wait_ge(s("inverses_out"), 16 * g)
                    then(V.tensor_copy(Xi[0:r, :], Ni[0:r, :]))
                    then(V.memset(Xi[0:r, 0:BLK * BLK:BLK + 1], 1.0))
                N3 = Ni[0:r, :].rearrange("i (s t) -> i s t", t=BLK)
                X3 = Xi[0:r, :].rearrange("i (s t) -> i s t", t=BLK)
                for j in PIECES[piece]:
                    w = BLK - 1 - j
                    new = Ti[0:r, 0:j * w].rearrange("i (c t) -> i c t", c=j)
                    then(V.tensor_tensor(new, N3[:, j:j + 1, j + 1:BLK].to_broadcast([r, j, w]),
                                         X3[:, 0:j, j:j + 1].to_broadcast([r, j, w]), ALU.mult))
                    last = V.tensor_tensor(X3[:, 0:j, j + 1:BLK], X3[:, 0:j, j + 1:BLK], new, ALU.add)
                    if j < BLK - 2:
                        then(last)
                    else:
                        last.then_inc(s("inverted"), 1)

            def logits(i, h):
                k, r, nk = ATT[i, h], ROWS[i], NKEYS[i]
                far = distances(i) if i == META_TILE else SC[:, sum(KEYS[:i]):sum(KEYS[:i]) + nk]
                job = f"S_{i}_{h}"
                product(dve, job)
                if k == 0:
                    dve.wait_ge(s("summed"), NJ)
                if k >= 2:
                    dve.wait_ge(s("exp"), k - 1)
                L = Lb[0:r, k % 2, 0:nk]
                empties(V.scalar_tensor_tensor(L, far, -SLOPES[h], slot(job)[0:r, 0:nk], ALU.mult, ALU.add), job)
                evacuated(dve, job)
                V.tensor_reduce(nmax[0:r, h:h + 1], L, AX.X, ALU.max, negate=True).then_inc(s("max"), 1)

            def inverse_sum(i, h):
                k, r = ATT[i, h], ROWS[i]
                dve.wait_ge(s("exp"), k + 1)
                if k >= HEADS:
                    dve.wait_ge(s("probs"), k - HEADS + 1)
                V.reciprocal(rinv[0:r, h:h + 1], rsum[0:r, h:h + 1]).then_inc(s("rinv"), 1)

            def second_blocks(p):
                b, job = BUF[p], f"nu_{p}"
                product(dve, job)
                for c in range(len(PAIRS[p])):
                    second = slice(CH * c + BLK, CH * (c + 1))
                    last = V.tensor_tensor(flat(R[second, b]), flat(R[second, b]), slot(job)[second, :], ALU.add)
                empties(last, job)

            def through_chunk(p):
                job = f"qg_{p}"
                product(dve, job)
                v = slot(job)[:, :].rearrange("p (c j n) -> p j c n", j=NJ, c=2)
                eye = eye2[:, :].rearrange("p (o n) -> p o n", o=1).to_broadcast([P, NJ, CH])
                for c, chunk in enumerate(PAIRS[p]):
                    r_ = AR[:, 1, :, CH * chunk:CH * (chunk + 1)]
                    V.tensor_tensor(QB[:, :, c, :], v[:, :, c, 0:CH], r_, ALU.add)
                    last = V.tensor_tensor(GT[:, :, c, :], v[:, :, c, CH:P], eye, ALU.add)
                empties(last, job)

            def state(c):
                p, n = (c + 1) // 2, (c + 1) % 2 if c else 0
                evacuated(dve, f"hy_{p}")
                new, decay = Z[:, (c + 1) % 2], PL[:, :, c:c + 1].to_broadcast([P, NJ, CH])
                if not c:
                    V.tensor_tensor(new, H[:, n], decay, ALU.mult).then_inc(s("state"), 1)
                    return
                job = f"zy_{c}"
                product(dve, job)
                v = slot(job)[:, :].rearrange("p (b j t) -> p b j t", b=2, j=2 * NJ)[:, :, 0:NJ]
                then(V.tensor_tensor(new, v[:, 0], H[:, n], ALU.add))
                V.tensor_tensor(new, new, decay, ALU.mult).then_inc(s("state"), 1)
                y = VY[:, :, CH * c:CH * (c + 1)]
                empties(V.tensor_tensor(y, y, v[:, 1], ALU.add), job)

            def center(j):
                product(dve, f"ym_{j}")
                y = halves(VY[:, j, PAD:TP])
                empties(V.scalar_tensor_tensor(y, banks(f"ym_{j}", HALF), -1.0 / HD, y, ALU.mult, ALU.add), f"ym_{j}")

            mine = {"sum": decay_sums, "bo": features, "sc": triangles, "inv": invert, "S": logits, "V": inverse_sum,
                    "nu": second_blocks, "qg": through_chunk, "zy": state, "ym": center}
            for kind, *which in MIXERS:
                if kind in mine:
                    mine[kind](*which)
            for j in range(NJ):
                y, root = VY[:, j, PAD:TP], Pb[:, j % 2, :]
                evacuated(dve, f"yv{j}")
                then(V.reciprocal(root, root))
                then(V.tensor_tensor(y, y, root, ALU.mult))
                then(V.tensor_scalar(y, y, par("gn_g", j), par("gn_b", j), ALU.mult, ALU.add))
                then(V.tensor_tensor(y, y, BONUS[:, j, PAD:TP], ALU.add))
                product(dve, f"g{j}")
                empties(V.tensor_tensor(halves(y), halves(y), banks(f"g{j}", HALF), ALU.mult), f"g{j}")

            low_parts(len(PROJ) + RING)

            def residual(job, k, i):
                ht = h_tok[0:ROWS[i], HROW[i], :]
                product(dve, job)
                empties(V.scalar_tensor_tensor(ht, ht, ALPHA, slot(job)[0:ROWS[i], :], ALU.mult, ALU.add), job)
                evacuated(dve, job)
                statistics(k, ht, ROWS[i])

            def low_mixed(n):
                i = TOKS[n]
                cols = H1COLS[i]
                low_features(len(TOKS) + n, i, f"h1T{i}", h1T_hi[:, :, cols], h1T_lo[:, :, cols], H1FROM[i])

            dve.wait_ge(s("gains"), 64)
            for n, i in enumerate(TOKS):
                ht = h_tok[0:ROWS[i], HROW[i], :]
                residual(f"mix{i}", 5 + n, i)
                normalise(5 + n, ht, ht, ROWS[i], gain1, s("mixed"))
                if n:
                    low_mixed(n - 1)
            low_mixed(len(TOKS) - 1)

            def gated(f):
                dve.wait_ge(s("gelu"), f + 1)
                product(dve, f"val{f}")
                empties(V.tensor_tensor(cv[:, f % 2, :], cv[:, f % 2, :], slot(f"val{f}")[:, 0:SEQ], ALU.mult), f"val{f}")

            def low_act(f):
                dve.wait_ge(s("act_high"), f + 1)
                V.tensor_tensor(act_lo[:, f, :], cv[:, f % 2, :], act_hi[:, f, :], ALU.subtract).then_inc(s("act_low"), 1)

            for f in range(NF):
                g, c_ = gs[:, f % 2, :], cv[:, f % 2, :]
                tap = lambda t: parT[:, NPAR + NF * t + f:NPAR + NF * t + f + 1]
                low_parts(due(f"gate{f}"))
                if f >= 2:
                    low_act(f - 2)
                    dve.wait_ge(s("act_low"), f - 1)
                evacuated(dve, f"gate{f}")
                then(V.tensor_scalar(c_, g[:, 2:SEQ + 2], tap(2), tap(CONV), ALU.mult, ALU.add))
                then(V.scalar_tensor_tensor(c_, g[:, 1:SEQ + 1], tap(1), c_, ALU.mult, ALU.add))
                V.scalar_tensor_tensor(c_, g[:, 0:SEQ], tap(0), c_, ALU.mult, ALU.add).then_inc(s("conv"), 1)
                low_parts(due(f"val{f}"))
                if f >= 1:
                    gated(f - 1)
            low_act(NF - 2)
            gated(NF - 1)
            low_act(NF - 1)
            low_parts(len(UNITS))
            for i in range(TILES):
                residual(f"down{i}", 10 + i, i)
                normalise(10 + i, h_tok[:, i, :], h_tok[:, i, :], P, gain2, s("out_ready"))

        @block.tensor
        def _(pe):
            def begin(job):
                if JOBS[job] >= NSLOT:
                    evacuated(pe, ORDER[JOBS[job] - NSLOT])

            def end_job(ins, job):
                ins.then_inc(written[JOBS[job] % NSLOT], 1)

            def mm(dst, pairs):
                for n, (a, b) in enumerate(pairs):
                    last = pe.matmul(dst, a, b, start=n == 0, stop=n == len(pairs) - 1)
                return last

            def in_parts(terms):
                return [pair for (ah, al), (bh, bl) in terms for pair in ((ah, bh), (ah, bl), (al, bh))]

            def unit(name):
                u = UNIT[name]
                pe.wait_ge(s("high"), u + 1)
                low_part_made(pe, u)
                hi, lo = weight_parts(u)
                return lambda k: (hi[:, P * k:P * (k + 1)], lo[:, P * k:P * (k + 1)])

            def by_halves(job, m, pairs, n=HALF):
                for b in range(2):
                    last = mm(slot(job)[0:m, 512 * b:512 * b + n], [(a, v[:, n * b:n * (b + 1)]) for a, v in pairs])
                end_job(last, job)

            def wide(dst, a, v, n):
                for lo in range(0, n, 512):
                    hi = min(n, lo + 512)
                    last = mm(dst[:, lo:hi], [(a, v[:, lo:hi])])
                return last

            pe.wait_ge(s("const"), N_CONST)

            def to_features(job, i, ready, count):
                begin(job)
                pe.wait_ge(ready, count)
                r = ROWS[i]
                for k in range(KT_D):
                    last = pe.transpose(slot(job)[:, P * k:P * k + r], h_tok[0:r, HROW[i], P * k:P * (k + 1)], ident[0:r, 0:r])
                end_job(last, job)

            for n, i in enumerate(TOKS):
                to_features(f"hT{i}", i, s("normed"), n + 1)

            begin("par")
            pe.wait_ge(s("par_in"), 16 * N_PAR_DMA)
            pe.transpose(slot("par")[:, 0:NPAR], par_rows[0:NPAR, 0:P], ident[0:NPAR, 0:NPAR])
            end_job(pe.transpose(slot("par")[:, NPAR:NPAR + 4 * NF], par_rows[0:4 * NF, P:2 * P], ident[0:4 * NF, 0:4 * NF]), "par")

            for i in TOKS:
                evacuated(pe, f"hT{i}")
            for job in ORDER[JOBS["p_q0"]:JOBS["z_0"]]:
                kind, n = job[:2], job[2:]
                begin(job)
                if kind == "p_":
                    w = unit(job)
                    by_halves(job, P, in_parts([(w(d), (hT_hi[:, d, :], hT_lo[:, d, :])) for d in range(KT_D)]))
                elif job == "ssq":
                    evacuated(pe, "p_q1")
                    by_halves(job, P, [(ones[:, :], tmpA[:, d, :]) for d in range(2)])
                elif job == "sskv":
                    evacuated(pe, "p_kv")
                    by_halves(job, P, [(ones[:, :], tmpA[:, 2, :])])
                elif job == "kmean":
                    evacuated(pe, "p_ki")
                    by_halves(job, IDX, [(ones[0:IDX, 0:IDX], aRaw[0:IDX, 3, :])])
                elif job == "kvar":
                    pe.wait_ge(s("key_squares"), 1)
                    by_halves(job, IDX, [(ones[0:IDX, 0:IDX], tmpA[0:IDX, 1, :])])
                elif job == "widx":
                    for i in range(TILES):
                        rows = slice(IDX, IDX + HEADS)
                        last = pe.transpose(slot(job)[:, HEADS * i:HEADS * (i + 1)], aRaw[rows, 3, QCOLS[i]], ident[rows, rows])
                    end_job(last, job)
                elif kind in ("qp", "qi"):
                    w = {"qp": wuq, "qi": wiq}[kind]
                    pe.wait_ge(s("w_low"), 64)
                    pe.wait_ge(s("low_normed"), 2)
                    by_halves(job, P, [(w[:, d, P * int(n):P * (int(n) + 1)], aRaw[:, d, :]) for d in range(2)])
                elif kind == "kp":
                    pe.wait_ge(s("low_normed"), 3)
                    by_halves(job, P, [(wuk[:, P * int(n):P * (int(n) + 1)], aRaw[:, 2, :])])
                elif kind == "vp":
                    for b, i in enumerate(((META_TILE, 0), (1, 2), (3,))[int(n)]):
                        last = mm(slot(job)[0:ROWS[i], 512 * b:512 * (b + 1)], [(aRaw[:, 2, QCOLS[i]], wuv)])
                    end_job(last, job)
                else:
                    i, h = int(job[2]), int(job[4])
                    r = head_rows(h)
                    pe.wait_ge(s("index_keys"), 1)
                    if h % 2:
                        pe.wait_ge(s("index_keys2"), 16)
                    evacuated(pe, f"qi{h // 2}")
                    end_job(wide(slot(job)[:, :], qiT[r, h // 2, QCOLS[i]], kiT[r, :], KEYS[i]), job)

            def lora(job, rows, j):
                pe.wait_ge(s("w_lora"), 32)
                pe.wait_ge(s("lora_in"), 1)
                w = wlora[rows, P * j:P * (j + 1)]
                mm(slot(job)[:, 0:META], [(w, wad[rows, 0:META])])
                end_job(mm(slot(job)[:, 512:1024], [(w, wad[rows, META:T])]), job)

            def decay(job, j):
                lora(job, slice(0, 64), j)

            def rate(job, j):
                lora(job, slice(64, 128), j)

            def key_norm(job, j):
                pe.wait_ge(s("kk_squares"), j + 1)
                by_halves(job, P, [(blk[:, :], tw[:, j % 2, :])], HP)

            def bonus(job, j):
                pe.wait_ge(s("bonus_in"), j + 1)
                by_halves(job, P, [(blk[:, :], tw[:, 0, :])], HP)

            def tokens(job, p, half):
                pair = PAIRS[p]
                cols = slice(CH * pair[0], CH * (pair[0] + len(pair)))
                pe.wait_ge(s("prepped"), 5 * NJ)
                evacuated(pe, f"bo_{NJ - 1}")
                for n in range(8):
                    j = 2 * half + n // 4
                    src = (AR[:, 0, j], BT[:, j], KT[:, j], VY[:, j])[n % 4]
                    last = pe.transpose(slot(job)[0:CH * len(pair), P * n:P * (n + 1)], src[:, cols], ident[:, :])
                end_job(last, job)

            def triangles(job, p, half):
                pair = PAIRS[p]
                for n in range(8):
                    jj, src, h = n // 4, (BT, KT)[n // 2 % 2], n % 2
                    j, lo = 2 * half + jj, 512 * h + P * (n // 2)
                    for c in range(len(pair)):
                        cc = slice(CH * pair[c], CH * (pair[c] + 1))
                        last = mm(slot(job)[chunk_rows(c), lo:lo + P],
                                  [(src[head_rows(h), j, cc], AR[head_rows(h), :, j, cc])])
                end_job(last, job)

            def instances(p):
                return [(c, j, h) for c in range(len(PAIRS[p])) for j in range(NJ) for h in range(2)]

            def first(c):
                return slice(CH * c, CH * c + BLK)

            def second(c):
                return slice(CH * c + BLK, CH * (c + 1))

            def x1(job, p):
                b = BUF[p]
                for half in range(2):
                    evacuated(pe, f"tk_{p}_{half}")
                    evacuated(pe, f"sc_{p}_{half}")
                for c, j, h in instances(p):
                    r, lo = chunk_rows(c), CH * (2 * j + h)
                    last = mm(slot(job)[r, lo:lo + CH], [(MSX[r, b, j, h, 192:256], Vtok[r, b, j, h])])
                end_job(last, job)

            def first_blocks(job, p):
                b = BUF[p]
                g = 0 if p in GROUPS[0] else 1
                pe.wait_ge(s("inverses_here"), 16 * sum(2 * len(PAIRS[q]) for pairs in GROUPS[:g + 1] for q in pairs))
                evacuated(pe, f"x_{p}")
                for c, j, h in instances(p):
                    lo = P * (2 * j + h)
                    last = mm(slot(job)[first(c), lo:lo + P], [(DI[first(c), b, j, h, 0:BLK], R[first(c), b, j, h])])
                end_job(last, job)

            def second_blocks(job, p):
                b = BUF[p]
                evacuated(pe, f"u0_{p}")
                for c, j, h in instances(p):
                    lo = P * (2 * j + h)
                    last = mm(slot(job)[second(c), lo:lo + P], [(MSX[first(c), b, j, h, BLK:2 * BLK], U0[first(c), j, h])])
                end_job(last, job)

            def solution(job, p):
                b = BUF[p]
                evacuated(pe, f"nu_{p}")
                for c, j, h in instances(p):
                    r, lo = chunk_rows(c), P * (2 * j + h)
                    last = mm(slot(job)[r, lo:lo + P], [(DI[r, b, j, h], R[r, b, j, h])])
                end_job(last, job)

            def through_chunk(job, p):
                b = BUF[p]
                evacuated(pe, f"u_{p}")
                for c, j, h in instances(p):
                    r, lo = chunk_rows(c), 512 * c + P * j
                    last = mm(slot(job)[head_rows(h), lo:lo + P], [(R[r, b, j, h, CH:P], MSX[r, b, j, h, 64:192])])
                end_job(last, job)

            def without_state(job, p):
                b = BUF[p]
                for c, j, h in instances(p):
                    r, hr, lo = chunk_rows(c), head_rows(h), 512 * c + CH * j
                    u, v, m = R[r, b, j, h, 0:CH], Vtok[r, b, j, h], MSX[r, b, j, h]
                    mm(slot(job)[hr, lo:lo + CH], [(m[:, 128:192], u), (m[:, 320:384], v)])
                    lo += NJ * CH
                    last = mm(slot(job)[hr, lo:lo + CH], [(u, m[:, 64:128]), (v, m[:, 256:320])])
                end_job(last, job)

            def state(job, c):
                p, n = (c + 1) // 2, (c + 1) % 2
                evacuated(pe, f"qg_{p}")
                pe.wait_ge(s("state"), c)
                for k in range(2):
                    for j in range(NJ):
                        for h in range(2):
                            hr, lo = head_rows(h), 512 * k + CH * j
                            z = Z[hr, c % 2, j]
                            last = mm(slot(job)[hr, lo:lo + CH], [(z, QB[hr, j, n]) if k else (GT[hr, j, n], z)])
                end_job(last, job)

            def logits(job, i, h):
                hr = head_rows(h)
                end_job(wide(slot(job)[0:ROWS[i], :], qT[hr, h // 2, QCOLS[i]], kT[hr, h // 2, :], NKEYS[i]), job)

            def transposes(job, i, h):
                k, r = ATT[i, h], ROWS[i]
                pe.wait_ge(s("probs"), k + 1)
                last = pe.transpose(slot(job)[0:META, 0:r], Pb[0:r, k % 2, 0:META], ident[0:r, 0:r])
                for lo in range(META, NKEYS[i], P):
                    last = pe.transpose(slot(job)[:, lo + P - META:lo + 2 * P - META], Pb[0:r, k % 2, lo:lo + P], ident[0:r, 0:r])
                end_job(last, job)

            def values(job, i, h):
                k, r, cols = ATT[i, h], ROWS[i], slice(HD * h, HD * (h + 1))
                evacuated(pe, f"T_{i}_{h}")
                terms = [(vtok[0:META, TILES, cols], PTm[0:META, k % 2, 0:r])]
                if i != META_TILE:
                    terms += [(vtok[:, t, cols], PT[:, k % 2, P * t:P * (t + 1)]) for t in range(i + 1)]
                end_job(mm(slot(job)[head_rows(h), 0:r], terms), job)

            def means(job, j):
                for p in range(len(PAIRS)):
                    evacuated(pe, f"hy_{p}")
                for c in range(1, NCH):
                    evacuated(pe, f"zy_{c}")
                by_halves(job, P, [(blk[:, :], VY[:, j, PAD:TP])])

            mine = {"z": decay, "a": rate, "ss": key_norm, "bo": bonus, "tk": tokens, "sc": triangles, "x": x1,
                    "u0": first_blocks, "nu": second_blocks, "u": solution, "qg": through_chunk, "hy": without_state,
                    "zy": state, "S": logits, "T": transposes, "O": values, "ym": means}
            for step in MIXERS:
                kind, *which = step
                if kind in mine and step != ("zy", 0):
                    begin(name_of(step))
                    mine[kind](name_of(step), *which)
            for j in range(NJ):
                begin(f"yv{j}")
                pe.wait_ge(s("y_squares"), j + 1)
                by_halves(f"yv{j}", P, [(blk[:, :], Lb[:, j % 2, :])])
                begin(f"g{j}")
                pe.wait_ge(s("w_gate"), 16)
                by_halves(f"g{j}", P, [(wgate[:, P * j:P * (j + 1)], sgd)])

            pe.wait_ge(s("w_out"), 32)
            for j in range(NJ):
                evacuated(pe, f"g{j}")
            for i in TOKS:
                job = f"mix{i}"
                begin(job)
                for b in range(2):
                    cols = slice(512 * b, 512 * (b + 1))
                    last = mm(slot(job)[0:ROWS[i], cols],
                              [(qT[:, j, QCOLS[i]], wout[:, j, cols]) for j in range(NJ)] +
                              [(VY[:, j, YCOLS[i]], wout[:, NJ + j, cols]) for j in range(NJ)])
                end_job(last, job)
            for n, i in enumerate(TOKS):
                to_features(f"h1T{i}", i, s("mixed"), n + 1)

            for i in TOKS:
                evacuated(pe, f"h1T{i}")
            for f in range(NF):
                job = f"gate{f}"
                w = unit(job)
                begin(job)
                for at, lo, hi in ((GATE_AT, 0, 512 - GATE_AT), (512, 512 - GATE_AT, SEQ + CONV - 1)):
                    last = mm(slot(job)[:, at:at + hi - lo],
                              in_parts([(w(d), (h1T_hi[:, d, lo:hi], h1T_lo[:, d, lo:hi])) for d in range(KT_D)]))
                end_job(last, job)
                job = f"val{f}"
                w = unit(job)
                begin(job)
                cols = slice(CONV - 1, SEQ + CONV - 1)
                end_job(mm(slot(job)[:, 0:SEQ], in_parts([(w(d), (h1T_hi[:, d, cols], h1T_lo[:, d, cols])) for d in range(KT_D)])), job)

            def down(f, i, start=False, stop=False):
                hi, lo = weight_parts(UNIT[f"down_{f}"])
                tile = (act_hi[:, f, P * i:P * (i + 1)], act_lo[:, f, P * i:P * (i + 1)])
                for b in range(2):
                    cols = slice(512 * b, 512 * (b + 1))
                    passes = in_parts([(tile, (hi[:, cols], lo[:, cols]))])
                    for n, (a, w) in enumerate(passes):
                        last = pe.matmul(slot(f"down{i}")[:, cols], a, w, start=start and n == 0, stop=stop and n == 2)
                return last

            for f in STREAMED:
                unit(f"down_{f}")
                pe.wait_ge(s("act_low"), f + 1)
                for i in range(TILES):
                    if f == 0:
                        begin(f"down{i}")
                    last = down(f, i, start=f == 0)
                last.then_inc(s("rows_used"), 1)
            pe.wait_ge(s("act_low"), NF)
            kept = KEPT + [f for f in range(NF) if f not in KEPT + STREAMED]
            for i in range(TILES):
                for f in kept:
                    if i == 0:
                        unit(f"down_{f}")
                    last = down(f, i, stop=f == kept[-1])
                end_job(last, f"down{i}")


_INS = ['x', 'meta', 'ln_in_g', 'ln_in_b', 'w_in', 'q_norm_g', 'w_uq', 'kv_norm_g', 'w_ukv', 'w_iq', 'idx_ln_g', 'idx_ln_b',
        'mu_shift', 'w0', 'w_decay_up', 'a0', 'w_aaa_up', 'w_gate_up', 'k_k', 'k_a', 'r_k', 'gn_g', 'gn_b', 'w_out',
        'ln1_g', 'ln1_b', 'w_ffn_up', 'conv_w', 'conv_b', 'w_ffn_down', 'ln2_g', 'ln2_b']
_OUTS = [((1, SEQ, D), 'float32')]


def kernel(**inputs):
    import numpy as _np
    import concourse.bacc as _bacc
    from concourse import mybir as _mybir
    from concourse.bass_utils import run_bass_kernel_spmd as _run

    nc = _bacc.Bacc("TRN2", target_bir_lowering=False, num_devices=1)
    arrays, args = {}, []
    for name in _INS:
        a = _np.ascontiguousarray(inputs[name])
        arrays[f"in_{name}_dram"] = a
        args.append(nc.dram_tensor(f"in_{name}_dram", a.shape, _mybir.dt.from_np(a.dtype), kind="ExternalInput").ap())
    for i, (shape, dtype) in enumerate(_OUTS):
        dt = _mybir.dt.from_np(_np.dtype(dtype))
        args.append(nc.dram_tensor(f"out_{i}_dram", shape, dt, kind="ExternalOutput").ap())
    hymba(nc, *args)
    r = _run(nc, [arrays], core_ids=[0])
    return r.results[0]["out_0_dram"]
```

```python
from contextlib import ExitStack

import concourse.bass as bass
from concourse import mybir

F32 = mybir.dt.float32
F32R = mybir.dt.float32r
ALU = mybir.AluOpType
ACT = mybir.ActivationFunctionType
AX = mybir.AxisListType

P = 128
D = 1024
KT_D = D // P
SEQ, META = 512, 16
T = SEQ + META
HALF = T // 2
TILES = SEQ // P
CH = 64
PAD = CH - META
NCH = SEQ // CH + 1
TP = NCH * CH
HP = TP // 2
HEADS, HD = 8, 64
NJ = HEADS // 2
Q_RANK, KV_RANK, IDX = 256, 128, 64
A_COLS = Q_RANK + KV_RANK + IDX + HEADS
TOPK = T // 4
FF = 2816
NF = FF // P
CONV = 3
LN_EPS, RMS_EPS, GN_EPS = 1e-5, 1e-6, 64e-5
ALPHA = 2.0 ** 0.25
KAPPA = 0.6065306597126334
IDX_SCALE = HEADS ** -0.5 * IDX ** -0.5
INVISIBLE, TAKEN, TAKEN_BELOW = -3.0e38, -3.4e38, -3.2e38
FAR = 1.0e34
SLOPES = [2.0 ** (-8.0 * (h + 1) / HEADS) for h in range(HEADS)]
KEYS = [META + P * (i + 1) for i in range(TILES)]

META_TILE = "m"
TOKS = [META_TILE] + list(range(TILES))
IX_ORDER = (3, 2, 1, 0)

COLS = {"q0": (0, 128), "q1": (128, 128), "kv": (256, 128), "ki": (384, 128),
        "wa": (A_COLS + 3 * 512, 128), "gd": (A_COLS + 3 * 512 + 128, 128)}
COLS |= {f"{x}{j}": (A_COLS + 512 * n + P * j, 128) for j in range(NJ) for n, x in enumerate("rkv")}
PROJ = list(COLS)
SHIFTED = PROJ[4:]
PAR_ROWS = (("mu", 14), ("w0", 4), ("a0", 4), ("k_k", 4), ("k_a", 4), ("r_k", 4), ("gn_g", 4), ("gn_b", 4),
            ("q_g", 2), ("kv_g", 1), ("i_g", 1), ("i_b", 1))
PAR = {name: sum(r for _, r in PAR_ROWS[:n]) for n, (name, _) in enumerate(PAR_ROWS)}
NPAR = sum(r for _, r in PAR_ROWS)
MU_TILE = {f"{x}{j}": 4 * n + j for n, x in enumerate("rkv") for j in range(NJ)} | {"wa": 12, "gd": 13}

PAIRS = [(0,)] + [(2 * i + 1, 2 * i + 2) for i in range(TILES)]
BUF = [0, 1, 2, 0, 1]
GROUPS = [[0, 1, 2], [3, 4]]
BLK = 32
FIRST_BLOCK = {p: sum(16 * len(PAIRS[q]) for q in g if q < p) for g in GROUPS for p in g}
BLOCKS = [sum(16 * len(PAIRS[p]) for p in g) for g in GROUPS]


POOL_COLUMN = 10
PIECES = [range(j, min(j + 8, BLK - 1)) for j in range(1, BLK - 1, 8)]


def scores(p):
    return [(kind, p, half) for half in range(2) for kind in ("tk", "sc")]


def inversion(g):
    return [("inv", g, n) for n in range(len(PIECES))]


def solve(p):
    return [(kind, p) for kind in ("u0", "nu", "u")]


def turn(p):
    return [("qg", p), ("hy", p)] + [("zy", c) for c in PAIRS[p]]


def attention(i):
    steps = []
    for n in range(HEADS + 3):
        for kind, h in (("S", n), ("V", n - 1), ("T", n - 2), ("O", n - 3), ("E", n)):
            if 0 <= h < HEADS:
                steps.append((kind, i, h))
    return steps


ATT_CUTS, INV_CUTS = (20, 25, 40), (3, 8)
WEIGHT = {"pow": 0, "kn": 2, "bo": 6, "tk": 2, "sc": 3, "x": 2, "inv": 3.2, "u0": 4, "nu": 2, "u": 4, "qg": 5,
          "hy": 6, "zy": 4}


def weight(step):
    if step[0] in WEIGHT:
        return WEIGHT[step[0]]
    return 0.8 if step[1] == META_TILE else 0.8 + step[1] / 4


def merged(a, b):
    out, sums, lists = [], [0.0, 0.0], [list(a), list(b)]
    totals = [sum(map(weight, steps)) for steps in lists]
    while lists[0] or lists[1]:
        n = 0 if lists[0] and (not lists[1] or sums[0] * totals[1] <= sums[1] * totals[0]) else 1
        step = lists[n].pop(0)
        sums[n] += weight(step)
        out.append(step)
    return out


def mixers():
    steps = [("ss",)]
    steps += merged(attention(3), [(kind, j) for j in range(NJ) for kind in ("pow", "kn", "bo")])
    steps += scores(0) + scores(1) + scores(2) + [("x", p) for p in GROUPS[0]]
    att = attention(2) + attention(1) + attention(0) + attention(META_TILE)
    rwkv = solve(0) + merged(turn(0), solve(1)) + merged(turn(1), scores(3)) + scores(4)
    behind = [("x", p) for p in GROUPS[1]] + solve(2) + turn(2)
    lag, back = INV_CUTS
    rwkv += behind[:lag] + merged(behind[lag:back], inversion(1)) + behind[back:]
    rwkv += solve(3) + merged(turn(3), solve(4)) + turn(4)
    came, inverted, back = ATT_CUTS
    steps += att[:came] + merged(att[came:inverted], inversion(0)) + att[inverted:back]
    return steps + merged(att[back:], rwkv) + [("ym", j) for j in range(NJ)]


RAW, RING = 2, 3
KEPT = list(range(NF - 4, NF))
STREAMED = list(range(NF - 4 - RING))


def weight_units():
    units = [f"p_{name}" for name in PROJ] + [f"out_{k}" for k in range(KT_D)]
    units += [f"{x}{f}" for f in range(NF) for x in ("gate", "val")]
    rest = [f for f in range(NF) if f not in KEPT]
    for n, f in enumerate(rest):
        units.append(f"down_{f}")
        if n in (3, 5, 7, 9):
            units.append(f"down_{KEPT[(n - 3) // 2]}")
    return units


UNITS = weight_units()
IN_RING = [n for n, name in enumerate(UNITS) if name[:4] != "out_" and name not in [f"down_{f}" for f in KEPT]]
UNIT = {name: n for n, name in enumerate(UNITS)}
FIRST_OUT = len(PROJ)
FIRST_UP = FIRST_OUT + KT_D
MIX_AHEAD = 2
POOL_UNITS = [0, 1, 2, 11, 13, 15, 17] + list(range(FIRST_OUT, FIRST_OUT + NJ))


def name_of(step):
    return "_".join(map(str, step))


NO_SLOT = ("V", "E", "inv", "pow")
MIXERS = mixers()


GROUP_NORM = ["yv", "g0", "g1", "yr0", "yr1", "g2", "yr2", "g3", "yr3"]


def psum_jobs():
    jobs = [f"hT{i}" for i in TOKS] + ["par"]
    jobs += ["p_q0", "p_q1", "p_kv", "p_ki", "ssq", "sskv", "p_wa", "kmean", "p_gd", "kvar", "widx"]
    jobs += [f"qi{j}" for j in range(NJ)] + ["p_r0"]
    each = lambda kind: [f"{kind}{j}" for j in range(NJ)]
    fill = {3: ["p_k0", "p_v0", "p_r1", "p_k1"] + each("qp"),
            2: ["p_v1", "p_r2"] + each("kp"),
            1: ["p_k2", "vp0", "vp1", "vp2", "p_v2"],
            0: ["p_r3"] + each("z_") + ["p_k3"] + each("a_") + ["p_v3"]}
    for i in IX_ORDER:
        index = [f"ix{i}_{h}" for h in range(HEADS)]
        jobs += index[0:HEADS // 2] + fill[i][0:1] + index[HEADS // 2:] + fill[i][1:]
    jobs += [name_of(step) for step in MIXERS if step[0] not in NO_SLOT and step != ("zy", 0)]
    jobs += GROUP_NORM
    for n, i in enumerate(TOKS):
        jobs.append(f"mix{i}")
        if n >= MIX_AHEAD:
            jobs.append(f"h1T{TOKS[n - MIX_AHEAD]}")
    jobs += [f"h1T{i}" for i in TOKS[-MIX_AHEAD:-1]] + ["gate0", "val0", f"h1T{TOKS[-1]}"]
    for f in range(1, NF):
        jobs += [f"gate{f}", f"val{f}"]
    return jobs + [f"down{i}" for i in range(TILES)]


ORDER = psum_jobs()
JOBS = {name: n for n, name in enumerate(ORDER)}


def due(job):
    n = RING + sum(name in JOBS and JOBS[name] < JOBS[job] for name in UNITS)
    return min(n, FIRST_OUT) if JOBS[job] < JOBS["ss"] else (IN_RING + RING * [len(UNITS)])[n]


NSLOT = 4
ATT = {step[1:]: n for n, step in enumerate(st for st in MIXERS if st[0] == "S")}
ATT_LIST = list(ATT)
N_CONST = 26
N_PAR_DMA = 16
ROWS = {i: P for i in range(TILES)} | {META_TILE: META}
NKEYS = {i: KEYS[i] for i in range(TILES)} | {META_TILE: META}
QCOLS = {i: slice(META + P * i, META + P * (i + 1)) for i in range(TILES)} | {META_TILE: slice(0, META)}
H1COLS = {i: slice(CONV - 1 + P * i, CONV - 1 + P * (i + 1)) for i in range(TILES)} | {META_TILE: slice(0, CONV - 1)}
H1FROM = {i: 0 for i in range(TILES)} | {META_TILE: META - CONV + 1}
GATE_AT = 254
HROW = {i: i for i in range(TILES)} | {META_TILE: TILES}


def head_rows(h):
    return slice(HD * (h % 2), HD * (h % 2) + HD)


def chunk_rows(c):
    return slice(CH * c, CH * c + CH)


def flat(v):
    n = len(v.shape)
    names = " ".join("abcde"[:n - 1])
    return v.rearrange(f"p {names} -> p ({names})")


def halves(v):
    return v.rearrange("p (b c) -> p b c", b=2)


def hymba(nc, x, meta, ln_in_g, ln_in_b, w_in, q_norm_g, w_uq, kv_norm_g, w_ukv, w_iq,
          idx_ln_g, idx_ln_b, mu_shift, w0, w_decay_up, a0, w_aaa_up, w_gate_up,
          k_k, k_a, r_k, gn_g, gn_b, w_out, ln1_g, ln1_b, w_ffn_up, conv_w, conv_b,
          w_ffn_down, ln2_g, ln2_b, out):
    with ExitStack() as ctx:
        def sb(name, *shape):
            return ctx.enter_context(nc.sbuf_tensor(name, [P, *shape], F32))

        ident, blk, mask, eye2 = sb("ident", P), sb("blk", P), sb("mask", P), sb("eye2", CH)
        dist = sb("dist", T)
        parT = sb("parT", NPAR + 4 * NF)
        heads, headsT = sb("heads", BLK), sb("headsT", P)
        h_tok = sb("h_tok", TILES + 1, D)
        stats, mv, mhalf, eps = sb("stats", 2, 6), sb("mv", 2, 4), sb("mhalf", 1), sb("eps", 3)
        wix = sb("wix", TILES, HEADS)
        m8 = sb("m8", 2, 8)
        nmax, rsum, rinv = sb("nmax", HEADS), sb("rsum", HEADS), sb("rinv", HEADS)
        Z = sb("Z", 2, NJ, HD)
        PL = sb("PL", NJ, NCH)
        SIZE = 46120
        arena_at = -(-nc.sbuf_base // 32) * 32
        sb("arena", SIZE)
        slots = [ctx.enter_context(nc.psum_tensor(f"slot{i}", [P, 1024], F32)) for i in range(NSLOT)]
        blocks_in = nc.dram_tensor("blocks_in", (sum(BLOCKS), BLK, BLK), F32, kind="Internal").ap()
        blocks_out = nc.dram_tensor("blocks_out", (sum(BLOCKS), BLK, BLK), F32, kind="Internal").ap()

        end = {}

        def lay(at, parts=False, **shapes):
            views = []
            for name, shape in shapes.items():
                n = 1
                for d in shape:
                    n *= d
                at = -(-at // 8) * 8
                assert at + n <= SIZE, (name, at + n)
                v = nc.alloc_sbuf_tensor_at(name, [P, n], F32R if parts else F32, offset=arena_at + 4 * at)[:, :]
                at += n
                end[name] = at
                if len(shape) > 1:
                    dims = "abcd"[:len(shape)]
                    v = v.rearrange(f"p ({' '.join(dims)}) -> p {' '.join(dims)}", **dict(zip(dims, shape)))
                views.append(v)
            return views

        AR, KT, BT, BONUS, VY, qT, kT, vtok, SC, praw, ptmp, wad, sgd = lay(
            0, AR=(2, NJ, TP), KT=(NJ, TP), BT=(NJ, TP), BONUS=(NJ, TP), VY=(NJ, TP), qT=(NJ, T), kT=(NJ, T),
            vtok=(TILES + 1, 512), SC=(sum(KEYS),), praw=(3, 1 + T), ptmp=(T,), wad=(T,), sgd=(T,))
        base = end["sgd"]
        w_hi, w_lo, hT_hi = lay(base, parts=True, w_hi=(RING, KT_D * P), w_lo=(RING, KT_D * P), hT_hi=(KT_D, T))
        hT_lo, = lay(end["KT"], parts=True, hT_lo=(KT_D, T))
        assert end["hT_lo"] <= end["BONUS"]
        ones, = lay(end["hT_lo"], ones=(P,))
        assert end["ones"] <= end["BONUS"]
        w_raw, = lay(0, w_raw=(RAW, KT_D * P))
        assert end["w_raw"] <= NJ * TP
        aRaw, tmpA, kiT, wuq, wiq, wuk, wuv, qiT, relu = lay(
            end["hT_hi"], aRaw=(4, T), tmpA=(3, T), kiT=(T,), wuq=(2, 512), wiq=(2, 512),
            wuk=(512,), wuv=(512,), qiT=(NJ, T), relu=(2, T))
        xin, = lay(end["VY"], xin=(TILES + 1, D))
        assert end["xin"] <= end["vtok"]
        gain_in, = lay(end["wuv"], gain_in=(2, D))
        par_rows = flat(tmpA)[:, 0:2 * P]
        csig, tw, reset = lay(end["hT_hi"], csig=(NJ, NCH * 65), tw=(TP,), reset=(NCH * 65,))
        aT, wlora = lay(end["kiT"], aT=(NJ, TP), wlora=(512,))
        Pp, = lay(base, Pp=(NJ, NCH * 65))
        assert end["reset"] <= end["tmpA"] and end["wlora"] <= end["wuv"]
        wgate = wad[:, 0:512]
        key_sq = flat(Pp)[:, 0:NJ * TP].rearrange("p (j t) -> p j t", j=NJ)
        key_norm = AR[:, 0, NJ - 1, :]
        wgate = wad[:, 0:512]
        R, Vtok, Ni, Xi, Ti, QB, GT, U0, MSX, DI, PT, PTm = lay(
            base, R=(3, NJ, 2, P), Vtok=(3, NJ, 2, HD), Ni=(BLK * BLK,), Xi=(BLK * BLK,), Ti=(256,), QB=(NJ, 2, HD),
            GT=(NJ, 2, HD), U0=(NJ, 2, P), MSX=(3, NJ, 2, 384), DI=(3, NJ, 2, HD), PT=(2, 4 * P), PTm=(2, P))
        H = wad[:, 0:2 * NJ * HD].rearrange("p (c j v) -> p c j v", c=2, j=NJ)
        Lb, Pb = lay(end["SC"], Lb=(2, T), Pb=(2, T))
        assert end["Pb"] <= end["ptmp"]
        y_sq, = lay(end["SC"], y_sq=(NJ, T))
        diag = dist[:, 0:2 * P].rearrange("p (a b) -> p a b", a=2)
        Tp = dist[:, 2 * P:T - P]
        o_hi, o_lo0 = lay(0, parts=True, o_hi=(KT_D, D), o_lo0=(1, D))
        y_lo, = lay(end["BT"], parts=True, y_lo=(NJ, TP))
        y_hi, att_hi, att_lo, o_lo4 = lay(
            end["VY"], parts=True, y_hi=(NJ, T), att_hi=(NJ, T), att_lo=(NJ, T), o_lo4=(NJ, D))
        assert end["o_lo0"] <= end["BT"] and end["y_lo"] <= end["BONUS"] and end["att_lo"] <= end["vtok"]
        act_hi, act_lo = lay(0, parts=True, act_hi=(NF, SEQ), act_lo=(NF, SEQ))
        h1T_hi, h1T_lo, u_hi, u_lo = lay(
            end["o_lo4"], parts=True, h1T_hi=(KT_D, SEQ + 2), h1T_lo=(KT_D, SEQ + 2), u_hi=(RING, KT_D * P), u_lo=(RING, KT_D * P))
        u_raw, gains = lay(end["u_lo"], u_raw=(RAW, KT_D * P), gains=(2, D))
        o_lo1, = lay(end["gains"], parts=True, o_lo1=(NJ - 1, D))
        gs, cv = lay(end["gains"], gs=(2, SEQ + 2), cv=(2, SEQ))
        assert end["act_lo"] <= end["o_lo4"] and end["MSX"] >= end["u_raw"] and end["u_lo"] >= end["U0"]
        y_root, = lay(end["u_lo"] - T - 8, y_root=(T,))
        k_hi, k_lo = lay(end["o_lo4"], parts=True, k_hi=(len(KEPT), D), k_lo=(len(KEPT), D))
        assert end["k_lo"] <= end["h1T_lo"]

        written = [ctx.enter_context(nc.semaphore(f"slot{i}_written")) for i in range(NSLOT)]
        emptied = [ctx.enter_context(nc.semaphore(f"slot{i}_emptied")) for i in range(NSLOT)]
        named = {}

        def s(name):
            if name not in named:
                named[name] = ctx.enter_context(nc.semaphore(name))
            return named[name]

        def slot(job):
            return slots[JOBS[job] % NSLOT]

        def banks(job, n):
            return halves(slot(job)[:, :])[:, :, 0:n]

        def product(eng, job):
            eng.wait_ge(written[JOBS[job] % NSLOT], JOBS[job] // NSLOT + 1)

        def empties(ins, job):
            ins.then_inc(emptied[JOBS[job] % NSLOT], 1)

        def evacuated(eng, job):
            eng.wait_ge(emptied[JOBS[job] % NSLOT], JOBS[job] // NSLOT + 1)

        def ring(u):
            return IN_RING.index(u)

        def raw_weights(u):
            return (w_raw if u < FIRST_OUT else u_raw)[:, u % RAW]

        def weight_parts(u):
            if FIRST_OUT <= u < FIRST_UP:
                k = u - FIRST_OUT
                return o_hi[:, k], o_lo0[:, 0] if k == 0 else o_lo1[:, k - 1] if k < NJ else o_lo4[:, k - NJ]
            if u not in IN_RING:
                k = KEPT.index(int(UNITS[u][5:]))
                return k_hi[:, k], k_lo[:, k]
            hi, lo = (w_hi, w_lo) if u < FIRST_UP else (u_hi, u_lo)
            return hi[:, ring(u) % RING], lo[:, ring(u) % RING]

        def unit_used(eng, u):
            if UNITS[u] in JOBS:
                product(eng, UNITS[u])
            else:
                eng.wait_ge(s("rows_used"), int(UNITS[u][5:]) + 1)

        def room_for(eng, u):
            if FIRST_OUT <= u < FIRST_UP:
                return
            if u not in IN_RING:
                product(eng, f"val{NF - 1}")
            elif ring(u) >= RING:
                unit_used(eng, IN_RING[ring(u) - RING])

        def low_part_made(eng, u):
            on_pool = sum(n <= u for n in POOL_UNITS)
            if u in POOL_UNITS:
                eng.wait_ge(s("low_pool"), on_pool)
            else:
                eng.wait_ge(s("low"), u + 1 - on_pool)

        def low_part(eng, u):
            hi, lo = weight_parts(u)
            eng.wait_ge(s("high"), u + 1)
            eng.tensor_tensor(lo, raw_weights(u), hi, ALU.subtract).then_inc(s("low_pool" if u in POOL_UNITS else "low"), 1)

        def par(name, j=0):
            return parT[:, PAR[name] + j:PAR[name] + j + 1]

        def distances(i):
            if i == META_TILE:
                return dist[0:META, T - P:T - P + META]
            return dist[:, T - KEYS[i]:T]

        block = ctx.enter_context(nc.Block())

        @block.sync
        def _(sp):
            win = w_in[0].rearrange("(k p) n -> p k n", p=P)
            wu = w_ffn_up[0].rearrange("(k p) n -> p k n", p=P)

            def load_unit(u):
                name = UNITS[u]
                if u >= RAW:
                    sp.wait_ge(s("high"), u - RAW + 1)
                    low_part_made(sp, u - RAW)
                if name.startswith(("down", "out")):
                    n = int(name.split("_")[1])
                    dst, src = raw_weights(u), (w_out if name[0] == "o" else w_ffn_down)[0, P * n:P * (n + 1), :]
                else:
                    if name.startswith("p_"):
                        lo = COLS[name[2:]][0]
                    else:
                        n = u - FIRST_UP
                        lo = FF * (n % 2) + P * (n // 2)
                    dst = raw_weights(u).rearrange("p (k n) -> p k n", k=KT_D)
                    src = (win if name.startswith("p_") else wu)[:, :, lo:lo + P]
                sp.dma_start(dst, src).then_inc(s(f"raw{u % RAW}"), 16)

            for i in TOKS:
                src = meta if i == META_TILE else x[0, P * i:P * (i + 1), :]
                sp.dma_start(xin[0:ROWS[i], HROW[i], :], src).then_inc(s(f"x_in{i}"), 16)
            for n, name in enumerate(PROJ):
                if n == 4:
                    sp.dma_start(wiq, w_iq[0].rearrange("(k p) n -> p k n", p=P)).then_inc(s("w_index"), 16)
                if n == 8:
                    sp.dma_start(wuq, w_uq[0].rearrange("(k p) n -> p k n", p=P)).then_inc(s("w_low"), 16)
                    ukv = w_ukv[0].rearrange("p (h t d) -> p h t d", h=HEADS, t=2)
                    for t, dst in enumerate((wuk, wuv)):
                        sp.dma_start(dst.rearrange("p (h d) -> p h d", h=HEADS), ukv[:, :, t, :]).then_inc(s("w_low"), 16)
                if n == len(PROJ) - 1:
                    product(sp, "vp2")
                    sp.dma_start(wlora[0:64, :], w_decay_up[0]).then_inc(s("w_lora"), 16)
                    sp.dma_start(wlora[64:128, :], w_aaa_up[0]).then_inc(s("w_lora"), 16)
                load_unit(n)
            first, came, went = 0, 0, 0
            for g, pairs in enumerate(GROUPS):
                for p in pairs:
                    evacuated(sp, f"sc_{p}_0")
                    evacuated(sp, f"sc_{p}_1")
                    for q in range(2 * len(PAIRS[p])):
                        src = MSX[BLK * q:BLK * (q + 1), BUF[p], :, :, BLK * (q % 2):BLK * (q % 2 + 1)]
                        lo = first + FIRST_BLOCK[p] + HEADS * q
                        dst = blocks_in[lo:lo + HEADS].rearrange("i s t -> s i t")
                        sp.dma_start(dst, src.rearrange("s j h t -> s (j h) t")).then_inc(s("blocks_out1"), 16)
                        went += 16
                sp.wait_ge(s("blocks_out1"), went)
                src = blocks_in[first:first + BLOCKS[g]].rearrange("i s t -> i (s t)")
                sp.dma_start(Ni[0:BLOCKS[g], :], src).then_inc(s("blocks_here"), 16)
                sp.wait_ge(s("inverted"), g + 1)
                sp.wait_ge(s("inverted_pool"), g + 1)
                dst = blocks_out[first:first + BLOCKS[g]].rearrange("i s t -> i (s t)")
                sp.dma_start(dst, Xi[0:BLOCKS[g], :]).then_inc(s("inverses_out"), 16)
                sp.wait_ge(s("inverses_out"), 16 * (g + 1))
                for p in pairs:
                    for q in range(2 * len(PAIRS[p])):
                        dst = DI[BLK * q:BLK * (q + 1), BUF[p], :, :, BLK * (q % 2):BLK * (q % 2 + 1)]
                        lo = first + FIRST_BLOCK[p] + HEADS * q
                        src = blocks_out[lo:lo + HEADS].rearrange("i s t -> s i t")
                        sp.dma_start(dst.rearrange("s j h t -> s (j h) t"), src).then_inc(s("inverses_here"), 16)
                first += BLOCKS[g]
            product(sp, f"hy_{len(PAIRS) - 1}")
            for u in range(FIRST_OUT, FIRST_OUT + RAW):
                load_unit(u)
            evacuated(sp, f"zy_{NCH - 1}")
            sp.dma_start(wgate, w_gate_up[0]).then_inc(s("w_gate"), 16)
            for u in range(FIRST_OUT + RAW, len(UNITS)):
                load_unit(u)
            for i in range(TILES):
                sp.wait_ge(s("out_ready"), i + 1)
                sp.dma_start(out[0, P * i:P * (i + 1), :], h_tok[:, i, :]).then_inc(s("stored"), 16)
            sp.wait_ge(s("stored"), 16 * TILES)

        @block.gpsimd
        def _(pool):
            def select(v, pattern, base, mult, op, value):
                return pool.affine_select(out=v, in_=v, compare_op=op, fill=value, base=base,
                                          pattern=pattern, channel_multiplier=mult)

            pool.memset(ident[:, :], 0.0).then_inc(s("const"), 1)
            pool.memset(eye2[:, :], 0.0).then_inc(s("const"), 1)
            pool.memset(mask[:, :], 1.0).then_inc(s("const"), 1)
            pool.memset(blk[:, :], 0.0).then_inc(s("const"), 1)
            pool.memset(ones, 1.0).then_inc(s("const"), 1)
            pool.memset(heads[:, :], 0.0).then_inc(s("const"), 1)
            pool.memset(headsT[:, :], 0.0).then_inc(s("const"), 1)
            pool.memset(mhalf[:, :], -0.5).then_inc(s("const"), 1)
            for k, v in enumerate((LN_EPS, RMS_EPS, GN_EPS)):
                pool.memset(eps[:, k:k + 1], v).then_inc(s("const"), 1)
            n_const = 11
            pool.wait_ge(s("const"), n_const)

            def const(ins):
                nonlocal n_const
                ins.then_inc(s("const"), 1)
                n_const += 1
                pool.wait_ge(s("const"), n_const)

            const(select(ident[:, :], [[-1, P]], 0, 1, ALU.not_equal, 1.0))
            for g in range(2):
                rows = slice(HD * g, HD * (g + 1))
                const(select(eye2[rows, :], [[-1, HD]], 0, 1, ALU.not_equal, 1.0))
                const(pool.memset(blk[rows, rows], 1.0))
                const(pool.memset(heads[rows, g:g + 1], 1.0))
                for kind in range(2):
                    const(select(mask[rows, CH * kind:CH * (kind + 1)], [[1, CH]], kind - 1, -1, ALU.is_ge, 0.0))
            for j in range(NJ):
                rows = slice(BLK * j, BLK * (j + 1))
                const(select(headsT[rows, :].rearrange("p (g f) -> p g f", g=2), [[1, 2], [0, HD]], 0, -1, ALU.not_equal, 1.0))
            pool.iota(dist[:, :], pattern=[[-1, T]], base=META + T - KEYS[0], channel_multiplier=1,
                      allow_small_or_imprecise_dtypes=True).then_inc(s("positions"), 1)

            def rstds(k0, k1):
                for k in range(k0, k1):
                    r = ROWS[(TOKS + TOKS + list(range(TILES)))[k]]
                    pool.wait_ge(s("var"), k + 1)
                    pool.tensor_tensor(mv[0:r, k % 2, 3:4], mv[0:r, k % 2, 2:3], mhalf[0:r, :], ALU.pow).then_inc(s("rstd"), 1)

            rstds(0, 1)
            for n, i in enumerate(TOKS):
                if n + 1 < len(TOKS):
                    rstds(n + 1, n + 2)
                pool.wait_ge(s("scaled"), n + 1)
                v = h_tok[0:ROWS[i], HROW[i], :]
                pool.tensor_tensor(v, v, gain_in[0:ROWS[i], 1, :], ALU.add).then_inc(s("normed"), 1)
            for u in POOL_UNITS[:RING]:
                low_part(pool, u)
            for v in (AR[:, 1, :, 0:PAD], KT[:, :, 0:PAD], VY[:, :, 0:PAD], praw[:, :, 0:1]):
                pool.memset(v, 0.0).then_inc(s("pads"), 1)
            low_units = [u for u in POOL_UNITS[RING:] if u < FIRST_OUT]
            for n, name in enumerate(SHIFTED):
                if n == 2:
                    pool.wait_ge(s("index_keys"), 1)
                    pool.dma_start(kiT[HD:2 * HD, :], kiT[0:HD, :]).then_inc(s("index_keys2"), 16)
                while low_units and low_units[0] < due(f"p_{name}"):
                    low_part(pool, low_units.pop(0))
                raw = praw[:, n % 3, :]
                evacuated(pool, f"p_{name}")
                pool.tensor_tensor(ptmp, raw[:, 0:T], raw[:, 1:T + 1], ALU.subtract).then_inc(s("shift_line"), 1)
                pool.wait_ge(s("shift_line"), 2 * n + 1)
                pool.tensor_scalar(ptmp, ptmp, par("mu", MU_TILE[name]), None, ALU.mult).then_inc(s("shift_line"), 1)
                pool.wait_ge(s("shift_line"), 2 * n + 2)
                if name in ("wa", "gd"):
                    dst = {"wa": wad, "gd": sgd}[name]
                else:
                    j = int(name[1])
                    dst = {"r": AR[:, 1, j], "k": KT[:, j], "v": VY[:, j]}[name[0]][:, PAD:TP]
                pool.tensor_tensor(dst, ptmp, raw[:, 1:T + 1], ALU.add).then_inc(s("shifted"), 1)
                pool.wait_ge(s("shifted"), n + 1)
            def decayed(j):
                pool.wait_ge(s("decay"), 3 * j + 3)
                pool.wait_ge(s("bonus_in"), j + 1)
                pool.wait_ge(s("kk_used"), j + 1)
                decay = Pp[:, j, :].rearrange("p (c t) -> p c t", t=CH + 1)
                for k, d in ((1, decay[:, :, 1:]), (0, decay[:, :, 0:CH])):
                    v = AR[:, k, j, :].rearrange("p (c t) -> p c t", t=CH)
                    pool.tensor_tensor(v, v, d, ALU.mult).then_inc(s("decayed"), 1)

            pool_steps = [0]

            def invert(g):
                r = BLOCKS[g]
                N3 = Ni[0:r, :].rearrange("i (s t) -> i s t", t=BLK)
                X3 = Xi[0:r, :].rearrange("i (s t) -> i s t", t=BLK)
                pool.wait_ge(s("inverses_begun"), g + 1)
                for j in range(POOL_COLUMN + 1, BLK - 1):
                    c, w = j - POOL_COLUMN, BLK - 1 - j
                    new = Tp[0:r, 0:c * w].rearrange("i (c t) -> i c t", c=c)
                    rows = X3[:, POOL_COLUMN:j, j + 1:BLK]
                    pool.tensor_tensor(new, N3[:, j:j + 1, j + 1:BLK].to_broadcast([r, c, w]),
                                       X3[:, POOL_COLUMN:j, j:j + 1].to_broadcast([r, c, w]), ALU.mult).then_inc(s("pool_step"), 1)
                    pool_steps[0] += 1
                    pool.wait_ge(s("pool_step"), pool_steps[0])
                    last = pool.tensor_tensor(rows, rows, new, ALU.add)
                    if j < BLK - 2:
                        last.then_inc(s("pool_step"), 1)
                        pool_steps[0] += 1
                        pool.wait_ge(s("pool_step"), pool_steps[0])
                    else:
                        last.then_inc(s("inverted_pool"), 1)

            for kind, *which in MIXERS:
                if kind == "bo":
                    decayed(*which)
                elif kind == "inv" and which[1] == 0:
                    invert(which[0])
            product(pool, "ym_0")
            for j in range(NJ):
                pool.wait_ge(s("att_high"), j + 1)
                pool.tensor_tensor(att_lo[:, j], qT[:, j], att_hi[:, j], ALU.subtract).then_inc(s("att_low"), 1)
                low_part(pool, FIRST_OUT + j)
            rstds(5, 14)

        @block.scalar
        def _(act):
            A = act.activation
            for k, v in enumerate((ln_in_g, ln_in_b)):
                act.dma_start(gain_in[:, k, :], v.rearrange("(o n) -> o n", o=1).to_broadcast([P, D])).then_inc(s("gain_in"), 16)
            row = 0
            for v, (name, n) in zip((mu_shift, w0, a0, k_k, k_a, r_k, gn_g, gn_b, q_norm_g, kv_norm_g, idx_ln_g, idx_ln_b), PAR_ROWS):
                if name == "r_k":
                    v = v.rearrange("l h d -> l (h d)")
                if name in ("i_g", "i_b"):
                    for c in range(2):
                        act.dma_start(par_rows[row:row + 1, IDX * c:IDX * (c + 1)], v).then_inc(s("par_in"), 16)
                else:
                    act.dma_start(par_rows[row:row + n, 0:P], v.rearrange("l (r p) -> (l r) p", p=P)).then_inc(s("par_in"), 16)
                row += n
            act.dma_start(par_rows[0:3 * NF, P:2 * P], conv_w[0].rearrange("t (r p) -> (t r) p", p=P)).then_inc(s("par_in"), 16)
            act.dma_start(par_rows[3 * NF:4 * NF, P:2 * P], conv_b.rearrange("l (r p) -> (l r) p", p=P)).then_inc(s("par_in"), 16)

            def evacuate(job, dst, src, func=ACT.Copy, **kw):
                product(act, job)
                empties(A(dst, src, func, **kw), job)

            made = [0]

            def high_parts(n):
                while made[0] < n:
                    u = made[0]
                    act.wait_ge(s(f"raw{u % RAW}"), 16 * (u // RAW + 1))
                    room_for(act, u)
                    A(weight_parts(u)[0], raw_weights(u), ACT.Copy).then_inc(s("high"), 1)
                    made[0] += 1

            for n, i in enumerate(TOKS):
                v = slot(f"hT{i}")[:, :].rearrange("p (k t) -> p k t", k=KT_D)[:, :, 0:ROWS[i]]
                product(act, f"hT{i}")
                A(hT_hi[:, :, QCOLS[i]], v, ACT.Copy).then_inc(s("h_high"), 1)
                if n >= 2:
                    high_parts(n - 1)
            evacuate("par", parT[:, :], slot("par")[:, 0:NPAR + 4 * NF])

            def decay(j):
                job = f"z_{j}"
                product(act, job)
                act.wait_ge(s("cleared"), 2)
                cs = csig[:, j, :].rearrange("p (c t) -> p c t", t=CH + 1)
                A(cs[:, 0, CH + 1 - META:], slot(job)[:, 0:META], ACT.Sigmoid, bias=par("w0", j))
                v = slot(job)[:, 512:1024].rearrange("p (c t) -> p c t", t=CH)
                empties(A(cs[:, 1:NCH, 1:], v, ACT.Sigmoid, bias=par("w0", j)), job)

            def rate(j):
                job = f"a_{j}"
                product(act, job)
                A(aT[:, j, PAD:CH], slot(job)[:, 0:META], ACT.Sigmoid, bias=par("a0", j))
                empties(A(aT[:, j, CH:TP], slot(job)[:, 512:1024], ACT.Sigmoid, bias=par("a0", j)), job)

            order = list(JOBS)
            n_shift = n_relu = 0
            for job in order[order.index("p_q0"):order.index("ss")]:
                kind, n = job[:2], job[2:]
                high_parts(due(job))
                if job in ("p_q0", "p_q1", "p_kv"):
                    k = ("p_q0", "p_q1", "p_kv").index(job)
                    product(act, job)
                    A(halves(aRaw[:, k, :]), banks(job, HALF), ACT.Copy)
                    empties(A(halves(tmpA[:, k, :]), banks(job, HALF), ACT.Square), job)
                elif job == "p_ki":
                    m = IDX + HEADS
                    evacuate(job, halves(aRaw[0:m, 3, :]), banks(job, HALF)[0:m])
                elif kind == "p_":
                    if n_shift >= 3:
                        act.wait_ge(s("shifted"), n_shift - 2)
                    else:
                        act.wait_ge(s("pads"), 4)
                    evacuate(job, halves(praw[:, n_shift % 3, 1:T + 1]), banks(job, HALF))
                    n_shift += 1
                elif kind in ("z_", "a_"):
                    (decay if kind == "z_" else rate)(int(n))
                elif kind == "ss":
                    k, rank = (0, Q_RANK) if job == "ssq" else (2, KV_RANK)
                    evacuate(job, halves(tmpA[:, k, :]), banks(job, HALF), ACT.Sqrt, bias=eps[:, 1:2], scale=1.0 / rank)
                elif job == "kmean":
                    evacuated(act, job)
                    A(tmpA[0:IDX, 1, :], aRaw[0:IDX, 3, :], ACT.Square).then_inc(s("key_squares"), 1)
                elif job == "kvar":
                    evacuated(act, job)
                    A(kiT[0:IDX, :], tmpA[0:IDX, 0, :], ACT.Sqrt).then_inc(s("key_root"), 1)
                elif job == "widx":
                    v = slot(job)[:, 0:TILES * HEADS].rearrange("p (i h) -> p i h", i=TILES)
                    evacuate(job, wix[:, :, :], v, scale=IDX_SCALE)
                elif kind in ("qp", "qi", "kp"):
                    dst = {"qp": qT, "qi": qiT, "kp": kT}[kind]
                    evacuate(job, halves(dst[:, int(n), :]), banks(job, HALF), scale=HD ** -0.5 if kind == "qp" else 1.0)
                elif job == "vp0":
                    product(act, job)
                    A(vtok[0:META, TILES, :], slot(job)[0:META, 0:512], ACT.Copy)
                    empties(A(vtok[:, 0, :], slot(job)[:, 512:1024], ACT.Copy), job)
                elif job == "vp1":
                    evacuate(job, vtok[:, 1:3, :], banks(job, 512))
                elif job == "vp2":
                    evacuate(job, vtok[:, 3, :], slot(job)[:, 0:512])
                else:
                    i = int(job[2])
                    if job == "ix3_0":
                        act.wait_ge(s("shifted"), 2)
                        A(wad[0:64, :], wad[0:64, :], ACT.Tanh).then_inc(s("lora_in"), 1)
                        A(sgd, sgd, ACT.Sigmoid).then_inc(s("lora_in"), 1)
                    if n_relu >= 2:
                        act.wait_ge(s("index_sum"), n_relu - 1)
                    evacuate(job, relu[:, n_relu % 2, 0:KEYS[i]], slot(job)[:, 0:KEYS[i]], ACT.Relu)
                    n_relu += 1


            def key_norms():
                act.wait_ge(s("shifted"), SHIFTED.index(f"k{NJ - 1}") + 1)
                product(act, f"p_{PROJ[-1]}")
                for j in range(NJ):
                    A(key_sq[:, j], KT[:, j, :], ACT.Square, scale=par("k_k", j)).then_inc(s("kk_squares"), 1)
                evacuate("ss", halves(key_norm), banks("ss", HP), ACT.Sqrt)

            def powers(j):
                act.wait_ge(s("summed"), j + 1)
                A(Pp[:, j, :], csig[:, j, :], ACT.Exp, scale=-KAPPA).then_inc(s("decay"), 1)
                act.wait_ge(s("decay"), 3 * j + 1)
                A(csig[:, j, :], csig[:, j, :], ACT.Exp, scale=KAPPA).then_inc(s("decay"), 1)
                v = Pp[:, j, :].rearrange("p (c t) -> p c t", t=CH + 1)[:, :, CH]
                A(PL[:, j, :], v, ACT.Copy).then_inc(s("decay"), 1)

            def tokens(p, half):
                rows, b = slice(0, CH * len(PAIRS[p])), BUF[p]
                job = f"tk_{p}_{half}"
                product(act, job)
                v = slot(job)[rows, :].rearrange("p (j q h k) -> p j q h k", j=2, q=4, h=2)
                for jj in range(2):
                    j = 2 * half + jj
                    A(R[rows, b, j, :, CH:P], v[:, jj, 0], ACT.Copy)
                    A(MSX[rows, b, j, :, 128:192], v[:, jj, 1], ACT.Copy)
                    A(MSX[rows, b, j, :, 320:384], v[:, jj, 2], ACT.Copy)
                    last = A(Vtok[rows, b, j], v[:, jj, 3], ACT.Copy)
                empties(last, job)

            def exponentials(i, h):
                k, r, nk = ATT[i, h], ROWS[i], NKEYS[i]
                act.wait_ge(s("max"), k + 1)
                if k >= 2:
                    product(act, "T_{}_{}".format(*ATT_LIST[k - 2]))
                A(Pb[0:r, k % 2, 0:nk], Lb[0:r, k % 2, 0:nk], ACT.Exp, bias=nmax[0:r, h:h + 1],
                  accum_out=rsum[0:r, h:h + 1]).then_inc(s("exp"), 1)

            def transposed(i, h):
                k, r = ATT[i, h], ROWS[i]
                job = f"T_{i}_{h}"
                product(act, job)
                if k >= 2:
                    product(act, "O_{}_{}".format(*ATT_LIST[k - 2]))
                last = A(PTm[0:META, k % 2, 0:r], slot(job)[0:META, 0:r], ACT.Copy)
                if i != META_TILE:
                    last = A(PT[:, k % 2, 0:P * (i + 1)], slot(job)[:, P:P * (i + 2)], ACT.Copy)
                empties(last, job)

            def attended(i, h):
                evacuate(f"O_{i}_{h}", qT[head_rows(h), h // 2, QCOLS[i]], slot(f"O_{i}_{h}")[head_rows(h), 0:ROWS[i]])

            def x1(p):
                rows = slice(0, CH * len(PAIRS[p]))
                v = slot(f"x_{p}")[rows, 0:512].rearrange("p (j h v) -> p j h v", j=NJ, h=2)
                evacuate(f"x_{p}", R[rows, BUF[p], :, :, 0:CH], v)

            def first_blocks(p):
                job = f"u0_{p}"
                product(act, job)
                for c in range(len(PAIRS[p])):
                    first = slice(CH * c, CH * c + BLK)
                    last = A(flat(U0[first]), slot(job)[first, :], ACT.Copy)
                empties(last, job)

            def solved(p):
                rows = slice(0, CH * len(PAIRS[p]))
                evacuate(f"u_{p}", flat(R[rows, BUF[p]]), slot(f"u_{p}")[rows, :])

            def without_state(p):
                job = f"hy_{p}"
                product(act, job)
                if p:
                    act.wait_ge(s("state"), PAIRS[p][0])
                for c, chunk in enumerate(PAIRS[p]):
                    v = slot(job)[:, 512 * c:512 * (c + 1)].rearrange("p (k j t) -> p k j t", k=2, j=NJ)
                    A(H[:, c], v[:, 0], ACT.Copy)
                    last = A(VY[:, :, CH * chunk:CH * (chunk + 1)], v[:, 1], ACT.Copy)
                empties(last, job)

            mine = {"ss": key_norms, "pow": powers, "tk": tokens, "E": exponentials,
                    "T": transposed, "O": attended, "x": x1, "u0": first_blocks, "u": solved, "hy": without_state}
            for kind, *which in MIXERS:
                if kind in mine:
                    mine[kind](*which)
            evacuated(act, f"O_{META_TILE}_{HEADS - 1}")
            for j in range(NJ):
                A(att_hi[:, j], qT[:, j], ACT.Copy).then_inc(s("att_high"), 1)
            for j in range(NJ):
                evacuated(act, f"ym_{j}")
                A(y_sq[:, j], VY[:, j, PAD:TP], ACT.Square).then_inc(s("y_squares"), 1)
            evacuate("yv", halves(y_root), banks("yv", HALF), ACT.Sqrt, bias=eps[:, 2:3], scale=1.0 / HD)
            for j in range(NJ):
                high_parts(FIRST_OUT + j + 2)
                act.wait_ge(s("att_low"), j + 1)
                evacuated(act, f"g{j}")
                A(y_hi[:, j], VY[:, j, PAD:TP], ACT.Copy).then_inc(s("y_high"), 1)
            def load_gains(g, b):
                for k, v in enumerate((g, b)):
                    act.dma_start(gains[:, k, :], v.to_broadcast([P, D])).then_inc(s("gains"), 16)

            load_gains(ln1_g, ln1_b)
            high_parts(FIRST_UP + RING)
            for i in TOKS:
                v = slot(f"h1T{i}")[:, :].rearrange("p (k t) -> p k t", k=KT_D)
                product(act, f"h1T{i}")
                A(h1T_hi[:, :, H1COLS[i]], v[:, :, H1FROM[i]:ROWS[i]], ACT.Copy).then_inc(s("h_high"), 1)

            act.wait_ge(s("mixed"), len(TOKS))
            load_gains(ln2_g, ln2_b)

            def gelu(f):
                act.wait_ge(s("conv"), f + 1)
                A(cv[:, f % 2, :], cv[:, f % 2, :], ACT.Gelu_apprx_tanh).then_inc(s("gelu"), 1)

            def high_act(f):
                evacuated(act, f"val{f}")
                A(act_hi[:, f, :], cv[:, f % 2, :], ACT.Copy).then_inc(s("act_high"), 1)

            for f in range(NF):
                high_parts(due(f"gate{f}"))
                if f >= 2:
                    high_act(f - 2)
                    act.wait_ge(s("conv"), f - 1)
                evacuate(f"gate{f}", gs[:, f % 2, :], slot(f"gate{f}")[:, GATE_AT:GATE_AT + SEQ + CONV - 1])
                high_parts(due(f"val{f}"))
                if f >= 1:
                    gelu(f - 1)
            high_act(NF - 2)
            gelu(NF - 1)
            high_act(NF - 1)
            high_parts(len(UNITS))

        @block.vector
        def _(dve):
            V = dve
            steps = [0]

            def then(ins):
                ins.then_inc(s("vector_step"), 1)
                steps[0] += 1
                dve.wait_ge(s("vector_step"), steps[0])

            def statistics(k, v, r):
                m = mv[0:r, k % 2, :]
                V.bn_stats(stats[0:r, 0, :], v[:, 0:512])
                then(V.bn_stats(stats[0:r, 1, :], v[:, 512:1024]))
                then(V.bn_aggr(m[:, 0:2], flat(stats[0:r])))
                V.tensor_scalar(m[:, 2:3], m[:, 1:2], LN_EPS, None, ALU.add).then_inc(s("var"), 1)

            def normalise(k, dst, v, r, gain, signal):
                m = mv[0:r, k % 2, :]
                dve.wait_ge(s("rstd"), k + 1)
                then(V.tensor_scalar(dst, v, m[:, 0:1], m[:, 3:4], ALU.subtract, ALU.mult))
                last = V.tensor_tensor(dst, dst, gain[0:r, 0, :], ALU.mult)
                if k < len(TOKS):
                    last.then_inc(s("scaled"), 1)
                    return
                then(last)
                V.tensor_tensor(dst, dst, gain[0:r, 1, :], ALU.add).then_inc(signal, 1)

            def norm_in(n):
                i = TOKS[n]
                if n == 0:
                    dve.wait_ge(s("gain_in"), 32)
                normalise(n, h_tok[0:ROWS[i], HROW[i], :], xin[0:ROWS[i], HROW[i], :], ROWS[i], gain_in, s("normed"))

            def low_features(n, i, job, hi, lo, first=0):
                v = slot(job)[:, :].rearrange("p (k t) -> p k t", k=KT_D)[:, :, first:ROWS[i]]
                dve.wait_ge(s("h_high"), n + 1)
                empties(V.tensor_tensor(lo, v, hi, ALU.subtract), job)

            def low_in(n):
                i = TOKS[n]
                low_features(n, i, f"hT{i}", hT_hi[:, :, QCOLS[i]], hT_lo[:, :, QCOLS[i]])

            for n, i in enumerate(TOKS):
                dve.wait_ge(s(f"x_in{i}"), 16)
                statistics(n, xin[0:ROWS[i], HROW[i], :], ROWS[i])
                if n:
                    norm_in(n - 1)
                if n >= 3:
                    low_in(n - 3)
            norm_in(len(TOKS) - 1)
            for n in range(len(TOKS) - 3, len(TOKS)):
                low_in(n)

            low_units = [u for u in range(len(UNITS)) if u not in POOL_UNITS]

            def low_parts(n):
                while low_units and low_units[0] < n:
                    low_part(dve, low_units.pop(0))

            low_parts(RING)

            dve.wait_ge(s("positions"), 1)
            then(V.scalar_tensor_tensor(dist[:, :], dist[:, :], -1.0, dist[:, :], ALU.mult, ALU.max))
            then(V.tensor_scalar(dist[0:CH, T - CH:T], dist[0:CH, T - CH:T], FAR, None, ALU.add))

            for k, (job, name, j) in enumerate((("ssq", "q_g", 0), ("ssq", "q_g", 1), ("sskv", "kv_g", 0))):
                root = tmpA[:, 0 if job == "ssq" else 2, :]
                low_parts(due(job))
                evacuated(dve, job)
                if k != 1:
                    then(V.reciprocal(root, root))
                V.scalar_tensor_tensor(aRaw[:, k, :], aRaw[:, k, :], par(name, j), root, ALU.mult, ALU.mult).then_inc(s("low_normed"), 1)
            dve.wait_ge(s("low_normed"), 3)
            key = aRaw[0:IDX, 3, :]
            low_parts(due("kmean"))
            product(dve, "kmean")
            empties(V.scalar_tensor_tensor(halves(key), banks("kmean", HALF)[0:IDX], -1.0 / IDX, halves(key), ALU.mult, ALU.add), "kmean")
            v0, t1, y = tmpA[0:IDX, 0, :], tmpA[0:IDX, 2, :], kiT[0:IDX, :]
            low_parts(due("kvar"))
            product(dve, "kvar")
            empties(V.tensor_scalar(halves(v0), banks("kvar", HALF)[0:IDX], 1.0 / IDX, LN_EPS, ALU.mult, ALU.add), "kvar")
            dve.wait_ge(s("key_root"), 1)
            then(V.reciprocal(y, y))
            then(V.tensor_tensor(t1, v0, y, ALU.mult))
            then(V.tensor_tensor(t1, t1, y, ALU.mult))
            then(V.tensor_scalar(t1, t1, -0.5, 1.5, ALU.mult, ALU.add))
            then(V.tensor_tensor(y, y, t1, ALU.mult))
            then(V.tensor_tensor(y, y, key, ALU.mult))
            V.tensor_scalar(y, y, par("i_g")[0:IDX], par("i_b")[0:IDX], ALU.mult, ALU.add).then_inc(s("index_keys"), 1)

            then(V.memset(m8[:, 1, :], TAKEN))
            evacuated(dve, "widx")
            n_sum = 0
            for m, i in enumerate(IX_ORDER):
                n = KEYS[i]
                sc = SC[:, sum(KEYS[:i]):sum(KEYS[:i]) + n]
                for h in range(HEADS):
                    low_parts(due(f"ix{i}_{h}"))
                    evacuated(dve, f"ix{i}_{h}")
                    if n_sum:
                        dve.wait_ge(s("index_sum"), n_sum)
                    v, w = relu[:, n_sum % 2, 0:n], wix[:, i, h:h + 1]
                    ins = V.scalar_tensor_tensor(sc, v, w, sc, ALU.mult, ALU.add) if h else V.tensor_scalar(sc, v, w, None, ALU.mult)
                    ins.then_inc(s("index_sum"), 1)
                    n_sum += 1
                dve.wait_ge(s("index_sum"), n_sum)
                then(V.memset(sc[0:CH, n - CH:n], INVISIBLE))
                if i == 0:
                    product(dve, "vp2")
                    V.memset(aT[:, :, 0:PAD], 0.0).then_inc(s("cleared"), 1)
                    V.memset(csig[:, :, 0:CH + 1 - META], 0.0)
                    chunk_heads = csig.rearrange("p j (c t) -> p j c t", t=CH + 1)[:, :, 1:, 0]
                    V.memset(chunk_heads, 0.0).then_inc(s("cleared"), 1)
                to = f"ix{IX_ORDER[m + 1]}_0" if i else "ss"
                fill = [job for job in ORDER[JOBS[f"ix{i}_0"]:JOBS[to]] if job in UNIT]
                few = 2 * TOPK > n
                ranked, count = sc, TOPK
                if few:
                    ranked, count = relu[:, 0, 0:n], n - TOPK
                    then(V.tensor_scalar(ranked[:, ::-1], sc, -1.0, None, ALU.mult))
                for k in range(count // 8):
                    if k % 4 == 0 and k // 4 < len(fill):
                        low_parts(due(fill[k // 4]))
                    then(V.max(m8[:, 0, :], ranked))
                    then(V.match_replace(ranked, m8[:, 0, :], ranked, TAKEN))
                then(V.max(m8[:, 0, :], ranked))
                then(V.tensor_copy(m8[:, 1, 0:count % 8], m8[:, 0, 0:count % 8]))
                then(V.match_replace(ranked, m8[:, 1, :], ranked, TAKEN))
                if few:
                    then(V.tensor_scalar(sc, ranked[:, ::-1], TAKEN_BELOW, FAR, ALU.is_le, ALU.mult))
                else:
                    then(V.tensor_scalar(sc, ranked, TAKEN_BELOW, FAR, ALU.is_gt, ALU.mult))
                then(V.tensor_tensor(sc, sc, distances(i), ALU.add))

            low_parts(FIRST_OUT)
            then(V.memset(reset, 1.0))
            then(V.memset(reset.rearrange("p (c t) -> p c t", t=CH + 1)[:, :, 0:1], 0.0))
            dve.wait_ge(s("cleared"), 2)
            for j in range(NJ):
                evacuated(dve, f"z_{j}")
                V.tensor_tensor_scan(csig[:, j, :], reset, csig[:, j, :], 0.0, ALU.mult, ALU.add).then_inc(s("summed"), 1)

            def features(j):
                grow = csig[:, j, :].rearrange("p (c t) -> p c t", t=CH + 1)[:, :, 1:]
                chunks = lambda v: v.rearrange("p (c t) -> p c t", t=CH)
                a_, r_, k_, b_ = AR[:, 0, j, :], AR[:, 1, j, :], KT[:, j, :], BT[:, j, :]
                product(dve, f"kn_{j}")
                ins = V.scalar_tensor_tensor(halves(a_), halves(k_), par("k_k", j), banks(f"kn_{j}", HP), ALU.mult, ALU.mult)
                empties(ins, f"kn_{j}")
                evacuated(dve, f"a_{j}")
                then(V.tensor_scalar(b_, aT[:, j, :], -1.0, par("k_a", j), ALU.add, ALU.mult))
                then(V.scalar_tensor_tensor(k_, b_, 1.0, k_, ALU.add, ALU.mult))
                if j:
                    product(dve, f"bo_{j - 1}")
                V.scalar_tensor_tensor(tw, r_, par("r_k", j), k_, ALU.mult, ALU.mult).then_inc(s("bonus_in"), 1)
                evacuated(dve, f"kn_{j}")
                V.scalar_tensor_tensor(b_, a_, -1.0, aT[:, j, :], ALU.mult, ALU.mult).then_inc(s("kk_used"), 1)
                dve.wait_ge(s("kk_used"), j + 1)
                dve.wait_ge(s("decay"), 3 * j + 3)
                V.tensor_tensor(chunks(b_), chunks(b_), grow, ALU.mult).then_inc(s("prepped"), 1)
                dve.wait_ge(s("bonus_in"), j + 1)
                V.tensor_tensor(chunks(k_), chunks(k_), grow, ALU.mult).then_inc(s("prepped"), 1)
                product(dve, f"bo_{j}")
                empties(V.tensor_tensor(halves(BONUS[:, j, :]), halves(VY[:, j, :]), banks(f"bo_{j}", HP), ALU.mult), f"bo_{j}")
                if j == NJ - 1:
                    dve.wait_ge(s("prepped"), 2 * NJ)
                    dve.wait_ge(s("decayed"), 2 * NJ)
                    V.memset(flat(DI), 0.0).then_inc(s("no_inverses"), 1)
                    dve.wait_ge(s("no_inverses"), 1)

            def triangles(p, half):
                rows, b = slice(0, CH * len(PAIRS[p])), BUF[p]
                m = mask[rows, :].rearrange("p (o n) -> p o n", o=1).to_broadcast([rows.stop, 2, P])
                job = f"sc_{p}_{half}"
                product(dve, job)
                for n in range(4):
                    j, h = 2 * half + n // 2, n % 2
                    dst = MSX[rows, b, j, h, :].rearrange("p (g n) -> p g n", g=2)[:, :, 0:P]
                    lo = 512 * h + 256 * (n // 2)
                    src = slot(job)[rows, lo:lo + 256].rearrange("p (g n) -> p g n", g=2)
                    last = V.tensor_tensor(dst, src, m, ALU.mult)
                empties(last, job)

            def invert(g, piece):
                r = BLOCKS[g]
                if piece == 0:
                    dve.wait_ge(s("blocks_here"), 16 * (g + 1))
                    if g:
                        dve.wait_ge(s("inverses_out"), 16 * g)
                    then(V.tensor_copy(Xi[0:r, :], Ni[0:r, :]))
                    V.memset(Xi[0:r, 0:BLK * BLK:BLK + 1], 1.0).then_inc(s("inverses_begun"), 1)
                    dve.wait_ge(s("inverses_begun"), g + 1)
                N3 = Ni[0:r, :].rearrange("i (s t) -> i s t", t=BLK)
                X3 = Xi[0:r, :].rearrange("i (s t) -> i s t", t=BLK)
                for j in PIECES[piece]:
                    c, w = min(j, POOL_COLUMN), BLK - 1 - j
                    new = Ti[0:r, 0:c * w].rearrange("i (c t) -> i c t", c=c)
                    then(V.tensor_tensor(new, N3[:, j:j + 1, j + 1:BLK].to_broadcast([r, c, w]),
                                         X3[:, 0:c, j:j + 1].to_broadcast([r, c, w]), ALU.mult))
                    last = V.tensor_tensor(X3[:, 0:c, j + 1:BLK], X3[:, 0:c, j + 1:BLK], new, ALU.add)
                    if j < BLK - 2:
                        then(last)
                    else:
                        last.then_inc(s("inverted"), 1)

            def logits(i, h):
                k, r, nk = ATT[i, h], ROWS[i], NKEYS[i]
                far = distances(i) if i == META_TILE else SC[:, sum(KEYS[:i]):sum(KEYS[:i]) + nk]
                job = f"S_{i}_{h}"
                product(dve, job)
                if k == 0:
                    dve.wait_ge(s("shifted"), len(SHIFTED))
                if k >= 2:
                    dve.wait_ge(s("exp"), k - 1)
                L = Lb[0:r, k % 2, 0:nk]
                empties(V.scalar_tensor_tensor(L, far, -SLOPES[h], slot(job)[0:r, 0:nk], ALU.mult, ALU.add), job)
                evacuated(dve, job)
                V.tensor_reduce(nmax[0:r, h:h + 1], L, AX.X, ALU.max, negate=True).then_inc(s("max"), 1)

            def inverse_sum(i, h):
                k, r = ATT[i, h], ROWS[i]
                dve.wait_ge(s("exp"), k + 1)
                then(V.reciprocal(rinv[0:r, h:h + 1], rsum[0:r, h:h + 1]))
                V.tensor_scalar(diag[0:r, k % 2, 0:r], ident[0:r, 0:r], rinv[0:r, h:h + 1], None, ALU.mult).then_inc(s("rinv"), 1)

            def second_blocks(p):
                b, job = BUF[p], f"nu_{p}"
                product(dve, job)
                for c in range(len(PAIRS[p])):
                    second = slice(CH * c + BLK, CH * (c + 1))
                    last = V.tensor_tensor(flat(R[second, b]), flat(R[second, b]), slot(job)[second, :], ALU.add)
                empties(last, job)

            def through_chunk(p):
                job = f"qg_{p}"
                product(dve, job)
                v = slot(job)[:, :].rearrange("p (c j n) -> p j c n", j=NJ, c=2)
                eye = eye2[:, :].rearrange("p (o n) -> p o n", o=1).to_broadcast([P, NJ, CH])
                for c, chunk in enumerate(PAIRS[p]):
                    r_ = AR[:, 1, :, CH * chunk:CH * (chunk + 1)]
                    V.tensor_tensor(QB[:, :, c, :], v[:, :, c, 0:CH], r_, ALU.add)
                    last = V.tensor_tensor(GT[:, :, c, :], v[:, :, c, CH:P], eye, ALU.add)
                empties(last, job)

            def state(c):
                p, n = (c + 1) // 2, (c + 1) % 2 if c else 0
                evacuated(dve, f"hy_{p}")
                new, decay = Z[:, (c + 1) % 2], PL[:, :, c:c + 1].to_broadcast([P, NJ, CH])
                if not c:
                    V.tensor_tensor(new, H[:, n], decay, ALU.mult).then_inc(s("state"), 1)
                    return
                job = f"zy_{c}"
                product(dve, job)
                v = slot(job)[:, :].rearrange("p (b j t) -> p b j t", b=2, j=2 * NJ)[:, :, 0:NJ]
                then(V.tensor_tensor(new, v[:, 0], H[:, n], ALU.add))
                V.tensor_tensor(new, new, decay, ALU.mult).then_inc(s("state"), 1)
                y = VY[:, :, CH * c:CH * (c + 1)]
                empties(V.tensor_tensor(y, y, v[:, 1], ALU.add), job)

            def center(j):
                product(dve, f"ym_{j}")
                y = halves(VY[:, j, PAD:TP])
                empties(V.scalar_tensor_tensor(y, banks(f"ym_{j}", HALF), -1.0 / HD, y, ALU.mult, ALU.add), f"ym_{j}")

            def inverse_norms():
                evacuated(dve, "ss")
                then(V.tensor_scalar(key_norm, key_norm, 1e-12, -1.0, ALU.max, ALU.mult))
                V.reciprocal(key_norm, key_norm).then_inc(s("key_norm"), 1)

            mine = {"ss": inverse_norms, "bo": features, "sc": triangles, "inv": invert, "S": logits, "V": inverse_sum,
                    "nu": second_blocks, "qg": through_chunk, "zy": state, "ym": center}
            for kind, *which in MIXERS:
                if kind in mine:
                    mine[kind](*which)
            def low_y(j):
                dve.wait_ge(s("y_high"), j + 1)
                V.tensor_tensor(y_lo[:, j, 0:T], VY[:, j, PAD:TP], y_hi[:, j], ALU.subtract).then_inc(s("y_low"), 1)

            evacuated(dve, "yv")
            V.reciprocal(y_root, y_root).then_inc(s("y_root"), 1)
            for j in range(NJ):
                y = VY[:, j, PAD:TP]
                product(dve, f"yr{j}")
                empties(V.tensor_tensor(halves(y), halves(y), banks(f"yr{j}", HALF), ALU.mult), f"yr{j}")
                evacuated(dve, f"yr{j}")
                then(V.tensor_scalar(y, y, par("gn_g", j), par("gn_b", j), ALU.mult, ALU.add))
                then(V.tensor_tensor(y, y, BONUS[:, j, PAD:TP], ALU.add))
                product(dve, f"g{j}")
                empties(V.tensor_tensor(halves(y), halves(y), banks(f"g{j}", HALF), ALU.mult), f"g{j}")
                if j:
                    low_y(j - 1)
            low_y(NJ - 1)
            product(dve, f"g{NJ - 1}")
            low_parts(FIRST_UP + RING)

            def residual(job, k, i):
                ht = h_tok[0:ROWS[i], HROW[i], :]
                product(dve, job)
                empties(V.scalar_tensor_tensor(ht, ht, ALPHA, slot(job)[0:ROWS[i], :], ALU.mult, ALU.add), job)
                evacuated(dve, job)
                statistics(k, ht, ROWS[i])

            def low_mixed(n):
                i = TOKS[n]
                cols = H1COLS[i]
                low_features(len(TOKS) + n, i, f"h1T{i}", h1T_hi[:, :, cols], h1T_lo[:, :, cols], H1FROM[i])

            dve.wait_ge(s("gains"), 32)
            for n, i in enumerate(TOKS):
                ht = h_tok[0:ROWS[i], HROW[i], :]
                residual(f"mix{i}", 5 + n, i)
                if n >= MIX_AHEAD:
                    low_mixed(n - MIX_AHEAD)
                normalise(5 + n, ht, ht, ROWS[i], gains, s("mixed"))
            for n in range(len(TOKS) - MIX_AHEAD, len(TOKS)):
                low_mixed(n)

            def gated(f):
                dve.wait_ge(s("gelu"), f + 1)
                product(dve, f"val{f}")
                empties(V.tensor_tensor(cv[:, f % 2, :], cv[:, f % 2, :], slot(f"val{f}")[:, 0:SEQ], ALU.mult), f"val{f}")

            def low_act(f):
                dve.wait_ge(s("act_high"), f + 1)
                V.tensor_tensor(act_lo[:, f, :], cv[:, f % 2, :], act_hi[:, f, :], ALU.subtract).then_inc(s("act_low"), 1)

            for f in range(NF):
                g, c_ = gs[:, f % 2, :], cv[:, f % 2, :]
                tap = lambda t: parT[:, NPAR + NF * t + f:NPAR + NF * t + f + 1]
                low_parts(due(f"gate{f}"))
                if f >= 2:
                    low_act(f - 2)
                    dve.wait_ge(s("act_low"), f - 1)
                evacuated(dve, f"gate{f}")
                then(V.tensor_scalar(c_, g[:, 2:SEQ + 2], tap(2), tap(CONV), ALU.mult, ALU.add))
                then(V.scalar_tensor_tensor(c_, g[:, 1:SEQ + 1], tap(1), c_, ALU.mult, ALU.add))
                V.scalar_tensor_tensor(c_, g[:, 0:SEQ], tap(0), c_, ALU.mult, ALU.add).then_inc(s("conv"), 1)
                low_parts(due(f"val{f}"))
                if f >= 1:
                    gated(f - 1)
            low_act(NF - 2)
            gated(NF - 1)
            low_act(NF - 1)
            low_parts(len(UNITS))
            dve.wait_ge(s("gains"), 64)
            for i in range(TILES):
                residual(f"down{i}", 10 + i, i)
                normalise(10 + i, h_tok[:, i, :], h_tok[:, i, :], P, gains, s("out_ready"))

        @block.tensor
        def _(pe):
            def begin(job):
                if JOBS[job] >= NSLOT:
                    evacuated(pe, ORDER[JOBS[job] - NSLOT])

            def end_job(ins, job):
                ins.then_inc(written[JOBS[job] % NSLOT], 1)

            def mm(dst, pairs):
                for n, (a, b) in enumerate(pairs):
                    last = pe.matmul(dst, a, b, start=n == 0, stop=n == len(pairs) - 1)
                return last

            def in_parts(terms):
                return [pair for (ah, al), (bh, bl) in terms for pair in ((ah, bh), (ah, bl), (al, bh))]

            def unit(name):
                u = UNIT[name]
                pe.wait_ge(s("high"), u + 1)
                low_part_made(pe, u)
                hi, lo = weight_parts(u)
                return lambda k: (hi[:, P * k:P * (k + 1)], lo[:, P * k:P * (k + 1)])

            def by_halves(job, m, pairs, n=HALF):
                for b in range(2):
                    last = mm(slot(job)[0:m, 512 * b:512 * b + n], [(a, v[:, n * b:n * (b + 1)]) for a, v in pairs])
                end_job(last, job)

            def wide(dst, a, v, n):
                for lo in range(0, n, 512):
                    hi = min(n, lo + 512)
                    last = mm(dst[:, lo:hi], [(a, v[:, lo:hi])])
                return last

            pe.wait_ge(s("const"), N_CONST)

            def to_features(job, i, ready, count):
                begin(job)
                pe.wait_ge(ready, count)
                r = ROWS[i]
                for k in range(KT_D):
                    last = pe.transpose(slot(job)[:, P * k:P * k + r], h_tok[0:r, HROW[i], P * k:P * (k + 1)], ident[0:r, 0:r])
                end_job(last, job)

            for n, i in enumerate(TOKS):
                to_features(f"hT{i}", i, s("normed"), n + 1)

            begin("par")
            pe.wait_ge(s("par_in"), 16 * N_PAR_DMA)
            pe.transpose(slot("par")[:, 0:NPAR], par_rows[0:NPAR, 0:P], ident[0:NPAR, 0:NPAR])
            end_job(pe.transpose(slot("par")[:, NPAR:NPAR + 4 * NF], par_rows[0:4 * NF, P:2 * P], ident[0:4 * NF, 0:4 * NF]), "par")

            def lora(job, rows, j):
                pe.wait_ge(s("w_lora"), 32)
                pe.wait_ge(s("lora_in"), 1)
                w = wlora[rows, P * j:P * (j + 1)]
                mm(slot(job)[:, 0:META], [(w, wad[rows, 0:META])])
                end_job(mm(slot(job)[:, 512:1024], [(w, wad[rows, META:T])]), job)

            for i in TOKS:
                evacuated(pe, f"hT{i}")
            for job in ORDER[JOBS["p_q0"]:JOBS["ss"]]:
                kind, n = job[:2], job[2:]
                begin(job)
                if kind == "p_":
                    w = unit(job)
                    by_halves(job, P, in_parts([(w(d), (hT_hi[:, d, :], hT_lo[:, d, :])) for d in range(KT_D)]))
                elif kind in ("z_", "a_"):
                    lora(job, slice(0, 64) if kind == "z_" else slice(64, 128), int(n))
                elif job == "ssq":
                    evacuated(pe, "p_q1")
                    by_halves(job, P, [(ones, tmpA[:, d, :]) for d in range(2)])
                elif job == "sskv":
                    evacuated(pe, "p_kv")
                    by_halves(job, P, [(ones, tmpA[:, 2, :])])
                elif job == "kmean":
                    evacuated(pe, "p_ki")
                    by_halves(job, IDX, [(ones[0:IDX, 0:IDX], aRaw[0:IDX, 3, :])])
                elif job == "kvar":
                    pe.wait_ge(s("key_squares"), 1)
                    by_halves(job, IDX, [(ones[0:IDX, 0:IDX], tmpA[0:IDX, 1, :])])
                elif job == "widx":
                    for i in range(TILES):
                        rows = slice(IDX, IDX + HEADS)
                        last = pe.transpose(slot(job)[:, HEADS * i:HEADS * (i + 1)], aRaw[rows, 3, QCOLS[i]], ident[rows, rows])
                    end_job(last, job)
                elif kind in ("qp", "qi"):
                    w = {"qp": wuq, "qi": wiq}[kind]
                    if kind == "qi":
                        pe.wait_ge(s("w_index"), 16)
                    else:
                        pe.wait_ge(s("w_low"), 48)
                    pe.wait_ge(s("low_normed"), 2)
                    by_halves(job, P, [(w[:, d, P * int(n):P * (int(n) + 1)], aRaw[:, d, :]) for d in range(2)])
                elif kind == "kp":
                    pe.wait_ge(s("w_low"), 48)
                    pe.wait_ge(s("low_normed"), 3)
                    by_halves(job, P, [(wuk[:, P * int(n):P * (int(n) + 1)], aRaw[:, 2, :])])
                elif kind == "vp":
                    for b, i in enumerate(((META_TILE, 0), (1, 2), (3,))[int(n)]):
                        last = mm(slot(job)[0:ROWS[i], 512 * b:512 * (b + 1)], [(aRaw[:, 2, QCOLS[i]], wuv)])
                    end_job(last, job)
                else:
                    i, h = int(job[2]), int(job[4])
                    r = head_rows(h)
                    pe.wait_ge(s("index_keys"), 1)
                    if h % 2:
                        pe.wait_ge(s("index_keys2"), 16)
                    evacuated(pe, f"qi{h // 2}")
                    end_job(wide(slot(job)[:, :], qiT[r, h // 2, QCOLS[i]], kiT[r, :], KEYS[i]), job)

            def head_sums(job, squares, n):
                for j in range(NJ):
                    for b in range(2):
                        last = mm(slot(job)[BLK * j:BLK * (j + 1), 512 * b:512 * b + n], [(heads[:, :], squares[:, j, n * b:n * (b + 1)])])
                end_job(last, job)

            def to_heads(job, j, v, n):
                rows = slice(BLK * j, BLK * (j + 1))
                by_halves(job, P, [(headsT[rows, :], v[rows])], n)

            def key_squares(job):
                pe.wait_ge(s("kk_squares"), NJ)
                head_sums(job, key_sq, HP)

            def key_norms(job, j):
                pe.wait_ge(s("key_norm"), 1)
                to_heads(job, j, key_norm, HP)

            def bonus(job, j):
                pe.wait_ge(s("bonus_in"), j + 1)
                by_halves(job, P, [(blk[:, :], tw)], HP)

            def tokens(job, p, half):
                pair = PAIRS[p]
                cols = slice(CH * pair[0], CH * (pair[0] + len(pair)))
                pe.wait_ge(s("prepped"), 2 * NJ)
                pe.wait_ge(s("decayed"), 2 * NJ)
                evacuated(pe, f"bo_{NJ - 1}")
                for n in range(8):
                    j = 2 * half + n // 4
                    src = (AR[:, 0, j], BT[:, j], KT[:, j], VY[:, j])[n % 4]
                    last = pe.transpose(slot(job)[0:CH * len(pair), P * n:P * (n + 1)], src[:, cols], ident[:, :])
                end_job(last, job)

            def triangles(job, p, half):
                pair = PAIRS[p]
                for n in range(8):
                    jj, src, h = n // 4, (BT, KT)[n // 2 % 2], n % 2
                    j, lo = 2 * half + jj, 512 * h + P * (n // 2)
                    for c in range(len(pair)):
                        cc = slice(CH * pair[c], CH * (pair[c] + 1))
                        last = mm(slot(job)[chunk_rows(c), lo:lo + P],
                                  [(src[head_rows(h), j, cc], AR[head_rows(h), :, j, cc])])
                end_job(last, job)

            def instances(p):
                return [(c, j, h) for c in range(len(PAIRS[p])) for j in range(NJ) for h in range(2)]

            def first(c):
                return slice(CH * c, CH * c + BLK)

            def second(c):
                return slice(CH * c + BLK, CH * (c + 1))

            def x1(job, p):
                b = BUF[p]
                for half in range(2):
                    evacuated(pe, f"tk_{p}_{half}")
                    evacuated(pe, f"sc_{p}_{half}")
                for c, j, h in instances(p):
                    r, lo = chunk_rows(c), CH * (2 * j + h)
                    last = mm(slot(job)[r, lo:lo + CH], [(MSX[r, b, j, h, 192:256], Vtok[r, b, j, h])])
                end_job(last, job)

            def first_blocks(job, p):
                b = BUF[p]
                g = 0 if p in GROUPS[0] else 1
                pe.wait_ge(s("inverses_here"), 16 * sum(2 * len(PAIRS[q]) for pairs in GROUPS[:g + 1] for q in pairs))
                evacuated(pe, f"x_{p}")
                for c, j, h in instances(p):
                    lo = P * (2 * j + h)
                    last = mm(slot(job)[first(c), lo:lo + P], [(DI[first(c), b, j, h, 0:BLK], R[first(c), b, j, h])])
                end_job(last, job)

            def second_blocks(job, p):
                b = BUF[p]
                evacuated(pe, f"u0_{p}")
                for c, j, h in instances(p):
                    lo = P * (2 * j + h)
                    last = mm(slot(job)[second(c), lo:lo + P], [(MSX[first(c), b, j, h, BLK:2 * BLK], U0[first(c), j, h])])
                end_job(last, job)

            def solution(job, p):
                b = BUF[p]
                evacuated(pe, f"nu_{p}")
                for c, j, h in instances(p):
                    r, lo = chunk_rows(c), P * (2 * j + h)
                    last = mm(slot(job)[r, lo:lo + P], [(DI[r, b, j, h], R[r, b, j, h])])
                end_job(last, job)

            def through_chunk(job, p):
                b = BUF[p]
                evacuated(pe, f"u_{p}")
                for c, j, h in instances(p):
                    r, lo = chunk_rows(c), 512 * c + P * j
                    last = mm(slot(job)[head_rows(h), lo:lo + P], [(R[r, b, j, h, CH:P], MSX[r, b, j, h, 64:192])])
                end_job(last, job)

            def without_state(job, p):
                b = BUF[p]
                for c, j, h in instances(p):
                    r, hr, lo = chunk_rows(c), head_rows(h), 512 * c + CH * j
                    u, v, m = R[r, b, j, h, 0:CH], Vtok[r, b, j, h], MSX[r, b, j, h]
                    mm(slot(job)[hr, lo:lo + CH], [(m[:, 128:192], u), (m[:, 320:384], v)])
                    lo += NJ * CH
                    last = mm(slot(job)[hr, lo:lo + CH], [(u, m[:, 64:128]), (v, m[:, 256:320])])
                end_job(last, job)

            def state(job, c):
                p, n = (c + 1) // 2, (c + 1) % 2
                evacuated(pe, f"qg_{p}")
                pe.wait_ge(s("state"), c)
                for k in range(2):
                    for j in range(NJ):
                        for h in range(2):
                            hr, lo = head_rows(h), 512 * k + CH * j
                            z = Z[hr, c % 2, j]
                            last = mm(slot(job)[hr, lo:lo + CH], [(z, QB[hr, j, n]) if k else (GT[hr, j, n], z)])
                end_job(last, job)

            def logits(job, i, h):
                hr = head_rows(h)
                end_job(wide(slot(job)[0:ROWS[i], :], qT[hr, h // 2, QCOLS[i]], kT[hr, h // 2, :], NKEYS[i]), job)

            def transposes(job, i, h):
                k, r = ATT[i, h], ROWS[i]
                pe.wait_ge(s("rinv"), k + 1)
                d = diag[0:r, k % 2, 0:r]
                last = mm(slot(job)[0:META, 0:r], [(Pb[0:r, k % 2, 0:META], d)])
                for lo in range(META, NKEYS[i], P):
                    last = mm(slot(job)[:, lo + P - META:lo + P - META + r], [(Pb[0:r, k % 2, lo:lo + P], d)])
                end_job(last, job)

            def values(job, i, h):
                k, r, cols = ATT[i, h], ROWS[i], slice(HD * h, HD * (h + 1))
                evacuated(pe, f"T_{i}_{h}")
                terms = [(vtok[0:META, TILES, cols], PTm[0:META, k % 2, 0:r])]
                if i != META_TILE:
                    terms += [(vtok[:, t, cols], PT[:, k % 2, P * t:P * (t + 1)]) for t in range(i + 1)]
                end_job(mm(slot(job)[head_rows(h), 0:r], terms), job)

            def means(job, j):
                for p in range(len(PAIRS)):
                    evacuated(pe, f"hy_{p}")
                for c in range(1, NCH):
                    evacuated(pe, f"zy_{c}")
                by_halves(job, P, [(blk[:, :], VY[:, j, PAD:TP])])

            mine = {"ss": key_squares, "kn": key_norms, "bo": bonus, "tk": tokens, "sc": triangles, "x": x1,
                    "u0": first_blocks, "nu": second_blocks, "u": solution, "qg": through_chunk, "hy": without_state,
                    "zy": state, "S": logits, "T": transposes, "O": values, "ym": means}
            for step in MIXERS:
                kind, *which = step
                if kind in mine and step != ("zy", 0):
                    begin(name_of(step))
                    mine[kind](name_of(step), *which)
            for job in GROUP_NORM:
                begin(job)
                if job == "yv":
                    pe.wait_ge(s("y_squares"), NJ)
                    head_sums(job, y_sq, HALF)
                elif job[0] == "g":
                    j = int(job[1])
                    pe.wait_ge(s("w_gate"), 16)
                    by_halves(job, P, [(wgate[:, P * j:P * (j + 1)], sgd)])
                else:
                    pe.wait_ge(s("y_root"), 1)
                    to_heads(job, int(job[2]), y_root, HALF)

            def mix(i):
                job = f"mix{i}"
                cols = slice(0, P) if i == META_TILE else QCOLS[i]
                begin(job)
                for k0 in (0, NJ):
                    for b in range(2):
                        out_cols = slice(512 * b, 512 * (b + 1))
                        for k in range(k0, k0 + NJ):
                            j = k - k0
                            if i == META_TILE and b == 0:
                                unit(f"out_{k}")
                                pe.wait_ge(s("y_low" if k0 else "att_low"), j + 1)
                            tile = (y_hi[:, j, cols], y_lo[:, j, cols]) if k0 else (att_hi[:, j, cols], att_lo[:, j, cols])
                            hi, lo = weight_parts(UNIT[f"out_{k}"])
                            passes = in_parts([(tile, (hi[:, out_cols], lo[:, out_cols]))])
                            for n, (a, w) in enumerate(passes):
                                last = pe.matmul(slot(job)[:, out_cols], a, w, start=k == 0 and n == 0, stop=k == KT_D - 1 and n == 2)
                end_job(last, job)

            for job in ORDER[JOBS[f"mix{META_TILE}"]:JOBS["gate0"]]:
                i = next(i for i in TOKS if job.endswith(str(i)))
                if job.startswith("mix"):
                    mix(i)
                else:
                    to_features(job, i, s("mixed"), TOKS.index(i) + 1)

            gate_cols = ((0, 512 - GATE_AT, GATE_AT), (512 - GATE_AT, SEQ + CONV - 1, 512))
            value_cols = ((CONV - 1, SEQ + CONV - 1, 0),)
            half = CONV - 1 + SEQ // 2
            value_halves = ((CONV - 1, half, 0), (half, SEQ + CONV - 1, SEQ // 2))

            def up(job, cols):
                w = unit(job)
                for lo, hi, at in cols:
                    last = mm(slot(job)[:, at:at + hi - lo],
                              in_parts([(w(d), (h1T_hi[:, d, lo:hi], h1T_lo[:, d, lo:hi])) for d in range(KT_D)]))
                return last

            for i in TOKS[:3]:
                evacuated(pe, f"h1T{i}")
            begin("gate0")
            up("gate0", gate_cols[:1])
            begin("val0")
            up("val0", value_halves[:1])
            to_features(f"h1T{TOKS[-1]}", TOKS[-1], s("mixed"), len(TOKS))
            for i in TOKS[3:]:
                evacuated(pe, f"h1T{i}")
            end_job(up("gate0", gate_cols[1:]), "gate0")
            end_job(up("val0", value_halves[1:]), "val0")
            for f in range(1, NF):
                for job, cols in ((f"gate{f}", gate_cols), (f"val{f}", value_cols)):
                    begin(job)
                    end_job(up(job, cols), job)

            def down(f, i, start=False, stop=False):
                hi, lo = weight_parts(UNIT[f"down_{f}"])
                tile = (act_hi[:, f, P * i:P * (i + 1)], act_lo[:, f, P * i:P * (i + 1)])
                for b in range(2):
                    cols = slice(512 * b, 512 * (b + 1))
                    passes = in_parts([(tile, (hi[:, cols], lo[:, cols]))])
                    for n, (a, w) in enumerate(passes):
                        last = pe.matmul(slot(f"down{i}")[:, cols], a, w, start=start and n == 0, stop=stop and n == 2)
                return last

            for f in STREAMED:
                unit(f"down_{f}")
                pe.wait_ge(s("act_low"), f + 1)
                for i in range(TILES):
                    if f == 0:
                        begin(f"down{i}")
                    last = down(f, i, start=f == 0)
                last.then_inc(s("rows_used"), 1)
            pe.wait_ge(s("act_low"), NF)
            kept = KEPT + [f for f in range(NF) if f not in KEPT + STREAMED]
            for i in range(TILES):
                for f in kept:
                    if i == 0:
                        unit(f"down_{f}")
                    last = down(f, i, stop=f == kept[-1])
                end_job(last, f"down{i}")


_INS = ['x', 'meta', 'ln_in_g', 'ln_in_b', 'w_in', 'q_norm_g', 'w_uq', 'kv_norm_g', 'w_ukv', 'w_iq', 'idx_ln_g', 'idx_ln_b',
        'mu_shift', 'w0', 'w_decay_up', 'a0', 'w_aaa_up', 'w_gate_up', 'k_k', 'k_a', 'r_k', 'gn_g', 'gn_b', 'w_out',
        'ln1_g', 'ln1_b', 'w_ffn_up', 'conv_w', 'conv_b', 'w_ffn_down', 'ln2_g', 'ln2_b']
_OUTS = [((1, SEQ, D), 'float32')]


def kernel(**inputs):
    import numpy as _np
    import concourse.bacc as _bacc
    from concourse import mybir as _mybir
    from concourse.bass_utils import run_bass_kernel_spmd as _run

    nc = _bacc.Bacc("TRN2", target_bir_lowering=False, num_devices=1)
    arrays, args = {}, []
    for name in _INS:
        a = _np.ascontiguousarray(inputs[name])
        arrays[f"in_{name}_dram"] = a
        args.append(nc.dram_tensor(f"in_{name}_dram", a.shape, _mybir.dt.from_np(a.dtype), kind="ExternalInput").ap())
    for i, (shape, dtype) in enumerate(_OUTS):
        dt = _mybir.dt.from_np(_np.dtype(dtype))
        args.append(nc.dram_tensor(f"out_{i}_dram", shape, dt, kind="ExternalOutput").ap())
    hymba(nc, *args)
    r = _run(nc, [arrays], core_ids=[0])
    return r.results[0]["out_0_dram"]
```
